# Optimizing a Trainium2 kernel written in Bass

```python
import math
import jax, jax.numpy as jnp
from jax import lax
import numpy as np

D_MODEL = 1024
BATCH = 1
SEQ = 256
DEPTH = 2

MEM_LEN = 256
HEAD_DIM = 64
MIX_WIDTH = 3 * D_MODEL // 4
MEM_WIDTH = D_MODEL - MIX_WIDTH
N_SB_HEADS = MIX_WIDTH // HEAD_DIM
DIFF_V_DIM = 2 * HEAD_DIM
N_DIFF_HEADS = MIX_WIDTH // DIFF_V_DIM
N_MEM_HEADS = 4
MEM_HEAD_DIM = MEM_WIDTH // N_MEM_HEADS
IN_WIDTH = 3 * MIX_WIDTH + MEM_WIDTH
ROPE_DIM = HEAD_DIM // 4
ROPE_THETA = 500000.0
BLOCK_Q = 128
D_FF_DENSE = ((8 * D_MODEL // 3 + 255) // 256) * 256
N_EXPERTS = 8
TOP_K = 2
D_FF_EXPERT = 7 * D_MODEL // 2
N_EVEN = (DEPTH + 1) // 2
N_ODD = DEPTH // 2
EPS = 1e-6
NEG_BIG = -1e30
POS_OFFSET_MAX = 4096

kernel_name = "hybrid_sb_diff_mem_moe_trunk"

def rms_norm(x, g):
    xf = x.astype(jnp.float32)
    y = xf * lax.rsqrt(jnp.mean(xf * xf, axis=-1, keepdims=True) + EPS)
    return (y * g.astype(jnp.float32)).astype(x.dtype)

def to_heads(t, n_heads, dim):
    b, s, _ = t.shape
    return t.reshape(b, s, n_heads, dim).transpose(0, 2, 1, 3)

def merge_heads(t):
    b, h, s, d = t.shape
    return t.transpose(0, 2, 1, 3).reshape(b, s, h * d)

def rope_tables(positions):
    inv_freq = ROPE_THETA ** (-jnp.arange(0, ROPE_DIM, 2, dtype=jnp.float32) / ROPE_DIM)
    ang = positions.astype(jnp.float32)[..., None] * inv_freq
    return jnp.cos(ang)[:, None], jnp.sin(ang)[:, None]

def partial_rope(t, cos, sin):
    half = ROPE_DIM // 2
    t1, t2, rest = t[..., :half], t[..., half:ROPE_DIM], t[..., ROPE_DIM:]
    c, s = cos.astype(t.dtype), sin.astype(t.dtype)
    return jnp.concatenate([t1 * c - t2 * s, t2 * c + t1 * s, rest], axis=-1)

def stick_breaking_attention(q, k, v):
    b, h, s, d = q.shape
    nb = s // BLOCK_Q
    scale = d ** -0.5
    qb = q.reshape(b, h, nb, BLOCK_Q, d).transpose(2, 0, 1, 3, 4)
    key_idx = jnp.arange(s)

    def block(args):
        qi, i = args
        z = jnp.einsum('bhqd,bhkd->bhqk', qi, k, preferred_element_type=jnp.float32) * scale
        q_idx = i * BLOCK_Q + jnp.arange(BLOCK_Q)
        strict = key_idx[None, :] < q_idx[:, None]
        log_beta = jax.nn.log_sigmoid(z)
        log_keep = jnp.where(strict, jax.nn.log_sigmoid(-z), 0.0)
        after = lax.cumsum(log_keep, axis=3, reverse=True) - log_keep
        w = jnp.where(strict, jnp.exp(log_beta + after), 0.0)
        return jnp.einsum('bhqk,bhkd->bhqd', w.astype(v.dtype), v)

    out = lax.map(block, (qb, jnp.arange(nb)))
    return out.transpose(1, 2, 0, 3, 4).reshape(b, h, s, d)

def differential_attention(q, k, v, lam):
    b, h, _, s, d = q.shape
    nb = s // BLOCK_Q
    scale = d ** -0.5
    qb = q.reshape(b, h, 2, nb, BLOCK_Q, d).transpose(3, 0, 1, 2, 4, 5)
    key_idx = jnp.arange(s)

    def block(args):
        qi, i = args
        sc = jnp.einsum('bhcqd,bhckd->bhcqk', qi, k, preferred_element_type=jnp.float32) * scale
        q_idx = i * BLOCK_Q + jnp.arange(BLOCK_Q)
        causal = key_idx[None, :] <= q_idx[:, None]
        p = jax.nn.softmax(jnp.where(causal, sc, NEG_BIG), axis=-1)
        w = p[:, :, 0] - lam * p[:, :, 1]
        return jnp.einsum('bhqk,bhkv->bhqv', w.astype(v.dtype), v)

    out = lax.map(block, (qb, jnp.arange(nb)))
    return out.transpose(1, 2, 0, 3, 4).reshape(b, h, s, 2 * d)

def memory_cross_attention(q, k, v):
    scale = q.shape[-1] ** -0.5
    sc = jnp.einsum('bhqd,bhmd->bhqm', q, k, preferred_element_type=jnp.float32) * scale
    p = jax.nn.softmax(sc, axis=-1)
    return jnp.einsum('bhqm,bhmd->bhqd', p.astype(v.dtype), v)

def swiglu(x, w_gate_up, w_down):
    g, u = jnp.split(x @ w_gate_up, 2, axis=-1)
    return (jax.nn.silu(g) * u) @ w_down

def moe_swiglu(x, w_router, w_gate_up, w_down):
    logits = jnp.einsum('bsd,de->bse', x, w_router, preferred_element_type=jnp.float32)
    top_val, top_idx = lax.top_k(logits, TOP_K)
    top_w = jax.nn.softmax(top_val, axis=-1)
    combine = jnp.sum(jax.nn.one_hot(top_idx, N_EXPERTS, dtype=jnp.float32)
                      * top_w[..., None], axis=-2)
    out = jnp.zeros_like(x)
    for e in range(N_EXPERTS):
        out = out + combine[..., e:e + 1].astype(x.dtype) * swiglu(x, w_gate_up[e], w_down[e])
    return out

def setup_inputs(seed: int = 0) -> dict:
    key = jax.random.key(seed)
    ks = jax.random.split(key, 24)
    f32 = jnp.float32
    nrm = lambda k, shape, scale: jax.random.normal(k, shape, f32) * scale
    gain = lambda k, shape: 1.0 + 0.02 * jax.random.normal(k, shape, f32)
    x = jax.random.normal(ks[0], (BATCH, SEQ, D_MODEL), f32)
    mem = jax.random.normal(ks[1], (BATCH, MEM_LEN, D_MODEL), f32)
    offset = jax.random.randint(ks[2], (BATCH, 1), 0, POS_OFFSET_MAX, dtype=jnp.int32)
    positions = (offset + jnp.arange(SEQ, dtype=jnp.int32)[None, :]).astype(jnp.int32)
    return {
        "x": x,
        "mem": mem,
        "positions": positions,
        "attn_norm": gain(ks[3], (DEPTH, D_MODEL)),
        "w_in": nrm(ks[4], (DEPTH, D_MODEL, IN_WIDTH), D_MODEL ** -0.5),
        "w_out": nrm(ks[5], (DEPTH, D_MODEL, D_MODEL), D_MODEL ** -0.5),
        "mem_norm": gain(ks[6], (D_MODEL,)),
        "w_mem_kv": nrm(ks[7], (DEPTH, D_MODEL, 2 * MEM_WIDTH), D_MODEL ** -0.5),
        "mem_q_norm": gain(ks[8], (DEPTH, MEM_HEAD_DIM)),
        "mem_k_norm": gain(ks[9], (DEPTH, MEM_HEAD_DIM)),
        "diff_q_norm": gain(ks[10], (N_ODD, HEAD_DIM)),
        "diff_k_norm": gain(ks[11], (N_ODD, HEAD_DIM)),
        "diff_lambda": nrm(ks[12], (N_ODD, 4, HEAD_DIM), 0.1),
        "diff_subln": gain(ks[13], (N_ODD, DIFF_V_DIM)),
        "ffn_norm": gain(ks[14], (DEPTH, D_MODEL)),
        "dense_w_gate_up": nrm(ks[15], (N_EVEN, D_MODEL, 2 * D_FF_DENSE), D_MODEL ** -0.5),
        "dense_w_down": nrm(ks[16], (N_EVEN, D_FF_DENSE, D_MODEL), D_FF_DENSE ** -0.5),
        "w_router": nrm(ks[17], (N_ODD, D_MODEL, N_EXPERTS), D_MODEL ** -0.5),
        "moe_w_gate_up": nrm(ks[18], (N_ODD, N_EXPERTS, D_MODEL, 2 * D_FF_EXPERT), D_MODEL ** -0.5),
        "moe_w_down": nrm(ks[19], (N_ODD, N_EXPERTS, D_FF_EXPERT, D_MODEL), D_FF_EXPERT ** -0.5),
    }

def reference(x, mem, positions, attn_norm, w_in, w_out, mem_norm, w_mem_kv, mem_q_norm,
              mem_k_norm, diff_q_norm, diff_k_norm, diff_lambda, diff_subln, ffn_norm,
              dense_w_gate_up, dense_w_down, w_router, moe_w_gate_up, moe_w_down):
    b, s, _ = x.shape
    cos, sin = rope_tables(positions)
    cos_d, sin_d = cos[:, :, None], sin[:, :, None]
    mem_n = rms_norm(mem, mem_norm)
    for i in range(DEPTH):
        j = i // 2
        h = rms_norm(x, attn_norm[i])
        proj = h @ w_in[i]
        q_mix = proj[..., :MIX_WIDTH]
        k_mix = proj[..., MIX_WIDTH:2 * MIX_WIDTH]
        v_mix = proj[..., 2 * MIX_WIDTH:3 * MIX_WIDTH]
        q_mem = proj[..., 3 * MIX_WIDTH:]
        kv_m = mem_n @ w_mem_kv[i]
        qm = rms_norm(to_heads(q_mem, N_MEM_HEADS, MEM_HEAD_DIM), mem_q_norm[i])
        km = rms_norm(to_heads(kv_m[..., :MEM_WIDTH], N_MEM_HEADS, MEM_HEAD_DIM), mem_k_norm[i])
        vm = to_heads(kv_m[..., MEM_WIDTH:], N_MEM_HEADS, MEM_HEAD_DIM)
        o_mem = memory_cross_attention(qm, km, vm)
        if i % 2 == 0:
            q = to_heads(q_mix, N_SB_HEADS, HEAD_DIM)
            k = to_heads(k_mix, N_SB_HEADS, HEAD_DIM)
            v = to_heads(v_mix, N_SB_HEADS, HEAD_DIM)
            o_mix = stick_breaking_attention(q, k, v)
        else:
            q = q_mix.reshape(b, s, N_DIFF_HEADS, 2, HEAD_DIM).transpose(0, 2, 3, 1, 4)
            k = k_mix.reshape(b, s, N_DIFF_HEADS, 2, HEAD_DIM).transpose(0, 2, 3, 1, 4)
            q = partial_rope(rms_norm(q, diff_q_norm[j]), cos_d, sin_d)
            k = partial_rope(rms_norm(k, diff_k_norm[j]), cos_d, sin_d)
            v = to_heads(v_mix, N_DIFF_HEADS, DIFF_V_DIM)
            lam_init = 0.8 - 0.6 * math.exp(-0.3 * i)
            lp = diff_lambda[j].astype(jnp.float32)
            lam = (jnp.exp(jnp.sum(lp[0] * lp[1])) - jnp.exp(jnp.sum(lp[2] * lp[3]))
                   + lam_init)
            o = differential_attention(q, k, v, lam)
            o_mix = rms_norm(o, diff_subln[j]) * (1.0 - lam_init)
        merged = jnp.concatenate([merge_heads(o_mix), merge_heads(o_mem)], axis=-1)
        x = x + merged @ w_out[i]
        h = rms_norm(x, ffn_norm[i])
        if i % 2 == 0:
            x = x + swiglu(h, dense_w_gate_up[j], dense_w_down[j])
        else:
            x = x + moe_swiglu(h, w_router[j], moe_w_gate_up[j], moe_w_down[j])
    return x


_drawn_inputs = setup_inputs


def setup_inputs(seed=0):
    import zlib

    import numpy as np

    out = dict(_drawn_inputs(seed))
    spreads = {}
    factors = {'mem_norm': 8.0,
     'mem_q_norm': 8.0,
     'mem_k_norm': 8.0,
     'diff_q_norm': 4.519,
     'diff_k_norm': 4.628,
     'diff_subln': 4.027}
    for name, (base, spread) in spreads.items():
        noise = np.random.default_rng([zlib.crc32(name.encode()), seed]).standard_normal(out[name].shape)
        drawn = base * np.exp(spread * noise) if base else spread * noise
        out[name] = __import__('jax').numpy.asarray(drawn.astype(out[name].dtype))
    for name, factor in factors.items():
        out[name] = (out[name] * factor).astype(out[name].dtype)
    return out
```

```python
import math
from contextlib import ExitStack

import numpy as np

import concourse.bass as bass
from concourse import mybir

ALU = mybir.AluOpType
ACT = mybir.ActivationFunctionType
AX = mybir.AxisListType
F32 = mybir.dt.float32
F32R = mybir.dt.float32r
I32 = mybir.dt.int32

P = 128
BANK = 512
RAW_SLOTS = 6
SPLIT_SLOTS = 3
AHEAD = 2
HEAD = 64
ROPE = HEAD // 4
ROPE_THETA = 500000.0
EPS = 1e-6
NEG_BIG = -1e30


def build(nc, x_in, mem, positions, attn_norm, w_in, w_out, mem_norm, w_mem_kv, mem_q_norm, mem_k_norm,
          diff_q_norm, diff_k_norm, diff_lambda, diff_subln, ffn_norm, dense_w_gate_up, dense_w_down,
          w_router, moe_w_gate_up, moe_w_down, out):
    _, S, D = x_in.shape
    TILES = S // P
    KD = D // P
    MIX = 3 * D // 4
    WIN = w_in.shape[2]
    FF = dense_w_down.shape[1]
    E = w_router.shape[2]
    FE = moe_w_down.shape[2]
    HALF = BANK // 2
    SCALE = float(HEAD) ** -0.5
    LAM_INIT = 0.8 - 0.6 * math.exp(-0.3 * 1)
    BLOCK = 4 * BANK
    QKW = 2 * MIX
    NSB = MIX // HEAD
    NDIFF = MIX // (2 * HEAD)
    NMEM = (D - MIX) // HEAD
    IN_GROUPS = WIN // BANK
    FF_GROUPS = FF // HALF
    FE_GROUPS = FE // BANK
    assert TILES == 2 and MIX == 768 and WIN == 5 * BANK and FF % HALF == 0 and FE % BANK == 0 and D == 2 * BANK

    BLK_MEM, n = 0, 4
    BLK_IN, BLK_OUT = [0, 0], [0, 0]
    BLK_IN[0], n = n, n + 2 * IN_GROUPS
    BLK_OUT[0], n = n, n + KD // 2
    BLK_FF, n = n, n + 2 * FF_GROUPS
    BLK_FD, n = n, n + FF // P // 2
    BLK_IN[1], n = n, n + 2 * IN_GROUPS
    BLK_OUT[1], n = n, n + KD // 2
    BLK_MOE = n
    GU_BLOCKS = 4 * FE_GROUPS
    DOWN_BLOCKS = FE // P // 2
    TURN_BLOCKS = GU_BLOCKS + DOWN_BLOCKS
    assert TURN_BLOCKS % RAW_SLOTS == 0 and TURN_BLOCKS % SPLIT_SLOTS == 0
    UNITS = [NSB + NMEM, NDIFF + NMEM]
    LOGIT, REST, FIRST, SECOND, MASK, PLACE1, TMP = range(7)
    fills = [("memT", f) for f in range(4)] + [("xT0", f) for f in range(4)] + [("km", l) for l in range(2)]
    for l in range(2):
        fills += [] if l == 0 else [("xT1", f) for f in range(4)]
        fills += [(f"qk{l}", c) for c in range(7)]
        fills += [(f"w{l}", u) for u in range(UNITS[l])]
        fills += [(f"oT{l}", f) for f in range(4)] + [(f"fT{l}", f) for f in range(4)]
        fills += [("hT", j) for j in range(FF_GROUPS)] if l == 0 else []
    fills += [("gather", f) for f in range(4)]
    FILL = {name: i for i, name in enumerate(fills)}
    FILL_MOE = len(fills)
    TURN_FILLS = 1 + FE_GROUPS + 4 + 4
    assert TURN_FILLS % 2 == 0
    MAX_EXTRA = TILES * S // (P + 1)

    ctx = ExitStack()
    with ctx:
        def sb(name, shape, dt=F32, to=None):
            return (to or ctx).enter_context(nc.sbuf_tensor(name, shape, dt))

        def sem(name):
            return ctx.enter_context(nc.semaphore(name))

        raw = sb("raw", [P, RAW_SLOTS, BLOCK])
        w_hi = sb("w_hi", [P, SPLIT_SLOTS, BLOCK], F32R)
        w_lo = sb("w_lo", [P, SPLIT_SLOTS, BLOCK], F32R)
        x = sb("x", [P, TILES, D])
        nat = sb("nat", [P, TILES, D])
        t_hi = sb("t_hi", [P, KD, S], F32R)
        t_lo = sb("t_lo", [P, KD, S], F32R)
        sil = sb("sil", [P, 2, BANK])
        hid = sb("hid", [P, 2, BANK])
        gain = sb("gain", [P, D])
        km_t = sb("km_t", [P, 2, 2, S])
        vm = sb("vm", [P, 2, TILES, 4 * HEAD])
        km = sb("km", [P, 2, TILES, 4 * HEAD])
        ident = sb("ident", [P, P])
        ones = sb("ones", [P, P])
        before = sb("before", [P, P])
        slot_row = sb("slot_row", [P, P])
        causal = sb("causal", [P, 3 * P])
        head_gain = sb("head_gain", [P, 2, HEAD])
        memq_gain = sb("memq_gain", [P, 2, HEAD])
        diff_gain = sb("diff_gain", [P, 2, HEAD])
        sub_gain = sb("sub_gain", [P, 2 * HEAD])
        lam4 = sb("lam4", [P, 4, HEAD])
        pos_i = sb("pos_i", [P, TILES], I32)
        norm_r = sb("norm_r", [P, 5, 3, TILES])
        stat = sb("stat", [P, 4, 3, 4])
        lam = sb("lam", [P, 5])
        gap = sb("gap", [P, 8, TILES])
        minus_half = sb("minus_half", [P, 24])
        inv_freq = sb("inv_freq", [P, TILES, ROPE // 2])
        down_row = sb("down_row", [P, E])
        ang = sb("ang", [P, 6, TILES, ROPE // 2])
        ang_i = sb("ang_i", [P, TILES, ROPE // 2], I32)
        head_r = sb("head_r", [P, 7, 2, 24])
        wr = sb("wr", [P, KD, E])
        wr_hi = sb("wr_hi", [P, KD, E], F32R)
        wr_lo = sb("wr_lo", [P, KD, E], F32R)
        route = sb("route", [P, 7, TILES, E])
        turn_slot = sb("turn_slot", [P, TILES, 12])
        turn_w = sb("turn_w", [P, TILES, 12])
        over = sb("over", [P, 5, E])
        table = sb("table", [P, 4])
        table_i = sb("table_i", [P, 4], I32)
        pick = sb("pick", [P, TILES, P], F32R)
        pick_t = sb("pick_t", [P, TILES, P], F32R)
        turn_cw = sb("turn_cw", [P, TILES])
        slot_w = sb("slot_w", [P, 1])

        with ExitStack() as here:
            proj = sb("proj", [P, TILES, WIN], to=here)
            qk_t = sb("qk_t", [P, 7, 2 * S], to=here)
            att = sb("att", [P, 2, 2 * BANK], to=here)
            keep = sb("keep", [P, 2, BANK], to=here)
            att_t = sb("att_t", [P, 2, BANK], to=here)
        with ExitStack() as here:
            h_hi = sb("h_hi", [P, FF // P, S], F32R, to=here)
            h_lo = sb("h_lo", [P, FF // P, S], F32R, to=here)
        with ExitStack() as here:
            e_hi = sb("e_hi", [P, FE // P, P], F32R, to=here)
            e_lo = sb("e_lo", [P, FE // P, P], F32R, to=here)
            n_hi = sb("n_hi", [P, TILES, D], F32R, to=here)
            n_lo = sb("n_lo", [P, TILES, D], F32R, to=here)
        g_hi, g_lo = (t[:, 0:KD // 2, :].rearrange("p a (b s) -> p (a b) s", b=2) for t in (t_hi, t_lo))
        y_hi, y_lo = (t[:, KD // 2:KD, :].rearrange("p a s -> p (a s)") for t in (t_hi, t_lo))

        ps = ctx.enter_context(nc.psum_tensor("ps", [P, 8, BANK], F32))
        SPARE = 4
        OUT = 6

        raw_landed = [sem(f"raw_landed{s}") for s in range(RAW_SLOTS)]
        hi_ready, lo_ready = sem("hi_ready"), sem("lo_ready")
        w_used = sem("w_used")
        fill_ready, fill_hi = sem("fill_ready"), sem("fill_hi")
        spare_taken = [sem(f"spare_taken{b}") for b in range(2)]
        acc_taken = [sem(f"acc_taken{b}") for b in range(2)]
        z_ready, z_taken = sem("z_ready"), [sem(f"z_taken{b}") for b in range(2)]
        head_ready, head_taken = sem("head_ready"), sem("head_taken")
        small_landed, mem_landed, x_landed = sem("small_landed"), sem("mem_landed"), sem("x_landed")
        gain_landed, consts_ready = sem("gain_landed"), sem("consts_ready")
        squares_ready, rstd_ready, nat_ready = sem("squares_ready"), sem("rstd_ready"), sem("nat_ready")
        km_copied, sums_ready, head_rstd_ready, heads_normed = (
            sem("km_copied"), sem("sums_ready"), sem("head_rstd_ready"), sem("heads_normed"))
        masked_ready, max_ready, exp_ready, att_ready = (
            sem("masked_ready"), sem("max_ready"), sem("exp_ready"), sem("att_ready"))
        sil_ready = sem("sil_ready")
        lam_sums, lam_exp = sem("lam_sums"), sem("lam_exp")
        ang_ready, rope_ready = sem("ang_ready"), sem("rope_ready")
        wr_hi_ready, wr_ready = sem("wr_hi_ready"), sem("wr_ready")
        logits_ready, gap_ready, gap_exp = sem("logits_ready"), sem("gap_ready"), sem("gap_exp")
        mask_ready, places_ready, table_ready = sem("mask_ready"), sem("places_ready"), sem("table_ready")
        n_hi_ready, n_ready, pick_ready = sem("n_hi_ready"), sem("n_ready"), sem("pick_ready")
        y_scaled, y_hi_ready, y_lo_ready = sem("y_scaled"), sem("y_hi_ready"), sem("y_lo_ready")
        dve_step, act_step, pool_step = sem("dve_step"), sem("act_step"), sem("pool_step")
        stored = sem("stored")

        def chain(eng, own):
            done = [0]

            def link(ins):
                done[0] += 1
                ins.then_inc(own, 1)
                eng.wait_ge(own, done[0])
            return link

        def taken(eng, f):
            eng.wait_ge(spare_taken[f % 2], f // 2 + 1)

        groups = [(f"mem{g}", g) for g in range(2)]
        for l in range(2):
            groups += [(f"in{l}.{g}", g % 2) for g in range(IN_GROUPS)] + [(f"out{l}.{p}", p) for p in range(2)]
            if l == 0:
                groups += [(f"ff{g}", g % 2) for g in range(FF_GROUPS)] + [(f"fd{p}", p) for p in range(2)]
        ACC = {name: (p, sum(q == p for _, q in groups[:i])) for i, (name, p) in enumerate(groups)}

        def group_taken(eng, name):
            p, uses = ACC[name]
            eng.wait_ge(acc_taken[p], uses + 1)

        ACC_MOE = [sum(q == p for _, q in groups) for p in range(2)]
        ACC_TURN = [(FE_GROUPS + 1) // 2, FE_GROUPS // 2]
        NORMS = {"km0": 0, "km1": 1, "qm0": 2, "q": 3, "k": 4, "qm1": 5, "sub": 6}
        NORM_N = [2 * NMEM] * 3 + [2 * 2 * NDIFF] * 2 + [2 * NMEM, 2 * NDIFF]
        NORM_W = [HEAD] * 6 + [2 * HEAD]

        block = ctx.enter_context(nc.Block())

        def rows(w, k0, kn, c0, cn):
            return w[k0 * P:(k0 + kn) * P, c0:c0 + cn].rearrange("(k p) n -> p k n", p=P)

        def halves(slot):
            v = slot.rearrange("p (k h n) -> p k h n", k=4, h=2)
            return v[:, :, 0, :], v[:, :, 1, :]

        dense = []
        for l in range(2):
            dense += [[(None, rows(w_mem_kv[l], k, 4, 0, BANK))] for k in (0, 4)]
        for l in range(2):
            dense += [[(None, rows(w_in[l], k, 4, g * BANK, BANK))] for g in range(IN_GROUPS) for k in (0, 4)]
            dense += [[(None, rows(w_out[l], k, 2, 0, D))] for k in range(0, KD, 2)]
            if l == 0:
                dense += [[(h, rows(dense_w_gate_up[0], k, 4, h * FF + g * HALF, HALF)) for h in range(2)]
                          for g in range(FF_GROUPS) for k in (0, 4)]
                dense += [[(None, rows(dense_w_down[0], k, 2, 0, D))] for k in range(0, FF // P, 2)]
        assert len(dense) == BLK_MOE

        def raw_count(n):
            return 16 * sum(len(dense[m]) for m in range(n % RAW_SLOTS, n + 1, RAW_SLOTS))

        RAW_MOE = [16 * (1 + sum(len(dense[m]) for m in range(s, BLK_MOE, RAW_SLOTS))) for s in range(RAW_SLOTS)]

        def wait_raw(eng, n, turn=None):
            s = n % RAW_SLOTS
            if turn is None and n < BLK_MOE:
                eng.wait_ge(raw_landed[s], raw_count(n))
            else:
                at = RAW_MOE[s] + 16 * ((n - BLK_MOE) // RAW_SLOTS)
                eng.wait_ge(raw_landed[s], at if turn is None else turn * (16 * TURN_BLOCKS // RAW_SLOTS) + at)

        @block.sync
        def _(sp):
            sp.dma_start(proj[:, :, 0:D], mem.rearrange("b (t p) d -> p (b t) d", p=P)).then_inc(mem_landed, 16)
            for b, parts in enumerate(dense):
                slot = raw[:, b % RAW_SLOTS, :]
                if b >= RAW_SLOTS:
                    sp.wait_ge(lo_ready, b - RAW_SLOTS + 1)
                for h, src in parts:
                    dst = slot.rearrange("p (k n) -> p k n", n=src.shape[2]) if h is None else halves(slot)[h]
                    sp.dma_start(dst, src).then_inc(raw_landed[b % RAW_SLOTS], 16)
                if b == 1:
                    sp.dma_start(x[:], x_in.rearrange("b (t p) d -> p (b t) d", p=P)).then_inc(x_landed, 16)

            def turn_loads(i, expert):
                gate_up = moe_w_gate_up[0, bass.ds(expert, 1)].rearrange("e (k p) n -> p (e k) n", p=P)
                down = moe_w_down[0, bass.ds(expert, 1)].rearrange("e (k p) n -> p (e k) n", p=P)
                for b in range(TURN_BLOCKS):
                    n = BLK_MOE + b
                    slot = raw[:, n % RAW_SLOTS, :]
                    sp.wait_ge(lo_ready, i * TURN_BLOCKS + (n - RAW_SLOTS + 1))
                    if b < GU_BLOCKS:
                        j, half, k = b // 4, b // 2 % 2, b % 2 * 4
                        src = gate_up[:, k:k + 4, half * FE + j * BANK:half * FE + (j + 1) * BANK]
                    else:
                        k = (b - GU_BLOCKS) * 2
                        src = down[:, k:k + 2, :]
                    sp.dma_start(slot.rearrange("p (k n) -> p k n", n=src.shape[2]), src)\
                      .then_inc(raw_landed[n % RAW_SLOTS], 16)

            with sp.Fori(0, E) as i:
                turn_loads(i, i)
            sp.wait_ge(table_ready, 1)
            turns = sp.value_load(table_i[0:1, 0:1], min_val=E, max_val=E + MAX_EXTRA)
            with sp.If(turns > E):
                with sp.Fori(E, turns) as i:
                    expert = sp.value_load(table_i[0:1, bass.ds(i - (E - 1), 1)], min_val=0, max_val=E - 1)
                    turn_loads(i, expert)
            for b in range(SPLIT_SLOTS):
                n = BLK_MOE + b
                sp.wait_ge(lo_ready, turns * TURN_BLOCKS + (n - RAW_SLOTS + 1))
                sp.dma_start(raw[0:16, n % RAW_SLOTS, 0:P], x_in[0, 0:16, 0:P]).then_inc(raw_landed[n % RAW_SLOTS], 16)
            sp.wait_ge(spare_taken[(FILL_MOE - 1) % 2], turns * (TURN_FILLS // 2) + ((FILL_MOE - 1) // 2 + 1))
            sp.dma_start(out.rearrange("b (t p) d -> p (b t) d", p=P), x[:]).then_inc(stored, 16)
            sp.wait_ge(stored, 16)

        @block.tensor
        def _(pe):
            def spare(f):
                if f >= 2:
                    taken(pe, f - 2)
                return ps[:, SPARE + f % 2, :]

            def product(dst, hi, lo, slot, c0, cn, first, last):
                pe.matmul(dst, hi, w_hi[:, slot, c0:c0 + cn], start=first, stop=False)
                pe.matmul(dst, lo, w_hi[:, slot, c0:c0 + cn], start=False, stop=False)
                return pe.matmul(dst, hi, w_lo[:, slot, c0:c0 + cn], start=False, stop=last)

            def acc_free(name):
                p, uses = ACC[name]
                if uses:
                    pe.wait_ge(acc_taken[p], uses)
                return p

            def group_block(b, b0, name):
                g, half = divmod(b - b0, 2)
                p = acc_free(f"{name}{g}") if half == 0 else ACC[f"{name}{g}"][0]
                pe.wait_ge(lo_ready, b + 1)
                for kk in range(4):
                    k = 4 * half + kk
                    for t in range(TILES):
                        mm = product(ps[:, 2 * p + t, :], t_hi[:, k, t * P:(t + 1) * P],
                                     t_lo[:, k, t * P:(t + 1) * P], b % SPLIT_SLOTS, kk * BANK, BANK, k == 0, k == KD - 1)
                mm.then_inc(w_used, 1)

            def wide_block(b, b0, name, chunks, hi, lo):
                if b == b0:
                    for p in range(2):
                        acc_free(f"{name}{p}")
                pe.wait_ge(lo_ready, b + 1)
                for kk in range(2):
                    k = 2 * (b - b0) + kk
                    for t in range(TILES):
                        for h in range(2):
                            mm = product(ps[:, 2 * t + h, :], hi[:, k, t * P:(t + 1) * P], lo[:, k, t * P:(t + 1) * P],
                                         b % SPLIT_SLOTS, kk * D + h * BANK, BANK, k == 0, k == chunks - 1)
                mm.then_inc(w_used, 1)

            def transpose_nat(name):
                for f in range(4):
                    bank = spare(FILL[(name, f)])
                    for j in range(4):
                        c, t = 2 * f + j // 2, j % 2
                        mm = pe.transpose(bank[:, j * P:(j + 1) * P], nat[:, t, c * P:(c + 1) * P], ident[:])
                    mm.then_inc(fill_ready, 1)

            def all_taken(name):
                for f in (2, 3):
                    taken(pe, FILL[(name, f)])

            def attention(l):
                U, n_mix, base = UNITS[l], UNITS[l] - NMEM, l * UNITS[0]

                def scores(u):
                    p = u % 2
                    if base + u >= 2:
                        pe.wait_ge(z_taken[p], (base + u) // 2)
                    if u < n_mix:
                        for half in range(1 + l):
                            c, s = (u // 2, u % 2) if l == 0 else (u, half)
                            taken(pe, FILL[(f"qk{l}", c)])
                            q, k = qk_t[64 * s:64 * s + 64, c, 0:S], qk_t[64 * s:64 * s + 64, c, S:2 * S]
                            z = ps[:, 2 * p + half, :]
                            pe.matmul(z[:, 0:P], q[:, 0:P], k[:, 0:P], start=True, stop=True)
                            mm = pe.matmul(z[:, P:3 * P], q[:, P:2 * P], k, start=True, stop=True)
                    else:
                        c, s = divmod(u - n_mix, 2)
                        taken(pe, FILL[(f"qk{l}", 6)])
                        for t in range(TILES):
                            mm = pe.matmul(ps[:, 2 * p, t * S:(t + 1) * S],
                                           qk_t[64 * s:64 * s + 64, 6, c * S + t * P:c * S + (t + 1) * P],
                                           km_t[64 * s:64 * s + 64, l, c, :], start=True, stop=True)
                    mm.then_inc(z_ready, 1)

                def turn(u):
                    bank = spare(FILL[(f"w{l}", u)])
                    if u < n_mix:
                        pe.wait_ge(att_ready, l * NSB + u + 1)
                    else:
                        pe.wait_ge(z_taken[u % 2], (base + u) // 2 + 1)
                    for j in range(3 if u < n_mix else 4):
                        mm = pe.transpose(bank[:, j * P:(j + 1) * P], att[:, u % 2, j * P:(j + 1) * P], ident[:])
                    mm.then_inc(fill_ready, 1)

                def values(u):
                    taken(pe, FILL[(f"w{l}", u)])
                    if base + u >= 2:
                        pe.wait_ge(head_taken, base + u - 1)
                    n = HEAD * (l + 1) if u < n_mix else HEAD
                    for t in range(TILES):
                        if u < n_mix:
                            parts = [[(0, 0)], [(1, 0), (2, 1)]][t]
                            v = proj[:, :, QKW + n * u:QKW + n * (u + 1)]
                        else:
                            parts = [(2 * t, 0), (2 * t + 1, 1)]
                            v = vm[:, l, :, n * (u - n_mix):n * (u - n_mix + 1)]
                        for j, s in parts:
                            mm = pe.matmul(ps[:, OUT + u % 2, t * n:(t + 1) * n], att_t[:, u % 2, j * P:(j + 1) * P],
                                           v[:, s, :], start=(j == parts[0][0]), stop=(j == parts[-1][0]))
                    mm.then_inc(head_ready, 1)

                for s in range(U + 2):
                    if s < U:
                        scores(s)
                    if 1 <= s <= U:
                        turn(s - 1)
                    if s >= 2:
                        values(s - 2)

            pe.wait_ge(consts_ready, 1)
            pe.wait_ge(nat_ready, TILES)
            transpose_nat("memT")
            all_taken("memT")
            for b in range(BLK_MEM, BLK_MEM + 4):
                group_block(b, BLK_MEM, "mem")
            for l in range(2):
                pe.wait_ge(nat_ready, [2, 4][l] * TILES)
                transpose_nat(f"xT{l}")
                all_taken(f"xT{l}")
                for b in range(BLK_IN[l], BLK_OUT[l]):
                    group_block(b, BLK_IN[l], f"in{l}.")
                if l == 0:
                    for m in range(2):
                        bank = spare(FILL[("km", m)])
                        pe.wait_ge(heads_normed, m + 1)
                        for j in range(4):
                            c, t = divmod(j, 2)
                            mm = pe.transpose(bank[:, j * P:(j + 1) * P], km[:, m, t, c * P:(c + 1) * P], ident[:])
                        mm.then_inc(fill_ready, 1)
                for g in (IN_GROUPS - 2, IN_GROUPS - 1):
                    group_taken(pe, f"in{l}.{g}")
                if l == 1:
                    pe.wait_ge(heads_normed, 6)
                for c in range(7):
                    bank = spare(FILL[(f"qk{l}", c)])
                    if c == 6:
                        pe.wait_ge(heads_normed, [3, 7][l])
                    for j in range(4):
                        a, t = divmod(j, 2)
                        col = MIX * a + c * P if c < 6 else 3 * MIX + a * P
                        mm = pe.transpose(bank[:, j * P:(j + 1) * P], proj[:, t, col:col + P], ident[:])
                    mm.then_inc(fill_ready, 1)
                attention(l)
                pe.wait_ge(head_taken, sum(UNITS[:l + 1]))
                if l == 1:
                    pe.wait_ge(heads_normed, 8)
                transpose_nat(f"oT{l}")
                all_taken(f"oT{l}")
                for b in range(BLK_OUT[l], BLK_OUT[l] + KD // 2):
                    wide_block(b, BLK_OUT[l], f"out{l}.", KD, t_hi, t_lo)
                pe.wait_ge(nat_ready, [3, 5][l] * TILES)
                transpose_nat(f"fT{l}")
                all_taken(f"fT{l}")
                if l == 1:
                    break
                for b in range(BLK_FF, BLK_IN[1]):
                    if b < BLK_FD:
                        group_block(b, BLK_FF, "ff")
                    else:
                        taken(pe, FILL[("hT", b - BLK_FD)])
                        wide_block(b, BLK_FD, "fd", FF // P, h_hi, h_lo)
                    j, odd = divmod(b - BLK_FF - 3, 2)
                    if odd == 0 and 0 <= j < FF_GROUPS:
                        bank = spare(FILL[("hT", j)])
                        p, uses = ACC[f"ff{j}"]
                        pe.wait_ge(acc_taken[p], uses + 1)
                        for i in range(4):
                            c, t = divmod(i, 2)
                            mm = pe.transpose(bank[:, i * P:(i + 1) * P],
                                              hid[:, j % 2, t * HALF + c * P:t * HALF + (c + 1) * P], ident[:])
                        mm.then_inc(fill_ready, 1)

            pe.wait_ge(wr_ready, 1)
            for t in range(TILES):
                logits = ps[:, OUT, t * E:(t + 1) * E]
                for k in range(KD):
                    hi, lo = t_hi[:, k, t * P:(t + 1) * P], t_lo[:, k, t * P:(t + 1) * P]
                    pe.matmul(logits, hi, wr_hi[:, k, :], start=(k == 0), stop=False)
                    pe.matmul(logits, lo, wr_hi[:, k, :], start=False, stop=False)
                    mm = pe.matmul(logits, hi, wr_lo[:, k, :], start=False, stop=(k == KD - 1))
            mm.then_inc(logits_ready, 1)
            pe.wait_ge(mask_ready, 1)
            place = ps[:, OUT + 1, :]
            pe.matmul(place[:, 0:E], before[:], route[:, MASK, 0, :], start=True, stop=True)
            pe.matmul(place[:, E:2 * E], ones[:], route[:, MASK, 0, :], start=True, stop=False)
            pe.matmul(place[:, E:2 * E], before[:], route[:, MASK, 1, :], start=False, stop=True)
            pe.matmul(place[:, 2 * E:3 * E], ones[:], route[:, MASK, 0, :], start=True, stop=False)
            pe.matmul(place[:, 2 * E:3 * E], ones[:], route[:, MASK, 1, :], start=False, stop=True).then_inc(places_ready, 1)

            def gather(bank_of):
                for f in range(4):
                    bank = bank_of(f)
                    part = (n_hi, n_lo)[f % 2]
                    for j in range(4):
                        k = f // 2 * 4 + j
                        for t in range(TILES):
                            mm = pe.matmul(bank[:, j * P:(j + 1) * P], part[:, t, k * P:(k + 1) * P], pick[:, t, :],
                                           start=(t == 0), stop=(t == TILES - 1))
                    mm.then_inc(fill_ready, 1)

            pe.wait_ge(n_ready, 1)
            pe.wait_ge(pick_ready, 1)
            gather(lambda f: spare(FILL[("gather", f)]))
            for f in (2, 3):
                taken(pe, FILL[("gather", f)])
            pe.wait_ge(table_ready, 1)
            turns = pe.value_load(table_i[0:1, 0:1], min_val=E, max_val=E + MAX_EXTRA)
            with pe.Fori(0, turns) as i:
                def turn_taken(f):
                    n = FILL_MOE + f
                    pe.wait_ge(spare_taken[n % 2], i * (TURN_FILLS // 2) + (n // 2 + 1))

                def turn_spare(f):
                    turn_taken(f - 2)
                    return ps[:, SPARE + (FILL_MOE + f) % 2, :]

                for b in range(TURN_BLOCKS):
                    n = BLK_MOE + b
                    if b < GU_BLOCKS and b % 4 == 0:
                        j = b // 4
                        pe.wait_ge(acc_taken[j % 2], i * ACC_TURN[j % 2] + (ACC_MOE[j % 2] + j // 2))
                    if b >= GU_BLOCKS:
                        turn_taken(1 + (b - GU_BLOCKS) // 2)
                    pe.wait_ge(lo_ready, i * TURN_BLOCKS + (n + 1))
                    if b < GU_BLOCKS:
                        j, half, k0 = b // 4, b // 2 % 2, b % 2 * 4
                        for kk in range(4):
                            k = k0 + kk
                            mm = product(ps[:, 2 * (j % 2) + half, :], g_hi[:, k, :], g_lo[:, k, :], n % SPLIT_SLOTS,
                                         kk * BANK, BANK, k == 0, k == KD - 1)
                    else:
                        for kk in range(2):
                            k = 2 * (b - GU_BLOCKS) + kk
                            for h in range(2):
                                mm = product(ps[:, OUT + h, :], e_hi[:, k, :], e_lo[:, k, :], n % SPLIT_SLOTS,
                                             kk * D + h * BANK, BANK, k == 0, k == FE // P - 1)
                    mm.then_inc(w_used, 1)
                    if b == 2:
                        bank = turn_spare(0)
                        for t in range(TILES):
                            pe.transpose(bank[:, t * P:(t + 1) * P], pick[:, t, :].bitcast(F32), ident[:])
                        for t in range(TILES):
                            mm = pe.matmul(bank[:, 2 * P:2 * P + 1], pick[:, t, :].bitcast(F32), turn_cw[:, t:t + 1],
                                           start=(t == 0), stop=(t == TILES - 1))
                        mm.then_inc(fill_ready, 1)
                    j, rest = divmod(b - 5, 4)
                    if rest == 0 and 0 <= j < FE_GROUPS:
                        bank = turn_spare(1 + j)
                        pe.wait_ge(acc_taken[j % 2], i * ACC_TURN[j % 2] + (ACC_MOE[j % 2] + j // 2 + 1))
                        for c in range(4):
                            mm = pe.transpose(bank[:, c * P:(c + 1) * P], hid[:, j % 2, c * P:(c + 1) * P], ident[:])
                        mm.then_inc(fill_ready, 1)
                pe.wait_ge(pick_ready, i + 2)
                gather(lambda f: turn_spare(1 + FE_GROUPS + f))
                for f in range(4):
                    h, t = divmod(f, 2)
                    bank = turn_spare(5 + FE_GROUPS + f)
                    pe.wait_ge(y_lo_ready, i * 2 + (h + 1))
                    pe.matmul(bank, pick_t[:, t, :], y_hi[:, h * BANK:(h + 1) * BANK], start=True, stop=False)
                    pe.matmul(bank, pick_t[:, t, :], y_lo[:, h * BANK:(h + 1) * BANK], start=False, stop=True)\
                      .then_inc(fill_ready, 1)

        @block.scalar
        def _(act):
            def bcast(dst, src):
                act.dma_start(dst, src).then_inc(small_landed, 16)

            for l in range(2):
                bcast(head_gain[:, l, :], mem_k_norm[l].partition_broadcast(P))
                bcast(memq_gain[:, l, :], mem_q_norm[l].partition_broadcast(P))
            bcast(diff_gain[:, 0, :], diff_q_norm[0].partition_broadcast(P))
            bcast(diff_gain[:, 1, :], diff_k_norm[0].partition_broadcast(P))
            bcast(sub_gain[:], diff_subln[0].partition_broadcast(P))
            bcast(lam4[:], diff_lambda[0].partition_broadcast(P))
            with nc.allow_non_contiguous_dma(reason="one position a partition"):
                bcast(pos_i[:], positions.rearrange("b (t p) -> p (b t)", p=P))
            bcast(wr[:], w_router[0].rearrange("(k p) e -> p k e", p=P))
            link = chain(act, act_step)
            split_at = [0]

            def split(n, turn=None):
                wait_raw(act, n, turn)
                if turn is None:
                    if n >= SPLIT_SLOTS:
                        act.wait_ge(w_used, n - SPLIT_SLOTS + 1)
                else:
                    act.wait_ge(w_used, turn * TURN_BLOCKS + (n - SPLIT_SLOTS + 1))
                act.copy(w_hi[:, n % SPLIT_SLOTS, :], raw[:, n % RAW_SLOTS, :]).then_inc(hi_ready, 1)

            def split_to(n):
                while split_at[0] < n:
                    split(split_at[0])
                    split_at[0] += 1

            def squares(s, src):
                for t in range(TILES):
                    ins = act.activation(sil[:].rearrange("p a n -> p (a n)"), src[:, t, :], ACT.Square,
                                         accum_out=norm_r[:, s, 0, t:t + 1])
                    if t < TILES - 1:
                        link(ins)
                ins.then_inc(squares_ready, 1)

            def take_hi(f, dst, want_used=None):
                act.wait_ge(fill_ready, f + 1)
                act.copy(dst, ps[:, SPARE + f % 2, 0:BANK].rearrange("p (a n) -> p a n", a=dst.shape[1])).then_inc(fill_hi, 1)

            def split_nat(name):
                for f in range(4):
                    take_hi(FILL[(name, f)], t_hi[:, 2 * f:2 * f + 2, :])

            act.wait_ge(mem_landed, 16)
            squares(0, proj[:, :, 0:D])
            split_to(SPLIT_SLOTS)
            act.wait_ge(x_landed, 16)
            act.wait_ge(rstd_ready, 1)
            squares(1, x)
            split_nat("memT")
            for b in range(BLK_MEM, BLK_MEM + 4):
                split_to(b + 1 + AHEAD)
                if b % 2:
                    l = b // 2
                    act.wait_ge(w_used, b + 1)
                    kv = ps[:, 2 * l:2 * l + 2, :]
                    act.copy(km[:, l, :, :], kv[:, :, 0:4 * HEAD]).then_inc(km_copied, 1)
                    act.copy(vm[:, l, :, :], kv[:, :, 4 * HEAD:8 * HEAD]).then_inc(acc_taken[l], 1)
            act.wait_ge(small_landed, 16 * 10)
            act.copy(wr_hi[:], wr[:]).then_inc(wr_hi_ready, 1)
            act.wait_ge(lam_sums, 1)
            act.activation(lam[:, 2:4], lam[:, 0:2], ACT.Exp).then_inc(lam_exp, 1)

            def unit(l, u):
                n_mix, base, p = UNITS[l] - NMEM, l * UNITS[0], u % 2
                a = att[:, p, :]
                if u >= 2:
                    act.wait_ge(fill_ready, FILL[(f"w{l}", u - 2)] + 1)
                if u < n_mix and l == 0:
                    act.wait_ge(z_ready, base + u + 1)
                    act.activation(a[:, 0:3 * P], ps[:, 2 * p, 0:3 * P], ACT.Sigmoid, scale=SCALE)
                    act.activation(a[:, 3 * P:6 * P], ps[:, 2 * p, 0:3 * P], ACT.Sigmoid, scale=-SCALE)\
                       .then_inc(z_taken[p], 1)
                elif u < n_mix:
                    act.wait_ge(max_ready, NMEM * l + u + 1)
                    for half in range(2):
                        for t, (c0, c1) in enumerate([(0, P), (P, 3 * P)]):
                            v = a[:, half * 3 * P + c0:half * 3 * P + c1]
                            ins = act.activation(v, v, ACT.Exp, bias=stat[:, u % 4, 0, 2 * half + t:2 * half + t + 1],
                                                 accum_out=stat[:, u % 4, 1, 2 * half + t:2 * half + t + 1])
                    ins.then_inc(exp_ready, 1)
                else:
                    act.wait_ge(max_ready, [u - n_mix, NMEM + u][l] + 1)
                    for t in range(TILES):
                        ins = act.activation(a[:, t * S:(t + 1) * S], ps[:, 2 * p, t * S:(t + 1) * S], ACT.Exp,
                                             scale=SCALE, bias=stat[:, u % 4, 0, t:t + 1], accum_out=stat[:, u % 4, 1, t:t + 1])
                    ins.then_inc(z_taken[p], 1)

            def take_weights(l, u):
                f = FILL[(f"w{l}", u)]
                act.wait_ge(fill_ready, f + 1)
                if l * UNITS[0] + u >= 2:
                    act.wait_ge(head_ready, l * UNITS[0] + u - 1)
                n = 3 * P if u < UNITS[l] - NMEM else 4 * P
                act.copy(att_t[:, u % 2, 0:n], ps[:, SPARE + f % 2, 0:n]).then_inc(spare_taken[f % 2], 1)

            for l in range(2):
                split_nat(f"xT{l}")
                for b in range(BLK_IN[l], BLK_OUT[l]):
                    split_to(b + 1 + AHEAD)
                    g, half = divmod(b - BLK_IN[l], 2)
                    if half and g % 2 == 0:
                        p, _ = ACC[f"in{l}.{g}"]
                        act.wait_ge(w_used, b + 1)
                        act.copy(proj[:, :, g * BANK:(g + 1) * BANK], ps[:, 2 * p:2 * p + 2, :]).then_inc(acc_taken[p], 1)
                split_to(BLK_OUT[l] + SPLIT_SLOTS)
                for c in range(0, 7, 2):
                    f = FILL[(f"qk{l}", c)]
                    act.wait_ge(fill_ready, f + 1)
                    act.copy(qk_t[:, c, :], ps[:, SPARE + f % 2, :]).then_inc(spare_taken[f % 2], 1)
                for s in range(UNITS[l] + 1):
                    if s < UNITS[l]:
                        unit(l, s)
                    if s >= 1:
                        take_weights(l, s - 1)
                split_nat(f"oT{l}")
                for b in range(BLK_OUT[l], BLK_OUT[l] + KD // 2):
                    split_to(b + 1 + AHEAD)
                split_to(BLK_OUT[l] + KD // 2 + SPLIT_SLOTS)
                for t in range(TILES):
                    group_taken(act, f"out{l}.{t}")
                squares([2, 4][l], x)
                split_nat(f"fT{l}")
                if l == 1:
                    break
                for b in range(BLK_FF, BLK_IN[1]):
                    split_to(b + 1 + AHEAD)
                    bb = b - BLK_FF
                    if bb % 2 and b < BLK_FD:
                        j = bb // 2
                        p, uses = ACC[f"ff{j}"]
                        act.wait_ge(w_used, b + 1)
                        if j >= 2:
                            act.wait_ge(acc_taken[p], uses)
                        act.activation(sil[:, j % 2, :].rearrange("p (t n) -> p t n", t=2),
                                       ps[:, 2 * p:2 * p + 2, 0:HALF], ACT.Silu).then_inc(sil_ready, 1)
                    j, odd = divmod(bb - 4, 2)
                    if odd == 0 and 0 <= j < FF_GROUPS:
                        take_hi(FILL[("hT", j)], h_hi[:, 2 * j:2 * j + 2, :])
                split_to(BLK_IN[1] + SPLIT_SLOTS)
                act.wait_ge(ang_ready, 1)
                act.activation(ang[:, 4, :, :], ang[:, 2, :, :], ACT.Sin)
                act.activation(ang[:, 5, :, :], ang[:, 3, :, :], ACT.Sin).then_inc(rope_ready, 1)
                for t in range(TILES):
                    group_taken(act, f"fd{t}")
                squares(3, x)

            act.copy(n_hi[:], nat[:]).then_inc(n_hi_ready, 1)
            act.wait_ge(gap_ready, 1)
            act.activation(gap[:, 1, :], gap[:, 0, :], ACT.Exp).then_inc(gap_exp, 1)

            def take_gather(f, f_wait, k):
                f_wait()
                act.copy(g_hi[:, k:k + 4, :], ps[:, SPARE + f % 2, :].rearrange("p (a n) -> p a n", a=4))\
                   .then_inc(spare_taken[f % 2], 1)

            for f in (0, 2):
                F = FILL[("gather", f)]
                take_gather(F, lambda: act.wait_ge(fill_ready, F + 1), 2 * f)
            act.wait_ge(table_ready, 1)
            turns = act.value_load(table_i[0:1, 0:1], min_val=E, max_val=E + MAX_EXTRA)
            with act.Fori(0, turns) as i:
                def filled(f):
                    act.wait_ge(fill_ready, i * TURN_FILLS + (FILL_MOE + f + 1))

                for b in range(TURN_BLOCKS):
                    if b % 4 == 3 and b < GU_BLOCKS:
                        j = b // 4
                        act.wait_ge(w_used, i * TURN_BLOCKS + (BLK_MOE + b + 1))
                        q = (j - 2) % 2
                        if j >= 2:
                            act.wait_ge(acc_taken[q], i * ACC_TURN[q] + (ACC_MOE[q] + j // 2))
                        act.activation(sil[:, j % 2, :], ps[:, 2 * (j % 2), :], ACT.Silu).then_inc(sil_ready, 1)
                    j, rest = divmod(b - 6, 4)
                    if rest == 0 and 0 <= j < FE_GROUPS:
                        filled(1 + j)
                        act.copy(e_hi[:, 4 * j:4 * j + 4, :],
                                 ps[:, SPARE + (FILL_MOE + 1 + j) % 2, :].rearrange("p (a n) -> p a n", a=4))\
                           .then_inc(fill_hi, 1)
                    if b < TURN_BLOCKS - 1:
                        split(BLK_MOE + b + SPLIT_SLOTS, i)
                for f in (0, 2):
                    n = FILL_MOE + 1 + FE_GROUPS + f
                    take_gather(n, lambda: filled(1 + FE_GROUPS + f), 2 * f)
                    h = f // 2
                    act.wait_ge(y_scaled, i * 2 + (h + 1))
                    act.copy(y_hi[:, h * BANK:(h + 1) * BANK], sil[:, h, :]).then_inc(y_hi_ready, 1)
                split(BLK_MOE + TURN_BLOCKS - 1 + SPLIT_SLOTS, i)
                act.wait_ge(y_lo_ready, i * 2 + 2)

        @block.vector
        def _(dve):
            link = chain(dve, dve_step)
            split_at = [0]

            def split(n, turn=None):
                if turn is None:
                    dve.wait_ge(hi_ready, n + 1)
                else:
                    dve.wait_ge(hi_ready, turn * TURN_BLOCKS + (n + 1))
                dve.tensor_tensor(w_lo[:, n % SPLIT_SLOTS, :], raw[:, n % RAW_SLOTS, :],
                                  w_hi[:, n % SPLIT_SLOTS, :].bitcast(F32), ALU.subtract).then_inc(lo_ready, 1)

            def split_to(n):
                while split_at[0] < n:
                    split(split_at[0])
                    split_at[0] += 1

            def norm(s, src):
                dve.wait_ge(rstd_ready, s + 1)
                dve.wait_ge(gain_landed, 16 * (s + 1))
                for t in range(TILES):
                    dve.scalar_tensor_tensor(out=nat[:, t, :], in0=src[:, t, :], scalar=norm_r[:, s, 2, t:t + 1],
                                             in1=gain[:], op0=ALU.mult, op1=ALU.mult).then_inc(nat_ready, 1)

            his = [0]
            normed = [0]

            def take_lo(f, dst, hi):
                his[0] += 1
                dve.wait_ge(fill_hi, his[0])
                dve.tensor_tensor(dst, ps[:, SPARE + f % 2, 0:BANK].rearrange("p (a n) -> p a n", a=dst.shape[1]),
                                  hi.bitcast(F32), ALU.subtract).then_inc(spare_taken[f % 2], 1)

            def split_nat(name):
                for f in range(4):
                    take_lo(FILL[(name, f)], t_lo[:, 2 * f:2 * f + 2, :], t_hi[:, 2 * f:2 * f + 2, :])

            def norm_heads(name, src, g, scale=None):
                m = NORMS[name]
                if m:
                    dve.wait_ge(heads_normed, normed[0])
                normed[0] = m + 1 + (m >= NORMS["k"])
                _, A, N, W = src.shape
                sums = head_r[:, m, 0, 0:A * N].rearrange("p (a n) -> p a n", a=A)
                rstd = head_r[:, m, 1, 0:A * N].rearrange("p (a n) -> p a n", a=A)
                for a in range(A):
                    sq = hid[:].rearrange("p a n -> p (a n)")[:, 0:N * W].rearrange("p (n w) -> p n w", w=W)
                    link(dve.tensor_tensor(sq, src[:, a], src[:, a], ALU.mult))
                    ins = dve.tensor_reduce(sums[:, a, :], sq, AX.X, ALU.add)
                    if a < A - 1:
                        link(ins)
                ins.then_inc(sums_ready, 1)
                dve.wait_ge(head_rstd_ready, m + 1)
                for a in range(A):
                    ins = dve.tensor_tensor(src[:, a], src[:, a], rstd[:, a].unsqueeze(2).to_broadcast([P, N, W]), ALU.mult)
                    if a == A - 1:
                        link(ins)
                for a in range(A):
                    ins = dve.tensor_tensor(src[:, a], src[:, a], g.unsqueeze(1).to_broadcast([P, N, W]), ALU.mult)
                ins.then_inc(heads_normed, 1)

            def add_sums(name, count):
                dve.wait_ge(w_used, count)
                for t in range(TILES):
                    dve.tensor_tensor(x[:, t, :], x[:, t, :], ps[:, 2 * t:2 * t + 2, :].rearrange("p a n -> p (a n)"),
                                      ALU.add).then_inc(acc_taken[t], 1)
                for t in range(TILES):
                    group_taken(dve, f"{name}{t}")

            dve.memset(keep[:], 1.0)
            link(dve.memset(turn_slot[:], -1.0))
            link(dve.memset(turn_w[:], 0.0))
            dve.wait_ge(mem_landed, 16)
            norm(0, proj[:, :, 0:D])
            split_to(SPLIT_SLOTS)
            split_nat("memT")
            dve.wait_ge(fill_ready, FILL[("memT", 3)] + 1)
            norm(1, x)
            dve.wait_ge(small_landed, 16 * 10)
            link(dve.tensor_tensor(hid[:, 0, 0:HEAD], lam4[:, 0, :], lam4[:, 1, :], ALU.mult))
            link(dve.tensor_tensor(hid[:, 0, HEAD:2 * HEAD], lam4[:, 2, :], lam4[:, 3, :], ALU.mult))
            dve.tensor_reduce(lam[:, 0:2], hid[:, 0, 0:2 * HEAD].rearrange("p (a n) -> p a n", a=2), AX.X, ALU.add)\
               .then_inc(lam_sums, 1)
            dve.wait_ge(lam_sums, 1)
            for b in range(BLK_MEM, BLK_MEM + 4):
                split_to(b + 1 + AHEAD)
                if b % 2:
                    l = b // 2
                    dve.wait_ge(km_copied, l + 1)
                    norm_heads(f"km{l}", km[:, l].rearrange("p t (h w) -> p t h w", w=HEAD), head_gain[:, l, :])
            dve.wait_ge(wr_hi_ready, 1)
            dve.tensor_tensor(wr_lo[:], wr[:], wr_hi[:].bitcast(F32), ALU.subtract).then_inc(wr_ready, 1)
            dve.wait_ge(lam_exp, 1)
            link(dve.tensor_tensor(lam[:, 4:5], lam[:, 3:4], lam[:, 2:3], ALU.subtract))
            link(dve.tensor_scalar(lam[:, 4:5], lam[:, 4:5], -LAM_INIT, None, ALU.add))

            def unit(l, u):
                n_mix, base, p = UNITS[l] - NMEM, l * UNITS[0], u % 2
                a = att[:, p, :]
                tiles = [(0, P), (P, 3 * P)]
                if u < n_mix and l == 0:
                    dve.wait_ge(masked_ready, u + 1)
                    for t, (c0, c1) in enumerate(tiles):
                        kp = a[:, 3 * P + c0:3 * P + c1][:, ::-1]
                        ins = dve.tensor_tensor_scan(keep[:, p, c0 + 2 * t:c1 + 2 * t][:, ::-1], kp, kp, 1.0, ALU.mult, ALU.bypass)
                    link(ins)
                    for t, (c0, c1) in enumerate(tiles):
                        ins = dve.tensor_tensor(a[:, c0:c1], a[:, c0:c1], keep[:, p, c0 + 2 * t + 1:c1 + 2 * t + 1], ALU.mult)
                    ins.then_inc(att_ready, 1)
                elif u < n_mix:
                    if u >= 2:
                        dve.wait_ge(fill_ready, FILL[(f"w{l}", u - 2)] + 1)
                    dve.wait_ge(z_ready, base + u + 1)
                    for half in range(2):
                        ins = dve.scalar_tensor_tensor(out=a[:, half * 3 * P:(half + 1) * 3 * P], in0=ps[:, 2 * p + half, 0:3 * P],
                                                       scalar=SCALE, in1=causal[:], op0=ALU.mult, op1=ALU.add)
                    ins.then_inc(z_taken[p], 1)
                    dve.wait_ge(z_taken[p], (base + u) // 2 + 1)
                    for half in range(2):
                        for t, (c0, c1) in enumerate(tiles):
                            ins = dve.tensor_reduce(stat[:, u % 4, 0, 2 * half + t:2 * half + t + 1],
                                                    a[:, half * 3 * P + c0:half * 3 * P + c1], AX.X, ALU.max, negate=True)
                    ins.then_inc(max_ready, 1)
                    dve.wait_ge(exp_ready, u + 1)
                    link(dve.reciprocal(stat[:, u % 4, 2, :], stat[:, u % 4, 1, :]))
                    link(dve.tensor_scalar(stat[:, u % 4, 2, 2:4], stat[:, u % 4, 2, 2:4], lam[:, 4:5], None, ALU.mult))
                    for t, (c0, c1) in enumerate(tiles):
                        ins = dve.tensor_scalar(a[:, 3 * P + c0:3 * P + c1], a[:, 3 * P + c0:3 * P + c1],
                                                stat[:, u % 4, 2, 2 + t:3 + t], None, ALU.mult)
                    link(ins)
                    for t, (c0, c1) in enumerate(tiles):
                        ins = dve.scalar_tensor_tensor(out=a[:, c0:c1], in0=a[:, c0:c1], scalar=stat[:, u % 4, 2, t:t + 1],
                                                       in1=a[:, 3 * P + c0:3 * P + c1], op0=ALU.mult, op1=ALU.add)
                    ins.then_inc(att_ready, 1)
                else:
                    dve.wait_ge(z_ready, base + u + 1)
                    link(dve.tensor_reduce(stat[:, u % 4, 0, 0:TILES], ps[:, 2 * p, :].rearrange("p (t n) -> p t n", t=TILES),
                                           AX.X, ALU.max))
                    dve.tensor_scalar(stat[:, u % 4, 0, 0:TILES], stat[:, u % 4, 0, 0:TILES], -SCALE, None, ALU.mult).then_inc(max_ready, 1)

            def take_head(l, u):
                n_mix = UNITS[l] - NMEM
                o = ps[:, OUT + u % 2, :]
                if u >= n_mix:
                    c0 = MIX + HEAD * (u - n_mix)
                    link(dve.reciprocal(stat[:, u % 4, 2, 0:TILES], stat[:, u % 4, 1, 0:TILES]))
                    dve.wait_ge(head_ready, l * UNITS[0] + u + 1)
                    for t in range(TILES):
                        ins = dve.tensor_scalar(nat[:, t, c0:c0 + HEAD], o[:, t * HEAD:(t + 1) * HEAD],
                                                stat[:, u % 4, 2, t:t + 1], None, ALU.mult)
                else:
                    n = HEAD * (l + 1)
                    dve.wait_ge(head_ready, l * UNITS[0] + u + 1)
                    ins = dve.tensor_copy(nat[:, :, n * u:n * (u + 1)], o[:, 0:2 * n].rearrange("p (t n) -> p t n", t=TILES))
                ins.then_inc(head_taken, 1)

            for l in range(2):
                split_nat(f"xT{l}")
                for b in range(BLK_IN[l], BLK_OUT[l]):
                    split_to(b + 1 + AHEAD)
                    g, half = divmod(b - BLK_IN[l], 2)
                    if half and g % 2 == 1:
                        p, uses = ACC[f"in{l}.{g}"]
                        dve.wait_ge(w_used, b + 1)
                        dve.tensor_copy(proj[:, :, g * BANK:(g + 1) * BANK], ps[:, 2 * p:2 * p + 2, :]).then_inc(acc_taken[p], 1)
                        if l == 1 and g == 1:
                            group_taken(dve, "in1.0")
                            group_taken(dve, "in1.1")
                            norm_heads("q", proj[:, :, 0:MIX].rearrange("p t (h w) -> p t h w", w=HEAD), diff_gain[:, 0, :])
                    if l == 1 and half and g == 2:
                        group_taken(dve, "in1.2")
                        norm_heads("k", proj[:, :, MIX:QKW].rearrange("p t (h w) -> p t h w", w=HEAD), diff_gain[:, 1, :])
                        dve.wait_ge(heads_normed, 5)
                        dve.wait_ge(rope_ready, 1)
                        half_rope = ROPE // 2
                        n = 2 * 2 * NDIFF
                        for t in range(TILES):
                            heads = proj[:, t, 0:QKW].rearrange("p (h w) -> p h w", w=HEAD)
                            t1, t2 = heads[:, :, 0:half_rope], heads[:, :, half_rope:ROPE]
                            sin, cos = (ang[:, 4 + a, t, :].unsqueeze(1).to_broadcast([P, n, half_rope]) for a in range(2))
                            tmp = [hid[:, a // 2, a % 2 * HALF:a % 2 * HALF + n * half_rope].rearrange("p (h w) -> p h w", w=half_rope)
                                   for a in range(4)]
                            dve.tensor_tensor(tmp[0], t1, cos, ALU.mult)
                            dve.tensor_tensor(tmp[1], t2, sin, ALU.mult)
                            dve.tensor_tensor(tmp[2], t2, cos, ALU.mult)
                            link(dve.tensor_tensor(tmp[3], t1, sin, ALU.mult))
                            dve.tensor_tensor(t1, tmp[0], tmp[1], ALU.subtract)
                            ins = dve.tensor_tensor(t2, tmp[2], tmp[3], ALU.add)
                            if t < TILES - 1:
                                link(ins)
                        ins.then_inc(heads_normed, 1)
                if l == 0:
                    for m in range(2):
                        f = FILL[("km", m)]
                        dve.wait_ge(fill_ready, f + 1)
                        dve.tensor_copy(km_t[:, m].rearrange("p c s -> p (c s)"), ps[:, SPARE + f % 2, :]).then_inc(spare_taken[f % 2], 1)
                group_taken(dve, f"in{l}.{IN_GROUPS - 1}")
                norm_heads(f"qm{l}", proj[:, :, 3 * MIX:WIN].rearrange("p t (h w) -> p t h w", w=HEAD), memq_gain[:, l, :])
                split_to(BLK_OUT[l] + SPLIT_SLOTS)
                for c in range(1, 7, 2):
                    f = FILL[(f"qk{l}", c)]
                    dve.wait_ge(fill_ready, f + 1)
                    dve.tensor_copy(qk_t[:, c, :], ps[:, SPARE + f % 2, :]).then_inc(spare_taken[f % 2], 1)
                for s in range(UNITS[l] + 2):
                    if s < UNITS[l]:
                        unit(l, s)
                    if s >= 2:
                        take_head(l, s - 2)
                if l == 1:
                    dve.wait_ge(head_taken, sum(UNITS))
                    link(dve.tensor_scalar(sub_gain[:], sub_gain[:], 1.0 - LAM_INIT, None, ALU.mult))
                    norm_heads("sub", nat[:, :, 0:MIX].rearrange("p t (h w) -> p t h w", w=2 * HEAD), sub_gain[:])
                split_nat(f"oT{l}")
                for b in range(BLK_OUT[l], BLK_OUT[l] + KD // 2):
                    split_to(b + 1 + AHEAD)
                add_sums(f"out{l}.", BLK_OUT[l] + KD // 2)
                split_to(BLK_OUT[l] + KD // 2 + SPLIT_SLOTS)
                norm([2, 4][l], x)
                split_nat(f"fT{l}")
                if l == 1:
                    break
                for b in range(BLK_FF, BLK_IN[1]):
                    split_to(b + 1 + AHEAD)
                    bb = b - BLK_FF
                    if bb % 2 and b < BLK_FD:
                        j = bb // 2
                        p, uses = ACC[f"ff{j}"]
                        dve.wait_ge(sil_ready, j + 1)
                        if j >= 2:
                            dve.wait_ge(fill_ready, FILL[("hT", j - 2)] + 1)
                        dve.tensor_tensor(hid[:, j % 2, :].rearrange("p (t n) -> p t n", t=2),
                                          ps[:, 2 * p:2 * p + 2, HALF:BANK], sil[:, j % 2, :].rearrange("p (t n) -> p t n", t=2),
                                          ALU.mult).then_inc(acc_taken[p], 1)
                    j, odd = divmod(bb - 4, 2)
                    if odd == 0 and 0 <= j < FF_GROUPS:
                        take_lo(FILL[("hT", j)], h_lo[:, 2 * j:2 * j + 2, :], h_hi[:, 2 * j:2 * j + 2, :])
                add_sums("fd", BLK_IN[1])
                split_to(BLK_IN[1] + SPLIT_SLOTS)
                norm(3, x)

            R = lambda a: route[:, a]
            wide = lambda v: v.unsqueeze(2).to_broadcast([P, TILES, E])
            down8 = down_row[:].unsqueeze(1).to_broadcast([P, TILES, E])
            dve.wait_ge(n_hi_ready, 1)
            dve.tensor_tensor(n_lo[:], nat[:], n_hi[:].bitcast(F32), ALU.subtract).then_inc(n_ready, 1)
            dve.wait_ge(logits_ready, 1)
            link(dve.tensor_copy(R(LOGIT), ps[:, OUT, 0:TILES * E].rearrange("p (t e) -> p t e", e=E)))
            for a in range(2):
                src, onehot = (LOGIT, FIRST) if a == 0 else (REST, SECOND)
                link(dve.tensor_reduce(gap[:, 2 + a, :], R(src), AX.X, ALU.max))
                link(dve.tensor_tensor(R(TMP), R(src), wide(gap[:, 2 + a, :]), ALU.is_equal))
                link(dve.tensor_tensor(R(TMP), R(TMP), down8, ALU.mult))
                link(dve.tensor_reduce(gap[:, 4, :], R(TMP), AX.X, ALU.min))
                link(dve.tensor_tensor(R(onehot), down8, wide(gap[:, 4, :]), ALU.is_equal))
                if a == 0:
                    link(dve.scalar_tensor_tensor(out=R(REST), in0=R(FIRST), scalar=NEG_BIG, in1=R(LOGIT), op0=ALU.mult, op1=ALU.add))
            dve.tensor_tensor(gap[:, 0, :], gap[:, 3, :], gap[:, 2, :], ALU.subtract).then_inc(gap_ready, 1)
            dve.tensor_tensor(R(MASK), R(FIRST), R(SECOND), ALU.add).then_inc(mask_ready, 1)
            dve.wait_ge(gap_exp, 1)
            link(dve.tensor_scalar(gap[:, 5, :], gap[:, 1, :], 1.0, None, ALU.add))
            link(dve.reciprocal(gap[:, 6, :], gap[:, 5, :]))
            link(dve.tensor_tensor(gap[:, 7, :], gap[:, 1, :], gap[:, 6, :], ALU.mult))
            link(dve.tensor_tensor(R(FIRST), R(FIRST), wide(gap[:, 6, :]), ALU.mult))
            link(dve.tensor_tensor(R(SECOND), R(SECOND), wide(gap[:, 7, :]), ALU.mult))
            link(dve.tensor_tensor(turn_w[:, :, 0:E], R(FIRST), R(SECOND), ALU.add))
            dve.wait_ge(places_ready, 1)
            place = ps[:, OUT + 1, :]
            link(dve.scalar_tensor_tensor(out=R(PLACE1), in0=place[:, 0:2 * E].rearrange("p (t e) -> p t e", e=E), scalar=1.0,
                                          in1=R(MASK), op0=ALU.add, op1=ALU.mult))
            link(dve.tensor_scalar(turn_slot[:, :, 0:E], R(PLACE1), -1.0, None, ALU.add))

            def make_pick(col, waited=True):
                dve.tensor_copy(turn_cw[:].unsqueeze(2), turn_w[:, :, col])
                for t in range(TILES):
                    ins = dve.tensor_scalar(pick[:, t, :], slot_row[:], turn_slot[:, t, col], None, ALU.is_equal)
                ins.then_inc(pick_ready, 1)

            make_pick(slice(0, 1))
            link(dve.tensor_scalar(over[:, 0, :], place[:, 2 * E:3 * E], float(P), None, ALU.is_gt))
            link(dve.tensor_tensor_scan(over[:, 1, :], over[:, 0, :], over[:, 0, :], 0.0, ALU.add, ALU.bypass))
            link(dve.tensor_tensor(over[:, 2, :], over[:, 1, :], over[:, 0, :], ALU.subtract))
            link(dve.tensor_scalar(table[:, 0:1], over[:, 1, E - 1:E], float(E), None, ALU.add))
            for r in range(MAX_EXTRA):
                link(dve.scalar_tensor_tensor(out=over[:, 3, :], in0=over[:, 2, :], scalar=float(r), in1=over[:, 0, :],
                                              op0=ALU.is_equal, op1=ALU.mult))
                sel = over[:, 3, :].unsqueeze(1).to_broadcast([P, TILES, E])
                link(dve.tensor_tensor(R(TMP), R(PLACE1), sel, ALU.mult))
                link(dve.tensor_reduce(gap[:, 4, :], R(TMP), AX.X, ALU.add))
                link(dve.tensor_scalar(turn_slot[:, :, E + r], gap[:, 4, :], -1.0 - P, None, ALU.add))
                link(dve.tensor_tensor(R(TMP), turn_w[:, :, 0:E], sel, ALU.mult))
                link(dve.tensor_reduce(turn_w[:, :, E + r], R(TMP), AX.X, ALU.add))
                link(dve.tensor_tensor(over[:, 4, :], over[:, 3, :], slot_row[:, 0:E], ALU.mult))
                link(dve.tensor_reduce(table[:, 1 + r:2 + r], over[:, 4, :], AX.X, ALU.add))
            dve.tensor_copy(table_i[:], table[:]).then_inc(table_ready, 1)

            def take_gather(f, k):
                dve.tensor_copy(g_lo[:, k:k + 4, :], ps[:, SPARE + f % 2, :].rearrange("p (a n) -> p a n", a=4))\
                   .then_inc(spare_taken[f % 2], 1)

            for f in (1, 3):
                F = FILL[("gather", f)]
                dve.wait_ge(fill_ready, F + 1)
                take_gather(F, 2 * (f - 1))
            dve.wait_ge(table_ready, 1)
            turns = dve.value_load(table_i[0:1, 0:1], min_val=E, max_val=E + MAX_EXTRA)
            HI_MOE, SIL_MOE = his[0], FF_GROUPS
            with dve.Fori(0, turns) as i:
                def filled(f):
                    dve.wait_ge(fill_ready, i * TURN_FILLS + (FILL_MOE + f + 1))
                    return FILL_MOE + f

                for b in range(TURN_BLOCKS):
                    if b % 4 == 3 and b < GU_BLOCKS:
                        j = b // 4
                        dve.wait_ge(sil_ready, i * FE_GROUPS + (SIL_MOE + j + 1))
                        if j >= 2:
                            filled(1 + j - 2)
                        dve.tensor_tensor(hid[:, j % 2, :], ps[:, 2 * (j % 2) + 1, :], sil[:, j % 2, :], ALU.mult)\
                           .then_inc(acc_taken[j % 2], 1)
                    if b == 3:
                        f = filled(0)
                        dve.tensor_copy(pick_t[:].rearrange("p t n -> p (t n)"), ps[:, SPARE + f % 2, 0:2 * P])
                        dve.tensor_copy(slot_w[:], ps[:, SPARE + f % 2, 2 * P:2 * P + 1]).then_inc(spare_taken[f % 2], 1)
                    if b == 15:
                        make_pick(bass.ds(i + 1, 1))
                    j, rest = divmod(b - 6, 4)
                    if rest == 0 and 0 <= j < FE_GROUPS:
                        n = FILL_MOE + 1 + j
                        dve.wait_ge(fill_hi, i * FE_GROUPS + (HI_MOE + j + 1))
                        dve.tensor_tensor(e_lo[:, 4 * j:4 * j + 4, :], ps[:, SPARE + n % 2, :].rearrange("p (a n) -> p a n", a=4),
                                          e_hi[:, 4 * j:4 * j + 4, :].bitcast(F32), ALU.subtract).then_inc(spare_taken[n % 2], 1)
                    if b < TURN_BLOCKS - 1:
                        split(BLK_MOE + b + SPLIT_SLOTS, i)
                dve.wait_ge(w_used, i * TURN_BLOCKS + (BLK_MOE + TURN_BLOCKS))
                for h in range(2):
                    dve.tensor_scalar(sil[:, h, :], ps[:, OUT + h, :], slot_w[:], None, ALU.mult).then_inc(y_scaled, 1)
                    f = 1 + 2 * h
                    take_gather(filled(1 + FE_GROUPS + f), 2 * (f - 1))
                for h in range(2):
                    dve.wait_ge(y_hi_ready, i * 2 + (h + 1))
                    dve.tensor_tensor(y_lo[:, h * BANK:(h + 1) * BANK], sil[:, h, :], y_hi[:, h * BANK:(h + 1) * BANK].bitcast(F32),
                                      ALU.subtract).then_inc(y_lo_ready, 1)
                split(BLK_MOE + TURN_BLOCKS - 1 + SPLIT_SLOTS, i)
                for f in range(4):
                    h, t = divmod(f, 2)
                    n = filled(5 + FE_GROUPS + f)
                    xs = x[:, t, h * BANK:(h + 1) * BANK]
                    dve.tensor_tensor(xs, xs, ps[:, SPARE + n % 2, :], ALU.add).then_inc(spare_taken[n % 2], 1)

        @block.gpsimd
        def _(pool):
            link = chain(pool, pool_step)
            gains = [mem_norm, attn_norm[0], ffn_norm[0], attn_norm[1], ffn_norm[1]]

            def load_gain(s):
                if s:
                    pool.wait_ge(nat_ready, TILES * s)
                pool.dma_start(gain[:], gains[s].partition_broadcast(P)).then_inc(gain_landed, 16)

            def rsqrt(dst, src, width, n):
                link(pool.tensor_scalar(dst, src, 1.0 / width, EPS, ALU.mult, ALU.add))
                return pool.tensor_tensor(dst, dst, minus_half[:, 0:n], ALU.pow)

            def norm_rstd(s):
                load_gain(s)
                pool.wait_ge(squares_ready, s + 1)
                rsqrt(norm_r[:, s, 2, :], norm_r[:, s, 0, :], D, TILES).then_inc(rstd_ready, 1)

            def head_rstd(name):
                m = NORMS[name]
                pool.wait_ge(sums_ready, m + 1)
                n = NORM_N[m]
                rsqrt(head_r[:, m, 1, 0:n], head_r[:, m, 0, 0:n], NORM_W[m], n).then_inc(head_rstd_ready, 1)

            link(pool.memset(minus_half[:], -0.5))
            link(pool.memset(ident[:], 0.0))
            link(pool.affine_select(out=ident[:], in_=ident[:], compare_op=ALU.not_equal, fill=1.0, base=0,
                                    pattern=[[-1, P]], channel_multiplier=1))
            link(pool.memset(ones[:], 1.0))
            link(pool.affine_select(out=before[:], in_=ones[:], compare_op=ALU.is_ge, fill=0.0, base=-1,
                                    pattern=[[1, P]], channel_multiplier=-1))
            link(pool.memset(causal[:], 0.0))
            for c in (0, 2 * P):
                link(pool.affine_select(out=causal[:, c:c + P], in_=causal[:, c:c + P], compare_op=ALU.is_ge, fill=NEG_BIG,
                                        base=0, pattern=[[-1, P]], channel_multiplier=1))
            link(pool.iota(slot_row[:], pattern=[[1, P]], base=0, channel_multiplier=0, allow_small_or_imprecise_dtypes=True))
            link(pool.iota(down_row[:], pattern=[[1, E]], base=-E, channel_multiplier=0, allow_small_or_imprecise_dtypes=True))
            for j in range(ROPE // 2):
                link(pool.memset(inv_freq[:, :, j], float(np.float32(ROPE_THETA ** (-2 * j / ROPE)))))
            pool.memset(table[:], 0.0).then_inc(consts_ready, 1)
            norm_rstd(0)
            norm_rstd(1)
            head_rstd("km0")
            head_rstd("km1")
            pool.wait_ge(small_landed, 16 * 10)
            A = lambda a: ang[:, a]
            two_pi = 2 * math.pi
            parts = [6.28125, float(np.float32(two_pi - 6.28125).astype(np.float16))]
            parts.append(two_pi - sum(parts))
            link(pool.tensor_copy(A(1)[:, :, 0], pos_i[:]))
            link(pool.tensor_tensor(A(0), inv_freq[:], A(1)[:, :, 0:1].to_broadcast([P, TILES, ROPE // 2]), ALU.mult))
            link(pool.tensor_scalar(A(1), A(0), 1.0 / two_pi, None, ALU.mult))
            link(pool.tensor_copy(ang_i[:], A(1)))
            link(pool.tensor_copy(A(1), ang_i[:]))
            for part in parts:
                link(pool.tensor_scalar(A(2), A(1), -part, None, ALU.mult))
                link(pool.tensor_tensor(A(0), A(0), A(2), ALU.add))

            def into_range(v):
                for op, bound, back in ((ALU.is_lt, -math.pi, two_pi), (ALU.is_gt, math.pi, -two_pi)):
                    link(pool.tensor_scalar(A(4), v, bound, back, op, ALU.mult))
                    link(pool.tensor_tensor(v, v, A(4), ALU.add))
                return pool.tensor_scalar(v, v, 3.1415925, -3.1415925, ALU.min, ALU.max)

            link(pool.tensor_copy(A(2), A(0)))
            link(into_range(A(2)))
            link(pool.tensor_scalar(A(3), A(2), math.pi / 2, None, ALU.add))
            into_range(A(3)).then_inc(ang_ready, 1)
            head_rstd("qm0")
            for u in range(NSB):
                p = u % 2
                pool.wait_ge(z_taken[p], u // 2 + 1)
                for c0, fill in ((0, 0.0), (3 * P, 1.0)):
                    v = att[:, p, c0:c0 + 4 * P].rearrange("p (a n) -> p a n", a=2)[:, :, 0:P]
                    ins = pool.affine_select(out=v, in_=v, compare_op=ALU.is_ge, fill=fill, base=-1,
                                             pattern=[[0, 2], [-1, P]], channel_multiplier=1)
                ins.then_inc(masked_ready, 1)
            norm_rstd(2)
            norm_rstd(3)
            for name in ("q", "k", "qm1", "sub"):
                head_rstd(name)
            norm_rstd(4)


_INS = ["x", "mem", "positions", "attn_norm", "w_in", "w_out", "mem_norm", "w_mem_kv", "mem_q_norm", "mem_k_norm",
        "diff_q_norm", "diff_k_norm", "diff_lambda", "diff_subln", "ffn_norm", "dense_w_gate_up", "dense_w_down",
        "w_router", "moe_w_gate_up", "moe_w_down"]


def kernel(**inputs):
    import concourse.bacc as _bacc
    from concourse.bass_utils import run_bass_kernel_spmd as _run

    nc = _bacc.Bacc("TRN2", target_bir_lowering=False, num_devices=1, dynamic_dma_scratch_size=4096)
    arrays, args = {}, []
    for name in _INS:
        a = np.ascontiguousarray(inputs[name])
        arrays[f"in_{name}"] = a
        args.append(nc.dram_tensor(f"in_{name}", a.shape, mybir.dt.from_np(a.dtype), kind="ExternalInput").ap())
    out = nc.dram_tensor("out_x", inputs["x"].shape, F32, kind="ExternalOutput").ap()
    build(nc, *args, out)
    r = _run(nc, [arrays], core_ids=[0])
    return r.results[0]["out_x"]
```

```python
import math
from contextlib import ExitStack

import numpy as np

import concourse.bass as bass
from concourse import mybir

ALU = mybir.AluOpType
ACT = mybir.ActivationFunctionType
AX = mybir.AxisListType
F32 = mybir.dt.float32
F32R = mybir.dt.float32r
I32 = mybir.dt.int32

P = 128
BANK = 512
RAW_SLOTS = 6
SPLIT_SLOTS = 3
AHEAD = 2
HEAD = 64
ROPE = HEAD // 4
ROPE_THETA = 500000.0
EPS = 1e-6
NEG_BIG = -1e30


def build(nc, x_in, mem, positions, attn_norm, w_in, w_out, mem_norm, w_mem_kv, mem_q_norm, mem_k_norm,
          diff_q_norm, diff_k_norm, diff_lambda, diff_subln, ffn_norm, dense_w_gate_up, dense_w_down,
          w_router, moe_w_gate_up, moe_w_down, out):
    _, S, D = x_in.shape
    TILES = S // P
    KD = D // P
    MIX = 3 * D // 4
    WIN = w_in.shape[2]
    FF = dense_w_down.shape[1]
    E = w_router.shape[2]
    FE = moe_w_down.shape[2]
    HALF = BANK // 2
    SCALE = float(HEAD) ** -0.5
    LAM_INIT = 0.8 - 0.6 * math.exp(-0.3 * 1)
    BLOCK = 4 * BANK
    QKW = 2 * MIX
    NSB = MIX // HEAD
    NDIFF = MIX // (2 * HEAD)
    NMEM = (D - MIX) // HEAD
    IN_GROUPS = WIN // BANK
    FF_GROUPS = FF // HALF
    FE_GROUPS = FE // BANK
    assert TILES == 2 and MIX == 768 and WIN == 5 * BANK and FF % HALF == 0 and FE % BANK == 0 and D == 2 * BANK

    BLK_IN, BLK_OUT = [0, 0], [0, 0]
    BLK_IN[0], n = 0, 2 * IN_GROUPS
    BLK_MEM, n = n, n + 4
    BLK_OUT[0], n = n, n + KD // 2
    BLK_FF, n = n, n + 2 * FF_GROUPS
    BLK_FD, n = n, n + FF // P // 2
    BLK_IN[1], n = n, n + 2 * IN_GROUPS
    BLK_OUT[1], n = n, n + KD // 2
    BLK_MOE = n
    GU_BLOCKS = 4 * FE_GROUPS
    DOWN_BLOCKS = FE // P // 2
    TURN_BLOCKS = GU_BLOCKS + DOWN_BLOCKS
    assert TURN_BLOCKS % RAW_SLOTS == 0 and TURN_BLOCKS % SPLIT_SLOTS == 0
    UNITS = [NSB + NMEM, NDIFF + NMEM]
    LOGIT, REST, FIRST, SECOND, MASK, PLACE1, TMP = range(7)
    MIXED = [BLK_MEM, BLK_IN[1] + 2 * (IN_GROUPS - 1)]
    PIECES = [4 * (BLK_OUT[l] - MIXED[l]) for l in range(2)]
    PIECE_AT = [{2: [0, 1], 3: [2, 3], **{i: [i] for i in range(4, PIECES[0])}},
                {s: [2 * s, 2 * s + 1] for s in range(PIECES[1] // 2)}]
    SPLIT_AT = [[3, 7, 11, 15], [8, 10]]
    LAG = [1, 2]
    STEP_FILLS = [{0: [("qk0", 1), ("memT", 0), ("memT", 1)], 1: [("memT", 2), ("memT", 3)], 2: [("qk0", 2)], 4: [("qk0", 3)],
                   6: [("qk0", 4)], 8: [("qk0", 5)], 10: [("qk0", 6)], 11: [("km", 0)]},
                  {0: [("qk1", 1)], 1: [("qk1", 2)], 2: [("qk1", 3)], 3: [("qk1", 4)], 4: [("qk1", 5), ("km", 1)],
                   6: [("qk1", 6)]}]
    fills = []
    for l in range(2):
        fills += [(f"xT{l}", f) for f in range(4)] + [(f"qk{l}", 0)]
        for s in range(UNITS[l] + LAG[l]):
            fills += STEP_FILLS[l].get(s, []) + ([(f"w{l}", s - LAG[l])] if s >= LAG[l] else [])
        fills += [(f"oT{l}", f) for f in range(4)] + [(f"fT{l}", f) for f in range(4)]
        fills += [("hT", j) for j in range(FF_GROUPS)] if l == 0 else []
    fills += [("gather", f) for f in range(4)]
    FILL = {name: i for i, name in enumerate(fills)}
    FILL_MOE = len(fills)
    TURN_FILLS = 1 + FE_GROUPS + 4 + 4
    assert TURN_FILLS % 2 == 0
    GATHER_AT = [GU_BLOCKS + 3 + 2 * f for f in range(4)]
    MAX_EXTRA = TILES * S // (P + 1)

    ctx = ExitStack()
    with ctx:
        def sb(name, shape, dt=F32, to=None):
            return (to or ctx).enter_context(nc.sbuf_tensor(name, shape, dt))

        def sem(name):
            return ctx.enter_context(nc.semaphore(name))

        raw = sb("raw", [P, RAW_SLOTS, BLOCK])
        w_hi = sb("w_hi", [P, SPLIT_SLOTS, BLOCK], F32R)
        w_lo = sb("w_lo", [P, SPLIT_SLOTS, BLOCK], F32R)
        x = sb("x", [P, TILES, D])
        nat = sb("nat", [P, TILES, D])
        t_hi = sb("t_hi", [P, KD, S], F32R)
        t_lo = sb("t_lo", [P, KD, S], F32R)
        sil = sb("sil", [P, 2, BANK])
        hid = sb("hid", [P, 2, BANK])
        gain = sb("gain", [P, D])
        km_t = sb("km_t", [P, 2, 2, S])
        vm = sb("vm", [P, 2, TILES, 4 * HEAD])
        km = sb("km", [P, 2, TILES, 4 * HEAD])
        ident = sb("ident", [P, P])
        ones = sb("ones", [P, P])
        before = sb("before", [P, P])
        slot_row = sb("slot_row", [P, P])
        causal = sb("causal", [P, 3 * P])
        head_gain = sb("head_gain", [P, 2, HEAD])
        memq_gain = sb("memq_gain", [P, 2, HEAD])
        diff_gain = sb("diff_gain", [P, 2, HEAD])
        sub_gain = sb("sub_gain", [P, 2 * HEAD])
        lam4 = sb("lam4", [P, 4, HEAD])
        pos_i = sb("pos_i", [P, TILES], I32)
        norm_r = sb("norm_r", [P, 5, 3, TILES])
        stat = sb("stat", [P, 4, 3, 4])
        lam = sb("lam", [P, 5])
        gap = sb("gap", [P, 8, TILES])
        minus_half = sb("minus_half", [P, 24])
        inv_freq = sb("inv_freq", [P, TILES, ROPE // 2])
        down_row = sb("down_row", [P, E])
        ang = sb("ang", [P, 6, TILES, ROPE // 2])
        ang_i = sb("ang_i", [P, TILES, ROPE // 2], I32)
        head_r = sb("head_r", [P, 7, 2, 24])
        wr = sb("wr", [P, KD, E])
        wr_split = sb("wr_split", [P, KD, 2 * E], F32R)
        logit_t = sb("logit_t", [2 * E, S])
        route = sb("route", [P, 7, TILES, E])
        turn_slot = sb("turn_slot", [P, TILES, 12])
        turn_w = sb("turn_w", [P, TILES, 12])
        over = sb("over", [P, 5, E])
        table = sb("table", [P, 4])
        table_i = sb("table_i", [P, 4], I32)
        pick = sb("pick", [P, TILES, P], F32R)
        pick_t = sb("pick_t", [P, TILES, P], F32R)
        turn_cw = sb("turn_cw", [P, TILES])
        slot_w = sb("slot_w", [P, 1])

        with ExitStack() as here:
            proj = sb("proj", [P, TILES, WIN], to=here)
            qk_t = sb("qk_t", [P, 7, 2 * S], to=here)
            att = sb("att", [P, 2, 2 * BANK], to=here)
            keep = sb("keep", [P, 2, BANK], to=here)
            att_t = sb("att_t", [P, 2, BANK], to=here)
        with ExitStack() as here:
            h_hi = sb("h_hi", [P, FF // P, S], F32R, to=here)
            h_lo = sb("h_lo", [P, FF // P, S], F32R, to=here)
        with ExitStack() as here:
            e_hi = sb("e_hi", [P, FE // P, P], F32R, to=here)
            e_lo = sb("e_lo", [P, FE // P, P], F32R, to=here)
            n_hi = sb("n_hi", [P, TILES, D], F32R, to=here)
            n_lo = sb("n_lo", [P, TILES, D], F32R, to=here)
        g_hi, g_lo = (t[:, 0:KD // 2, :].rearrange("p a (b s) -> p (a b) s", b=2) for t in (t_hi, t_lo))
        y_hi, y_lo = (t[:, KD // 2:KD, :].rearrange("p a s -> p (a s)") for t in (t_hi, t_lo))

        ps = ctx.enter_context(nc.psum_tensor("ps", [P, 8, BANK], F32))
        SPARE = 4
        OUT = 6

        raw_landed = [sem(f"raw_landed{s}") for s in range(RAW_SLOTS)]
        hi_ready, lo_ready = sem("hi_ready"), sem("lo_ready")
        w_used = sem("w_used")
        fill_ready, fill_hi = sem("fill_ready"), sem("fill_hi")
        spare_taken = [sem(f"spare_taken{b}") for b in range(2)]
        acc_taken = [sem(f"acc_taken{b}") for b in range(2)]
        z_ready, z_taken = sem("z_ready"), [sem(f"z_taken{b}") for b in range(2)]
        head_ready, head_taken = sem("head_ready"), sem("head_taken")
        small_landed, mem_landed = sem("small_landed"), sem("mem_landed")
        x_landed = [sem(f"x_landed{t}") for t in range(TILES)]
        gain_landed, consts_ready = sem("gain_landed"), sem("consts_ready")
        squares_ready, rstd_ready, nat_ready = sem("squares_ready"), sem("rstd_ready"), sem("nat_ready")
        km_copied, sums_ready, head_rstd_ready, heads_normed = (
            sem("km_copied"), sem("sums_ready"), sem("head_rstd_ready"), sem("heads_normed"))
        masked_ready, max_ready, exp_ready, att_ready = (
            sem("masked_ready"), sem("max_ready"), sem("exp_ready"), sem("att_ready"))
        sil_ready = sem("sil_ready")
        tile0_summed = sem("tile0_summed")
        lam_sums, lam_exp = sem("lam_sums"), sem("lam_exp")
        ang_ready, rope_ready = sem("ang_ready"), sem("rope_ready")
        wr_hi_ready, wr_ready = sem("wr_hi_ready"), sem("wr_ready")
        logits_ready, gap_ready, gap_exp = sem("logits_ready"), sem("gap_ready"), sem("gap_exp")
        logits_copied = sem("logits_copied")
        mask_ready, places_ready, table_ready = sem("mask_ready"), sem("places_ready"), sem("table_ready")
        n_hi_ready, n_ready, pick_ready = sem("n_hi_ready"), sem("n_ready"), sem("pick_ready")
        y0_summed = sem("y0_summed")
        y_scaled, y_hi_ready, y_lo_ready = sem("y_scaled"), sem("y_hi_ready"), sem("y_lo_ready")
        dve_step, act_step, pool_step = sem("dve_step"), sem("act_step"), sem("pool_step")
        stored = sem("stored")

        def chain(eng, own):
            done = [0]

            def link(ins):
                done[0] += 1
                ins.then_inc(own, 1)
                eng.wait_ge(own, done[0])
            return link

        def taken(eng, f):
            eng.wait_ge(spare_taken[f % 2], f // 2 + 1)

        groups = []
        for l in range(2):
            groups += [(f"in{l}.{g}", 1 if l and g == IN_GROUPS - 1 else g % 2) for g in range(IN_GROUPS)]
            groups += [(f"mem{g}", 1) for g in range(2)] if l == 0 else []
            groups += [(f"out{l}.{p}", p) for p in range(2)]
            if l == 0:
                groups += [(f"ff{g}", g % 2) for g in range(FF_GROUPS)] + [(f"fd{p}", p) for p in range(2)]
        ACC = {name: (p, sum(q == p for _, q in groups[:i])) for i, (name, p) in enumerate(groups)}

        def group_taken(eng, name):
            p, uses = ACC[name]
            eng.wait_ge(acc_taken[p], uses + 1)

        ACC_MOE = [sum(q == p for _, q in groups) for p in range(2)]
        ACC_TURN = [(FE_GROUPS + 1) // 2, FE_GROUPS // 2]
        NORMS = {"qm0": 0, "km0": 1, "km1": 2, "q": 3, "k": 4, "qm1": 5, "sub": 6}
        NORM_N = [2 * NMEM] * 3 + [2 * 2 * NDIFF] * 2 + [2 * NMEM, 2 * NDIFF]
        NORM_W = [HEAD] * 6 + [2 * HEAD]

        block = ctx.enter_context(nc.Block())

        def rows(w, k0, kn, c0, cn):
            return w[k0 * P:(k0 + kn) * P, c0:c0 + cn].rearrange("(k p) n -> p k n", p=P)

        def halves(slot):
            v = slot.rearrange("p (k h n) -> p k h n", k=4, h=2)
            return v[:, :, 0, :], v[:, :, 1, :]

        dense = []
        for l in range(2):
            dense += [[(None, rows(w_in[l], k, 4, g * BANK, BANK))] for g in range(IN_GROUPS) for k in (0, 4)]
            if l == 0:
                dense += [[(None, rows(w_mem_kv[m], k, 4, 0, BANK))] for m in range(2) for k in (0, 4)]
            dense += [[(None, rows(w_out[l], k, 2, 0, D))] for k in range(0, KD, 2)]
            if l == 0:
                dense += [[(h, rows(dense_w_gate_up[0], k, 4, h * FF + g * HALF, HALF)) for h in range(2)]
                          for g in range(FF_GROUPS) for k in (0, 4)]
                dense += [[(None, rows(dense_w_down[0], k, 2, 0, D))] for k in range(0, FF // P, 2)]
        assert len(dense) == BLK_MOE

        def raw_count(n):
            return 16 * sum(len(dense[m]) for m in range(n % RAW_SLOTS, n + 1, RAW_SLOTS))

        RAW_MOE = [16 * (1 + sum(len(dense[m]) for m in range(s, BLK_MOE, RAW_SLOTS))) for s in range(RAW_SLOTS)]

        def wait_raw(eng, n, turn=None):
            s = n % RAW_SLOTS
            if turn is None and n < BLK_MOE:
                eng.wait_ge(raw_landed[s], raw_count(n))
            else:
                at = RAW_MOE[s] + 16 * ((n - BLK_MOE) // RAW_SLOTS)
                eng.wait_ge(raw_landed[s], at if turn is None else turn * (16 * TURN_BLOCKS // RAW_SLOTS) + at)

        @block.sync
        def _(sp):
            for t in range(TILES):
                sp.dma_start(x[:, t, :], x_in[0, t * P:(t + 1) * P, :]).then_inc(x_landed[t], 16)
            for b, parts in enumerate(dense):
                slot = raw[:, b % RAW_SLOTS, :]
                if b >= RAW_SLOTS:
                    sp.wait_ge(lo_ready, b - RAW_SLOTS + 1)
                for h, src in parts:
                    dst = slot.rearrange("p (k n) -> p k n", n=src.shape[2]) if h is None else halves(slot)[h]
                    sp.dma_start(dst, src).then_inc(raw_landed[b % RAW_SLOTS], 16)
                if b == SPLIT_SLOTS - 1:
                    sp.dma_start(proj[:, :, 0:D], mem.rearrange("b (t p) d -> p (b t) d", p=P)).then_inc(mem_landed, 16)

            def turn_loads(i, expert):
                gate_up = moe_w_gate_up[0, bass.ds(expert, 1)].rearrange("e (k p) n -> p (e k) n", p=P)
                down = moe_w_down[0, bass.ds(expert, 1)].rearrange("e (k p) n -> p (e k) n", p=P)
                for b in range(TURN_BLOCKS):
                    n = BLK_MOE + b
                    slot = raw[:, n % RAW_SLOTS, :]
                    sp.wait_ge(lo_ready, i * TURN_BLOCKS + (n - RAW_SLOTS + 1))
                    if b < GU_BLOCKS:
                        j, half, k = b // 4, b // 2 % 2, b % 2 * 4
                        src = gate_up[:, k:k + 4, half * FE + j * BANK:half * FE + (j + 1) * BANK]
                    else:
                        k = (b - GU_BLOCKS) * 2
                        src = down[:, k:k + 2, :]
                    sp.dma_start(slot.rearrange("p (k n) -> p k n", n=src.shape[2]), src)\
                      .then_inc(raw_landed[n % RAW_SLOTS], 16)

            with sp.Fori(0, E) as i:
                turn_loads(i, i)
            sp.wait_ge(table_ready, 1)
            turns = sp.value_load(table_i[0:1, 0:1], min_val=E, max_val=E + MAX_EXTRA)
            with sp.If(turns > E):
                with sp.Fori(E, turns) as i:
                    expert = sp.value_load(table_i[0:1, bass.ds(i - (E - 1), 1)], min_val=0, max_val=E - 1)
                    turn_loads(i, expert)
            for b in range(SPLIT_SLOTS):
                n = BLK_MOE + b
                sp.wait_ge(lo_ready, turns * TURN_BLOCKS + (n - RAW_SLOTS + 1))
                sp.dma_start(raw[0:16, n % RAW_SLOTS, 0:P], x_in[0, 0:16, 0:P]).then_inc(raw_landed[n % RAW_SLOTS], 16)
            sp.wait_ge(spare_taken[(FILL_MOE - 1) % 2], turns * (TURN_FILLS // 2) + ((FILL_MOE - 1) // 2 + 1))
            sp.dma_start(out.rearrange("b (t p) d -> p (b t) d", p=P), x[:]).then_inc(stored, 16)
            sp.wait_ge(stored, 16)

        @block.tensor
        def _(pe):
            def spare(f):
                if f >= 2:
                    taken(pe, f - 2)
                return ps[:, SPARE + f % 2, :]

            def product(dst, hi, lo, slot, c0, cn, first, last):
                pe.matmul(dst, hi, w_hi[:, slot, c0:c0 + cn], start=first, stop=False)
                pe.matmul(dst, lo, w_hi[:, slot, c0:c0 + cn], start=False, stop=False)
                return pe.matmul(dst, hi, w_lo[:, slot, c0:c0 + cn], start=False, stop=last)

            def acc_free(name):
                p, uses = ACC[name]
                if uses:
                    pe.wait_ge(acc_taken[p], uses)
                return p

            def group_tile(b, b0, name, t):
                g, half = divmod(b - b0, 2)
                p = ACC[f"{name}{g}"][0]
                for kk in range(4):
                    k = 4 * half + kk
                    mm = product(ps[:, 2 * p + t, :], t_hi[:, k, t * P:(t + 1) * P], t_lo[:, k, t * P:(t + 1) * P],
                                 b % SPLIT_SLOTS, kk * BANK, BANK, k == 0, k == KD - 1)
                return mm

            def group_block(b, b0, name):
                g, half = divmod(b - b0, 2)
                if half == 0:
                    acc_free(f"{name}{g}")
                pe.wait_ge(lo_ready, b + 1)
                for t in range(TILES):
                    mm = group_tile(b, b0, name, t)
                mm.then_inc(w_used, 1)

            def wide_tile(b, b0, chunks, hi, lo, t):
                for kk in range(2):
                    k = 2 * (b - b0) + kk
                    for h in range(2):
                        mm = product(ps[:, 2 * t + h, :], hi[:, k, t * P:(t + 1) * P], lo[:, k, t * P:(t + 1) * P],
                                     b % SPLIT_SLOTS, kk * D + h * BANK, BANK, k == 0, k == chunks - 1)
                return mm

            def wide_block(b, b0, name, chunks, hi, lo):
                if b == b0:
                    for p in range(2):
                        acc_free(f"{name}{p}")
                pe.wait_ge(lo_ready, b + 1)
                for t in range(TILES):
                    mm = wide_tile(b, b0, chunks, hi, lo, t)
                    if t == 0 and 2 * (b - b0) + 2 == chunks:
                        mm.then_inc(tile0_summed, 1)
                mm.then_inc(w_used, 1)

            def fill_nat(name, f):
                bank = spare(FILL[(name, f)])
                t, c0 = f // 2, 4 * (f % 2)
                for j in range(4):
                    mm = pe.transpose(bank[:, j * P:(j + 1) * P], nat[:, t, (c0 + j) * P:(c0 + j + 1) * P], ident[:])
                mm.then_inc(fill_ready, 1)

            def first_block(name, tile_ready, b, tile_block):
                pe.wait_ge(lo_ready, b + 1)
                for t in range(TILES):
                    tile_ready(t)
                    fill_nat(name, 2 * t)
                    fill_nat(name, 2 * t + 1)
                    taken(pe, FILL[(name, 2 * t)])
                    mm = tile_block(t)
                mm.then_inc(w_used, 1)

            def all_taken(name):
                for f in (2, 3):
                    taken(pe, FILL[(name, f)])

            def piece(l, i):
                m, kk = divmod(i, 4)
                b = MIXED[l] + m
                name = f"mem{m // 2}" if l == 0 else f"in1.{IN_GROUPS - 1}"
                half = m % 2
                if kk == 0:
                    if half == 0:
                        acc_free(name)
                    pe.wait_ge(lo_ready, b + 1)
                if l == 0 and i == 0:
                    all_taken("memT")
                k = 4 * half + kk
                for t in range(TILES):
                    mm = product(ps[:, 2 + t, :], t_hi[:, k, t * P:(t + 1) * P], t_lo[:, k, t * P:(t + 1) * P],
                                 b % SPLIT_SLOTS, kk * BANK, BANK, k == 0, k == KD - 1)
                if kk == 3:
                    mm.then_inc(w_used, 1)

            def step_fill(l, name, c):
                if name == "memT":
                    if c == 0:
                        pe.wait_ge(nat_ready, 2 * TILES)
                    return fill_nat(name, c)
                bank = spare(FILL[(name, c)])
                if name == "km":
                    pe.wait_ge(heads_normed, [2, 3][c])
                elif c == 6:
                    pe.wait_ge(heads_normed, [1, 7][l])
                for j in range(4):
                    a, t = divmod(j, 2)
                    if name == "km":
                        src = km[:, c, t, a * P:(a + 1) * P]
                    else:
                        col = MIX * a + c * P if c < 6 else 3 * MIX + a * P
                        src = proj[:, t, col:col + P]
                    mm = pe.transpose(bank[:, j * P:(j + 1) * P], src, ident[:])
                mm.then_inc(fill_ready, 1)

            def attention(l):
                U, n_mix, base = UNITS[l], UNITS[l] - NMEM, l * UNITS[0]

                def scores(u):
                    last = base + (u - 1 if l and u <= n_mix else u - 2)
                    if last >= 0 and u:
                        pe.wait_ge(z_taken[last % 2], last // 2 + 1)
                    if u < n_mix:
                        for half in range(1 + l):
                            c, s = (u // 2, u % 2) if l == 0 else (u, half)
                            taken(pe, FILL[(f"qk{l}", c)])
                            q, k = qk_t[64 * s:64 * s + 64, c, 0:S], qk_t[64 * s:64 * s + 64, c, S:2 * S]
                            z = ps[:, u % 2 if l == 0 else half, :]
                            pe.matmul(z[:, 0:P], q[:, 0:P], k[:, 0:P], start=True, stop=True)
                            mm = pe.matmul(z[:, P:3 * P], q[:, P:2 * P], k, start=True, stop=True)
                    else:
                        c, s = divmod(u - n_mix, 2)
                        taken(pe, FILL[(f"qk{l}", 6)])
                        if u == n_mix:
                            taken(pe, FILL[("km", l)])
                        for t in range(TILES):
                            mm = pe.matmul(ps[:, u % 2, t * S:(t + 1) * S],
                                           qk_t[64 * s:64 * s + 64, 6, c * S + t * P:c * S + (t + 1) * P],
                                           km_t[64 * s:64 * s + 64, l, c, :], start=True, stop=True)
                    mm.then_inc(z_ready, 1)

                def turn(u):
                    bank = spare(FILL[(f"w{l}", u)])
                    if u < n_mix:
                        pe.wait_ge(att_ready, l * NSB + u + 1)
                    else:
                        pe.wait_ge(z_taken[u % 2], (base + u) // 2 + 1)
                    for j in range(3 if u < n_mix else 4):
                        mm = pe.transpose(bank[:, j * P:(j + 1) * P], att[:, u % 2, j * P:(j + 1) * P], ident[:])
                    mm.then_inc(fill_ready, 1)

                def values(u):
                    taken(pe, FILL[(f"w{l}", u)])
                    if base + u >= 2:
                        pe.wait_ge(head_taken, base + u - 1)
                    if l == 1 and u == 4:
                        group_taken(pe, f"in1.{IN_GROUPS - 1}")
                    n = HEAD * (l + 1) if u < n_mix else HEAD
                    for t in range(TILES):
                        if u < n_mix:
                            parts = [[(0, 0)], [(1, 0), (2, 1)]][t]
                            v = proj[:, :, QKW + n * u:QKW + n * (u + 1)]
                        else:
                            parts = [(2 * t, 0), (2 * t + 1, 1)]
                            v = vm[:, l, :, n * (u - n_mix):n * (u - n_mix + 1)]
                        for j, s in parts:
                            mm = pe.matmul(ps[:, OUT + u % 2, t * n:(t + 1) * n], att_t[:, u % 2, j * P:(j + 1) * P],
                                           v[:, s, :], start=(j == parts[0][0]), stop=(j == parts[-1][0]))
                    mm.then_inc(head_ready, 1)

                step_fill(l, f"qk{l}", 0)
                for s in range(U + LAG[l] + 1):
                    for name, c in STEP_FILLS[l].get(s, []):
                        step_fill(l, name, c)
                    if s < U:
                        scores(s)
                    pieces = PIECE_AT[l].get(s, [])
                    for i in pieces[:1]:
                        piece(l, i)
                    if 0 <= s - LAG[l] < U:
                        turn(s - LAG[l])
                    for i in pieces[1:]:
                        piece(l, i)
                    if s > LAG[l]:
                        values(s - LAG[l] - 1)

            pe.wait_ge(consts_ready, 1)
            for l in range(2):
                acc_free(f"in{l}.0")
                first_block(f"xT{l}", lambda t: pe.wait_ge(nat_ready, [0, 3][l] * TILES + t + 1), BLK_IN[l],
                            lambda t: group_tile(BLK_IN[l], BLK_IN[l], f"in{l}.", t))
                for f in (1, 3):
                    taken(pe, FILL[(f"xT{l}", f)])
                for b in range(BLK_IN[l] + 1, MIXED[l]):
                    group_block(b, BLK_IN[l], f"in{l}.")
                for g in (2, 3, 4)[:3 - l]:
                    group_taken(pe, f"in{l}.{g}")
                if l == 1:
                    pe.wait_ge(heads_normed, 6)
                attention(l)
                pe.wait_ge(head_taken, sum(UNITS[:l + 1]))
                if l == 1:
                    pe.wait_ge(heads_normed, 8)
                for p in range(2):
                    acc_free(f"out{l}.{p}")
                first_block(f"oT{l}", lambda t: None, BLK_OUT[l],
                            lambda t: wide_tile(BLK_OUT[l], BLK_OUT[l], KD, t_hi, t_lo, t))
                for b in range(BLK_OUT[l] + 1, BLK_OUT[l] + KD // 2):
                    if b == BLK_OUT[l] + 2:
                        for f in (1, 3):
                            taken(pe, FILL[(f"oT{l}", f)])
                    wide_block(b, BLK_OUT[l], f"out{l}.", KD, t_hi, t_lo)
                if l == 1:
                    for f in range(4):
                        pe.wait_ge(nat_ready, 4 * TILES + f // 2 + 1)
                        fill_nat("fT1", f)
                    all_taken("fT1")
                if l == 1:
                    break
                acc_free("ff0")
                first_block("fT0", lambda t: pe.wait_ge(nat_ready, 2 * TILES + t + 1), BLK_FF,
                            lambda t: group_tile(BLK_FF, BLK_FF, "ff", t))
                for f in (1, 3):
                    taken(pe, FILL[("fT0", f)])
                for b in range(BLK_FF + 1, BLK_IN[1]):
                    if b < BLK_FD:
                        group_block(b, BLK_FF, "ff")
                    else:
                        taken(pe, FILL[("hT", b - BLK_FD)])
                        wide_block(b, BLK_FD, "fd", FF // P, h_hi, h_lo)
                    j, odd = divmod(b - BLK_FF - 3, 2)
                    if odd == 0 and 0 <= j < FF_GROUPS:
                        bank = spare(FILL[("hT", j)])
                        p, uses = ACC[f"ff{j}"]
                        pe.wait_ge(acc_taken[p], uses + 1)
                        for i in range(4):
                            c, t = divmod(i, 2)
                            mm = pe.transpose(bank[:, i * P:(i + 1) * P],
                                              hid[:, j % 2, t * HALF + c * P:t * HALF + (c + 1) * P], ident[:])
                        mm.then_inc(fill_ready, 1)

            pe.wait_ge(wr_ready, 1)
            logits = ps[:, OUT, 0:S]
            for k in range(KD):
                pe.matmul(logits[0:2 * E], wr_split[:, k, :], t_hi[:, k, :], start=(k == 0), stop=False)
                mm = pe.matmul(logits[0:E], wr_split[:, k, 0:E], t_lo[:, k, :], start=False, stop=(k == KD - 1))
            mm.then_inc(logits_ready, 1)
            pe.wait_ge(logits_copied, 1)
            for t in range(TILES):
                mm = pe.transpose(ps[:, OUT, t * 2 * E:(t + 1) * 2 * E], logit_t[:, t * P:(t + 1) * P], ident[0:2 * E, 0:2 * E])
            mm.then_inc(logits_ready, 1)
            pe.wait_ge(mask_ready, 1)
            place = ps[:, OUT + 1, :]
            pe.matmul(place[:, 0:E], before[:], route[:, MASK, 0, :], start=True, stop=True)
            pe.matmul(place[:, E:2 * E], ones[:], route[:, MASK, 0, :], start=True, stop=False)
            pe.matmul(place[:, E:2 * E], before[:], route[:, MASK, 1, :], start=False, stop=True)
            pe.matmul(place[:, 2 * E:3 * E], ones[:], route[:, MASK, 0, :], start=True, stop=False)
            pe.matmul(place[:, 2 * E:3 * E], ones[:], route[:, MASK, 1, :], start=False, stop=True).then_inc(places_ready, 1)

            def gather(f, bank):
                part = (n_hi, n_lo)[f % 2]
                for j in range(4):
                    k = f // 2 * 4 + j
                    for t in range(TILES):
                        mm = pe.matmul(bank[:, j * P:(j + 1) * P], part[:, t, k * P:(k + 1) * P], pick[:, t, :],
                                       start=(t == 0), stop=(t == TILES - 1))
                mm.then_inc(fill_ready, 1)

            pe.wait_ge(n_ready, 1)
            pe.wait_ge(pick_ready, 1)
            for f in range(4):
                gather(f, spare(FILL[("gather", f)]))
            for f in (2, 3):
                taken(pe, FILL[("gather", f)])
            pe.wait_ge(table_ready, 1)
            turns = pe.value_load(table_i[0:1, 0:1], min_val=E, max_val=E + MAX_EXTRA)
            with pe.Fori(0, turns) as i:
                def turn_taken(f):
                    n = FILL_MOE + f
                    pe.wait_ge(spare_taken[n % 2], i * (TURN_FILLS // 2) + (n // 2 + 1))

                def turn_spare(f):
                    turn_taken(f - 2)
                    return ps[:, SPARE + (FILL_MOE + f) % 2, :]

                for b in range(TURN_BLOCKS):
                    n = BLK_MOE + b
                    if b < GU_BLOCKS and b % 4 == 0:
                        j = b // 4
                        pe.wait_ge(acc_taken[j % 2], i * ACC_TURN[j % 2] + (ACC_MOE[j % 2] + j // 2))
                    if b >= GU_BLOCKS:
                        turn_taken(1 + (b - GU_BLOCKS) // 2)
                    pe.wait_ge(lo_ready, i * TURN_BLOCKS + (n + 1))
                    if b < GU_BLOCKS:
                        j, half, k0 = b // 4, b // 2 % 2, b % 2 * 4
                        for kk in range(4):
                            k = k0 + kk
                            mm = product(ps[:, 2 * (j % 2) + half, :], g_hi[:, k, :], g_lo[:, k, :], n % SPLIT_SLOTS,
                                         kk * BANK, BANK, k == 0, k == KD - 1)
                    else:
                        for h in range(2):
                            for kk in range(2):
                                k = 2 * (b - GU_BLOCKS) + kk
                                mm = product(ps[:, OUT + h, :], e_hi[:, k, :], e_lo[:, k, :], n % SPLIT_SLOTS,
                                             kk * D + h * BANK, BANK, k == 0, k == FE // P - 1)
                            if b == TURN_BLOCKS - 1 and h == 0:
                                mm.then_inc(y0_summed, 1)
                    mm.then_inc(w_used, 1)
                    if b == 2:
                        bank = turn_spare(0)
                        for t in range(TILES):
                            pe.transpose(bank[:, t * P:(t + 1) * P], pick[:, t, :].bitcast(F32), ident[:])
                        for t in range(TILES):
                            mm = pe.matmul(bank[:, 2 * P:2 * P + 1], pick[:, t, :].bitcast(F32), turn_cw[:, t:t + 1],
                                           start=(t == 0), stop=(t == TILES - 1))
                        mm.then_inc(fill_ready, 1)
                    j, rest = divmod(b - 5, 4)
                    if rest == 0 and 0 <= j < FE_GROUPS:
                        bank = turn_spare(1 + j)
                        pe.wait_ge(acc_taken[j % 2], i * ACC_TURN[j % 2] + (ACC_MOE[j % 2] + j // 2 + 1))
                        for c in range(4):
                            mm = pe.transpose(bank[:, c * P:(c + 1) * P], hid[:, j % 2, c * P:(c + 1) * P], ident[:])
                        mm.then_inc(fill_ready, 1)
                    if b in GATHER_AT:
                        f = GATHER_AT.index(b)
                        if f == 0:
                            pe.wait_ge(pick_ready, i + 2)
                        gather(f, turn_spare(1 + FE_GROUPS + f))
                for f in range(4):
                    h, t = divmod(f, 2)
                    bank = turn_spare(5 + FE_GROUPS + f)
                    pe.wait_ge(y_lo_ready, i * 2 + (h + 1))
                    pe.matmul(bank, pick_t[:, t, :], y_hi[:, h * BANK:(h + 1) * BANK], start=True, stop=False)
                    pe.matmul(bank, pick_t[:, t, :], y_lo[:, h * BANK:(h + 1) * BANK], start=False, stop=True)\
                      .then_inc(fill_ready, 1)

        @block.scalar
        def _(act):
            def bcast(dst, src):
                act.dma_start(dst, src).then_inc(small_landed, 16)

            for l in range(2):
                bcast(head_gain[:, l, :], mem_k_norm[l].partition_broadcast(P))
                bcast(memq_gain[:, l, :], mem_q_norm[l].partition_broadcast(P))
            bcast(diff_gain[:, 0, :], diff_q_norm[0].partition_broadcast(P))
            bcast(diff_gain[:, 1, :], diff_k_norm[0].partition_broadcast(P))
            bcast(sub_gain[:], diff_subln[0].partition_broadcast(P))
            bcast(lam4[:], diff_lambda[0].partition_broadcast(P))
            with nc.allow_non_contiguous_dma(reason="one position a partition"):
                bcast(pos_i[:], positions.rearrange("b (t p) -> p (b t)", p=P))
            bcast(wr[:], w_router[0].rearrange("(k p) e -> p k e", p=P))
            link = chain(act, act_step)
            split_at = [0]

            def split(n, turn=None):
                wait_raw(act, n, turn)
                if turn is None:
                    if n >= SPLIT_SLOTS:
                        act.wait_ge(w_used, n - SPLIT_SLOTS + 1)
                else:
                    act.wait_ge(w_used, turn * TURN_BLOCKS + (n - SPLIT_SLOTS + 1))
                act.copy(w_hi[:, n % SPLIT_SLOTS, :], raw[:, n % RAW_SLOTS, :]).then_inc(hi_ready, 1)

            def split_to(n):
                while split_at[0] < n:
                    split(split_at[0])
                    split_at[0] += 1

            def squares(s, src, t):
                if s + t:
                    act.wait_ge(squares_ready, TILES * s + t)
                act.activation(sil[:].rearrange("p a n -> p (a n)"), src[:, t, :], ACT.Square,
                               accum_out=norm_r[:, s, 0, t:t + 1]).then_inc(squares_ready, 1)

            def take_hi(f, dst, want_used=None):
                act.wait_ge(fill_ready, f + 1)
                act.copy(dst, ps[:, SPARE + f % 2, 0:BANK].rearrange("p (a n) -> p a n", a=dst.shape[1])).then_inc(fill_hi, 1)

            def take_nat(name, f):
                t, c0 = f // 2, 4 * (f % 2)
                take_hi(FILL[(name, f)], t_hi[:, c0:c0 + 4, t * P:(t + 1) * P])

            def split_nat(name):
                for f in range(4):
                    take_nat(name, f)

            def norm_and_split(s, added, name, b):
                for t in range(TILES):
                    group_taken(act, f"{added}{t}")
                    squares(s, x, t)
                    if t == 1:
                        split_to(b + SPLIT_SLOTS)
                    for f in (2 * t, 2 * t + 1):
                        take_nat(name, f)

            act.wait_ge(pool_step, 1)
            act.activation(stat[:, 0, 0, :], minus_half[:, 0:4], ACT.Square)
            for t in range(TILES):
                act.wait_ge(x_landed[t], 16)
                squares(0, x, t)
            def unit(l, u):
                n_mix, base, p = UNITS[l] - NMEM, l * UNITS[0], u % 2
                a = att[:, p, :]
                if u >= 2:
                    act.wait_ge(fill_ready, FILL[(f"w{l}", u - 2)] + 1)
                if u < n_mix and l == 0:
                    act.wait_ge(z_ready, base + u + 1)
                    act.activation(a[:, 0:3 * P], ps[:, p, 0:3 * P], ACT.Sigmoid, scale=SCALE)
                    act.activation(a[:, 3 * P:6 * P], ps[:, p, 0:3 * P], ACT.Sigmoid, scale=-SCALE)\
                       .then_inc(z_taken[p], 1)
                elif u < n_mix:
                    act.wait_ge(max_ready, NMEM * l + u + 1)
                    for half in range(2):
                        for t, (c0, c1) in enumerate([(0, P), (P, 3 * P)]):
                            v = a[:, half * 3 * P + c0:half * 3 * P + c1]
                            ins = act.activation(v, v, ACT.Exp, bias=stat[:, u % 4, 0, 2 * half + t:2 * half + t + 1],
                                                 accum_out=stat[:, u % 4, 1, 2 * half + t:2 * half + t + 1])
                    ins.then_inc(exp_ready, 1)
                else:
                    act.wait_ge(max_ready, [u - n_mix, NMEM + u][l] + 1)
                    for t in range(TILES):
                        ins = act.activation(a[:, t * S:(t + 1) * S], ps[:, p, t * S:(t + 1) * S], ACT.Exp,
                                             scale=SCALE, bias=stat[:, u % 4, 0, t:t + 1], accum_out=stat[:, u % 4, 1, t:t + 1])
                    ins.then_inc(z_taken[p], 1)

            def take_weights(l, u):
                f = FILL[(f"w{l}", u)]
                act.wait_ge(fill_ready, f + 1)
                if l * UNITS[0] + u >= 2:
                    act.wait_ge(head_ready, l * UNITS[0] + u - 1)
                n = 3 * P if u < UNITS[l] - NMEM else 4 * P
                act.copy(att_t[:, u % 2, 0:n], ps[:, SPARE + f % 2, 0:n]).then_inc(spare_taken[f % 2], 1)

            def take_step_fills(l, s):
                for name, c in STEP_FILLS[l].get(s, []):
                    f = FILL[(name, c)]
                    if name == "memT":
                        take_nat(name, c)
                    elif name != "km" and c % 2 == 0:
                        act.wait_ge(fill_ready, f + 1)
                        act.copy(qk_t[:, c, :], ps[:, SPARE + f % 2, :]).then_inc(spare_taken[f % 2], 1)

            def take_sums(l, m):
                act.wait_ge(w_used, MIXED[l] + m + 1)
                if l == 0:
                    kv = ps[:, 2:4, :]
                    act.copy(km[:, m // 2, :, :], kv[:, :, 0:4 * HEAD]).then_inc(km_copied, 1)
                    act.copy(vm[:, m // 2, :, :], kv[:, :, 4 * HEAD:8 * HEAD]).then_inc(acc_taken[1], 1)
                else:
                    act.copy(proj[:, :, WIN - BANK:WIN], ps[:, 2:4, :]).then_inc(acc_taken[1], 1)

            for l in range(2):
                if l == 0:
                    split_to(1)
                    for f in range(4):
                        take_nat("xT0", f)
                        if f % 2:
                            split_to(1 + (f + 1) // 2)
                for b in range(BLK_IN[l], MIXED[l]):
                    split_to(b + 1 + AHEAD)
                    g, half = divmod(b - BLK_IN[l], 2)
                    if l == 0 and b == 0:
                        act.wait_ge(mem_landed, 16)
                        for t in range(TILES):
                            squares(1, proj[:, :, 0:D], t)
                        act.wait_ge(nat_ready, 2 * TILES)
                    if l == 0 and b == 4:
                        act.wait_ge(small_landed, 16 * 10)
                        act.copy(wr_split[:, :, 0:E], wr[:]).then_inc(wr_hi_ready, 1)
                        act.wait_ge(lam_sums, 1)
                        act.activation(lam[:, 2:4], lam[:, 0:2], ACT.Exp).then_inc(lam_exp, 1)
                    if l == 0 and b == 6:
                        act.wait_ge(ang_ready, 1)
                        act.activation(ang[:, 4, :, :], ang[:, 2, :, :], ACT.Sin)
                        act.activation(ang[:, 5, :, :], ang[:, 3, :, :], ACT.Sin).then_inc(rope_ready, 1)
                    if half and (l == 1 or g % 2 == 0):
                        p, _ = ACC[f"in{l}.{g}"]
                        act.wait_ge(w_used, b + 1)
                        act.copy(proj[:, :, g * BANK:(g + 1) * BANK], ps[:, 2 * p:2 * p + 2, :]).then_inc(acc_taken[p], 1)
                split_to(MIXED[l] + SPLIT_SLOTS)
                f = FILL[(f"qk{l}", 0)]
                act.wait_ge(fill_ready, f + 1)
                act.copy(qk_t[:, 0, :], ps[:, SPARE + f % 2, :]).then_inc(spare_taken[f % 2], 1)
                for s in range(UNITS[l] + LAG[l]):
                    take_step_fills(l, s)
                    if l == 1 and s >= LAG[1]:
                        take_weights(l, s - LAG[1])
                    if s < UNITS[l]:
                        unit(l, s)
                    if l == 0 and s >= LAG[0]:
                        take_weights(l, s - LAG[0])
                    for i in PIECE_AT[l].get(s, []):
                        if i % 8 == 7:
                            take_sums(l, i // 4)
                    if s in SPLIT_AT[l]:
                        split_to(split_at[0] + 1)
                split_nat(f"oT{l}")
                for b in range(BLK_OUT[l], BLK_OUT[l] + KD // 2):
                    split_to(b + 1 + AHEAD)
                norm_and_split([2, 4][l], f"out{l}.", f"fT{l}", BLK_OUT[l] + KD // 2)
                if l == 1:
                    break
                for b in range(BLK_FF, BLK_IN[1]):
                    split_to(b + 1 + AHEAD)
                    bb = b - BLK_FF
                    if bb % 2 and b < BLK_FD:
                        j = bb // 2
                        p, uses = ACC[f"ff{j}"]
                        act.wait_ge(w_used, b + 1)
                        if j >= 2:
                            act.wait_ge(acc_taken[p], uses)
                        act.activation(sil[:, j % 2, :].rearrange("p (t n) -> p t n", t=2),
                                       ps[:, 2 * p:2 * p + 2, 0:HALF], ACT.Silu).then_inc(sil_ready, 1)
                    j, odd = divmod(bb - 4, 2)
                    if odd == 0 and 0 <= j < FF_GROUPS:
                        take_hi(FILL[("hT", j)], h_hi[:, 2 * j:2 * j + 2, :])
                norm_and_split(3, "fd", "xT1", BLK_IN[1])

            act.copy(n_hi[:], nat[:]).then_inc(n_hi_ready, 1)
            act.activation(stat[:, 0, 0, :], minus_half[:, 0:4], ACT.Exp)
            act.wait_ge(gap_ready, 1)
            act.activation(gap[:, 1, :], gap[:, 0, :], ACT.Exp).then_inc(gap_exp, 1)

            def take_gather(f, k):
                act.copy(g_hi[:, k:k + 4, :], ps[:, SPARE + f % 2, :].rearrange("p (a n) -> p a n", a=4))\
                   .then_inc(spare_taken[f % 2], 1)

            for f in (0, 2):
                F = FILL[("gather", f)]
                act.wait_ge(fill_ready, F + 1)
                take_gather(F, 2 * f)
            act.wait_ge(table_ready, 1)
            turns = act.value_load(table_i[0:1, 0:1], min_val=E, max_val=E + MAX_EXTRA)
            with act.Fori(0, turns) as i:
                def filled(f):
                    act.wait_ge(fill_ready, i * TURN_FILLS + (FILL_MOE + f + 1))

                for b in range(TURN_BLOCKS):
                    if b % 4 == 3 and b < GU_BLOCKS:
                        j = b // 4
                        act.wait_ge(w_used, i * TURN_BLOCKS + (BLK_MOE + b + 1))
                        q = (j - 2) % 2
                        if j >= 2:
                            act.wait_ge(acc_taken[q], i * ACC_TURN[q] + (ACC_MOE[q] + j // 2))
                        act.activation(sil[:, j % 2, :], ps[:, 2 * (j % 2), :], ACT.Silu).then_inc(sil_ready, 1)
                    j, rest = divmod(b - 6, 4)
                    if rest == 0 and 0 <= j < FE_GROUPS:
                        filled(1 + j)
                        act.copy(e_hi[:, 4 * j:4 * j + 4, :],
                                 ps[:, SPARE + (FILL_MOE + 1 + j) % 2, :].rearrange("p (a n) -> p a n", a=4))\
                           .then_inc(fill_hi, 1)
                    if b - 1 in GATHER_AT[::2]:
                        f = GATHER_AT.index(b - 1)
                        filled(1 + FE_GROUPS + f)
                        take_gather(FILL_MOE + 1 + FE_GROUPS + f, 2 * f)
                    if b < TURN_BLOCKS - 1:
                        split(BLK_MOE + b + SPLIT_SLOTS, i)
                for h in range(2):
                    act.wait_ge(y_scaled, i * 2 + (h + 1))
                    act.copy(y_hi[:, h * BANK:(h + 1) * BANK], sil[:, h, :]).then_inc(y_hi_ready, 1)
                split(BLK_MOE + TURN_BLOCKS - 1 + SPLIT_SLOTS, i)
                act.wait_ge(y_lo_ready, i * 2 + 2)

        @block.vector
        def _(dve):
            link = chain(dve, dve_step)
            split_at = [0]

            def split(n, turn=None):
                if turn is None:
                    dve.wait_ge(hi_ready, n + 1)
                else:
                    dve.wait_ge(hi_ready, turn * TURN_BLOCKS + (n + 1))
                dve.tensor_tensor(w_lo[:, n % SPLIT_SLOTS, :], raw[:, n % RAW_SLOTS, :],
                                  w_hi[:, n % SPLIT_SLOTS, :].bitcast(F32), ALU.subtract).then_inc(lo_ready, 1)

            def split_to(n):
                while split_at[0] < n:
                    split(split_at[0])
                    split_at[0] += 1

            def norm(s, src, t):
                if t == 0:
                    dve.wait_ge(gain_landed, 16 * (s + 1))
                dve.wait_ge(rstd_ready, TILES * s + t + 1)
                dve.scalar_tensor_tensor(out=nat[:, t, :], in0=src[:, t, :], scalar=norm_r[:, s, 2, t:t + 1],
                                         in1=gain[:], op0=ALU.mult, op1=ALU.mult).then_inc(nat_ready, 1)

            his = [0]

            def take_lo(f, dst, hi):
                his[0] += 1
                dve.wait_ge(fill_hi, his[0])
                dve.tensor_tensor(dst, ps[:, SPARE + f % 2, 0:BANK].rearrange("p (a n) -> p a n", a=dst.shape[1]),
                                  hi.bitcast(F32), ALU.subtract).then_inc(spare_taken[f % 2], 1)

            def take_nat(name, f):
                t, c0 = f // 2, 4 * (f % 2)
                take_lo(FILL[(name, f)], t_lo[:, c0:c0 + 4, t * P:(t + 1) * P], t_hi[:, c0:c0 + 4, t * P:(t + 1) * P])

            def split_nat(name):
                for f in range(4):
                    take_nat(name, f)

            def norm_parts(name):
                heads = lambda v, w=HEAD: v.rearrange("p t (h w) -> p t h w", w=w)
                l = int(name[2]) if name[1:2] == "m" else 1
                src, g = {"km": (heads(km[:, l]), head_gain[:, l, :]),
                          "qm": (heads(proj[:, :, 3 * MIX:WIN]), memq_gain[:, l, :]),
                          "q": (heads(proj[:, :, 0:MIX]), diff_gain[:, 0, :]),
                          "k": (heads(proj[:, :, MIX:QKW]), diff_gain[:, 1, :]),
                          "su": (heads(nat[:, :, 0:MIX], 2 * HEAD), sub_gain[:])}[name[:2]]
                return NORMS[name], src, g

            def head_sums(name):
                m, src, _ = norm_parts(name)
                if m:
                    dve.wait_ge(sums_ready, m)
                _, A, N, W = src.shape
                sums = head_r[:, m, 0, 0:A * N].rearrange("p (a n) -> p a n", a=A)
                for a in range(A):
                    sq = hid[:].rearrange("p a n -> p (a n)")[:, 0:N * W].rearrange("p (n w) -> p n w", w=W)
                    link(dve.tensor_tensor(sq, src[:, a], src[:, a], ALU.mult))
                    ins = dve.tensor_reduce(sums[:, a, :], sq, AX.X, ALU.add)
                    if a < A - 1:
                        link(ins)
                ins.then_inc(sums_ready, 1)

            def head_apply(name):
                m, src, g = norm_parts(name)
                _, A, N, W = src.shape
                rstd = head_r[:, m, 1, 0:A * N].rearrange("p (a n) -> p a n", a=A)
                dve.wait_ge(head_rstd_ready, m + 1)
                for a in range(A):
                    ins = dve.tensor_tensor(src[:, a], src[:, a], rstd[:, a].unsqueeze(2).to_broadcast([P, N, W]), ALU.mult)
                    if a == A - 1:
                        link(ins)
                for a in range(A):
                    ins = dve.tensor_tensor(src[:, a], src[:, a], g.unsqueeze(1).to_broadcast([P, N, W]), ALU.mult)
                ins.then_inc(heads_normed, 1)

            def norm_and_split(s, added, order, name, b):
                for t in range(TILES):
                    if t == 0:
                        dve.wait_ge(tile0_summed, order + 1)
                    else:
                        dve.wait_ge(w_used, b)
                    dve.tensor_tensor(x[:, t, :], x[:, t, :], ps[:, 2 * t:2 * t + 2, :].rearrange("p a n -> p (a n)"),
                                      ALU.add).then_inc(acc_taken[t], 1)
                    if t == 1:
                        for f in (0, 1):
                            take_nat(name, f)
                    group_taken(dve, f"{added}{t}")
                    norm(s, x, t)
                for f in (2, 3):
                    split_to(b + f)
                    take_nat(name, f)
                split_to(b + SPLIT_SLOTS)

            dve.memset(keep[:], 1.0)
            link(dve.memset(turn_slot[:], -1.0))
            link(dve.memset(turn_w[:], 0.0))
            for t in range(TILES):
                norm(0, x, t)

            def lambda_sums():
                dve.wait_ge(small_landed, 16 * 10)
                link(dve.tensor_tensor(hid[:, 0, 0:HEAD], lam4[:, 0, :], lam4[:, 1, :], ALU.mult))
                link(dve.tensor_tensor(hid[:, 0, HEAD:2 * HEAD], lam4[:, 2, :], lam4[:, 3, :], ALU.mult))
                dve.tensor_reduce(lam[:, 0:2], hid[:, 0, 0:2 * HEAD].rearrange("p (a n) -> p a n", a=2), AX.X, ALU.add)\
                   .then_inc(lam_sums, 1)
                dve.wait_ge(lam_sums, 1)

            def lambda_end():
                dve.wait_ge(wr_hi_ready, 1)
                dve.tensor_tensor(wr_split[:, :, E:2 * E], wr[:], wr_split[:, :, 0:E].bitcast(F32), ALU.subtract).then_inc(wr_ready, 1)
                dve.wait_ge(lam_exp, 1)
                link(dve.tensor_tensor(lam[:, 4:5], lam[:, 3:4], lam[:, 2:3], ALU.subtract))
                link(dve.tensor_scalar(lam[:, 4:5], lam[:, 4:5], -LAM_INIT, None, ALU.add))
                link(dve.tensor_scalar(sub_gain[:], sub_gain[:], 1.0 - LAM_INIT, None, ALU.mult))

            def turn_by_position():
                dve.wait_ge(heads_normed, 5)
                dve.wait_ge(rope_ready, 1)
                half_rope = ROPE // 2
                n = 2 * 2 * NDIFF
                for t in range(TILES):
                    heads = proj[:, t, 0:QKW].rearrange("p (h w) -> p h w", w=HEAD)
                    t1, t2 = heads[:, :, 0:half_rope], heads[:, :, half_rope:ROPE]
                    sin, cos = (ang[:, 4 + a, t, :].unsqueeze(1).to_broadcast([P, n, half_rope]) for a in range(2))
                    tmp = [hid[:, a // 2, a % 2 * HALF:a % 2 * HALF + n * half_rope].rearrange("p (h w) -> p h w", w=half_rope)
                           for a in range(4)]
                    dve.tensor_tensor(tmp[0], t1, cos, ALU.mult)
                    dve.tensor_tensor(tmp[1], t2, sin, ALU.mult)
                    dve.tensor_tensor(tmp[2], t2, cos, ALU.mult)
                    link(dve.tensor_tensor(tmp[3], t1, sin, ALU.mult))
                    dve.tensor_tensor(t1, tmp[0], tmp[1], ALU.subtract)
                    ins = dve.tensor_tensor(t2, tmp[2], tmp[3], ALU.add)
                    if t < TILES - 1:
                        link(ins)
                ins.then_inc(heads_normed, 1)

            def unit(l, u):
                n_mix, base, p = UNITS[l] - NMEM, l * UNITS[0], u % 2
                a = att[:, p, :]
                tiles = [(0, P), (P, 3 * P)]
                if u < n_mix and l == 0:
                    dve.wait_ge(masked_ready, u + 1)
                    for t, (c0, c1) in enumerate(tiles):
                        kp = a[:, 3 * P + c0:3 * P + c1][:, ::-1]
                        ins = dve.tensor_tensor_scan(keep[:, p, c0 + 2 * t:c1 + 2 * t][:, ::-1], kp, kp, 1.0, ALU.mult, ALU.bypass)
                    link(ins)
                    for t, (c0, c1) in enumerate(tiles):
                        ins = dve.tensor_tensor(a[:, c0:c1], a[:, c0:c1], keep[:, p, c0 + 2 * t + 1:c1 + 2 * t + 1], ALU.mult)
                    ins.then_inc(att_ready, 1)
                elif u < n_mix:
                    if u >= 2:
                        dve.wait_ge(fill_ready, FILL[(f"w{l}", u - 2)] + 1)
                    dve.wait_ge(z_ready, base + u + 1)
                    for half in range(2):
                        ins = dve.scalar_tensor_tensor(out=a[:, half * 3 * P:(half + 1) * 3 * P], in0=ps[:, half, 0:3 * P],
                                                       scalar=SCALE, in1=causal[:], op0=ALU.mult, op1=ALU.add)
                    ins.then_inc(z_taken[p], 1)
                    dve.wait_ge(z_taken[p], (base + u) // 2 + 1)
                    for half in range(2):
                        for t, (c0, c1) in enumerate(tiles):
                            ins = dve.tensor_reduce(stat[:, u % 4, 0, 2 * half + t:2 * half + t + 1],
                                                    a[:, half * 3 * P + c0:half * 3 * P + c1], AX.X, ALU.max, negate=True)
                    ins.then_inc(max_ready, 1)
                else:
                    dve.wait_ge(z_ready, base + u + 1)
                    link(dve.tensor_reduce(stat[:, u % 4, 0, 0:TILES], ps[:, p, :].rearrange("p (t n) -> p t n", t=TILES),
                                           AX.X, ALU.max))
                    dve.tensor_scalar(stat[:, u % 4, 0, 0:TILES], stat[:, u % 4, 0, 0:TILES], -SCALE, None, ALU.mult).then_inc(max_ready, 1)

            def differ(u):
                a, tiles = att[:, u % 2, :], [(0, P), (P, 3 * P)]
                dve.wait_ge(exp_ready, u + 1)
                link(dve.reciprocal(stat[:, u % 4, 2, :], stat[:, u % 4, 1, :]))
                link(dve.tensor_scalar(stat[:, u % 4, 2, 2:4], stat[:, u % 4, 2, 2:4], lam[:, 4:5], None, ALU.mult))
                for t, (c0, c1) in enumerate(tiles):
                    ins = dve.tensor_scalar(a[:, 3 * P + c0:3 * P + c1], a[:, 3 * P + c0:3 * P + c1],
                                            stat[:, u % 4, 2, 2 + t:3 + t], None, ALU.mult)
                link(ins)
                for t, (c0, c1) in enumerate(tiles):
                    ins = dve.scalar_tensor_tensor(out=a[:, c0:c1], in0=a[:, c0:c1], scalar=stat[:, u % 4, 2, t:t + 1],
                                                   in1=a[:, 3 * P + c0:3 * P + c1], op0=ALU.mult, op1=ALU.add)
                ins.then_inc(att_ready, 1)

            def take_head(l, u):
                n_mix = UNITS[l] - NMEM
                o = ps[:, OUT + u % 2, :]
                if u >= n_mix:
                    c0 = MIX + HEAD * (u - n_mix)
                    link(dve.reciprocal(stat[:, u % 4, 2, 0:TILES], stat[:, u % 4, 1, 0:TILES]))
                    dve.wait_ge(head_ready, l * UNITS[0] + u + 1)
                    for t in range(TILES):
                        ins = dve.tensor_scalar(nat[:, t, c0:c0 + HEAD], o[:, t * HEAD:(t + 1) * HEAD],
                                                stat[:, u % 4, 2, t:t + 1], None, ALU.mult)
                else:
                    n = HEAD * (l + 1)
                    dve.wait_ge(head_ready, l * UNITS[0] + u + 1)
                    ins = dve.tensor_copy(nat[:, :, n * u:n * (u + 1)], o[:, 0:2 * n].rearrange("p (t n) -> p t n", t=TILES))
                ins.then_inc(head_taken, 1)

            def take_step_fills(l, s):
                for name, c in STEP_FILLS[l].get(s, []):
                    f = FILL[(name, c)]
                    if name == "memT":
                        take_nat(name, c)
                    elif name == "km" or c % 2:
                        dst = km_t[:, c].rearrange("p c s -> p (c s)") if name == "km" else qk_t[:, c, :]
                        dve.wait_ge(fill_ready, f + 1)
                        dve.tensor_copy(dst, ps[:, SPARE + f % 2, :]).then_inc(spare_taken[f % 2], 1)

            for l in range(2):
                if l == 0:
                    split_to(1)
                    for f in range(4):
                        take_nat("xT0", f)
                        if f % 2:
                            split_to(1 + (f + 1) // 2)
                for b in range(BLK_IN[l], MIXED[l]):
                    split_to(min(b + 1 + AHEAD, MIXED[l]) if l else b + 1 + AHEAD)
                    g, half = divmod(b - BLK_IN[l], 2)
                    if l == 0 and half and g % 2 == 1:
                        p, uses = ACC[f"in{l}.{g}"]
                        dve.wait_ge(w_used, b + 1)
                        dve.tensor_copy(proj[:, :, g * BANK:(g + 1) * BANK], ps[:, 2 * p:2 * p + 2, :]).then_inc(acc_taken[p], 1)
                    if l == 0 and b == 0:
                        dve.wait_ge(fill_ready, FILL[("xT0", 3)] + 1)
                        dve.wait_ge(mem_landed, 16)
                        for t in range(TILES):
                            norm(1, proj[:, :, 0:D], t)
                    if l == 0 and b == 2:
                        lambda_sums()
                    if l == 0 and b == 5:
                        lambda_end()
                    if l == 1 and b == BLK_IN[1]:
                        dve.wait_ge(km_copied, 2)
                        head_sums("km1")
                    if l == 1 and b == BLK_IN[1] + 1:
                        head_apply("km1")
                    if l == 1 and b == BLK_IN[1] + 3:
                        for g in range(2):
                            group_taken(dve, f"in1.{g}")
                        head_sums("q")
                    if l == 1 and b == BLK_IN[1] + 5:
                        head_apply("q")
                        group_taken(dve, "in1.2")
                        head_sums("k")
                    if l == 1 and b == BLK_IN[1] + 7:
                        head_apply("k")
                        turn_by_position()
                split_to(MIXED[l] + SPLIT_SLOTS)
                for s in range(UNITS[l] + LAG[l] + 1):
                    take_step_fills(l, s)
                    if s < UNITS[l]:
                        unit(l, s)
                    if l == 1 and 1 <= s <= NDIFF:
                        differ(s - 1)
                    if s > LAG[l]:
                        take_head(l, s - LAG[l] - 1)
                    if s - 1 in SPLIT_AT[l]:
                        split_to(split_at[0] + 1)
                    if (l, s) == (0, 4) or (l, s) == (1, 4):
                        group_taken(dve, f"in{l}.{IN_GROUPS - 1}")
                        head_sums(f"qm{l}")
                    if (l, s) == (0, 5) or (l, s) == (1, 5):
                        head_apply(f"qm{l}")
                    if (l, s) == (0, 8):
                        dve.wait_ge(km_copied, 1)
                        head_sums("km0")
                    if (l, s) == (0, 9):
                        head_apply("km0")
                    if (l, s) == (1, NDIFF + LAG[1]):
                        dve.wait_ge(head_taken, UNITS[0] + NDIFF)
                        head_sums("sub")
                    if (l, s) == (1, NDIFF + LAG[1] + 2):
                        head_apply("sub")
                split_nat(f"oT{l}")
                for b in range(BLK_OUT[l], BLK_OUT[l] + KD // 2):
                    split_to(min(b + 1 + AHEAD, BLK_OUT[l] + KD // 2 + 1))
                norm_and_split([2, 4][l], f"out{l}.", 2 * l, f"fT{l}", BLK_OUT[l] + KD // 2)
                if l == 1:
                    break
                for b in range(BLK_FF, BLK_IN[1]):
                    split_to(min(b + 1 + AHEAD, BLK_IN[1] + 1))
                    bb = b - BLK_FF
                    if bb % 2 and b < BLK_FD:
                        j = bb // 2
                        p, uses = ACC[f"ff{j}"]
                        dve.wait_ge(sil_ready, j + 1)
                        if j >= 2:
                            dve.wait_ge(fill_ready, FILL[("hT", j - 2)] + 1)
                        dve.tensor_tensor(hid[:, j % 2, :].rearrange("p (t n) -> p t n", t=2),
                                          ps[:, 2 * p:2 * p + 2, HALF:BANK], sil[:, j % 2, :].rearrange("p (t n) -> p t n", t=2),
                                          ALU.mult).then_inc(acc_taken[p], 1)
                    j, odd = divmod(bb - 4, 2)
                    if odd == 0 and 0 <= j < FF_GROUPS:
                        take_lo(FILL[("hT", j)], h_lo[:, 2 * j:2 * j + 2, :], h_hi[:, 2 * j:2 * j + 2, :])
                norm_and_split(3, "fd", 1, "xT1", BLK_IN[1])

            R = lambda a: route[:, a]
            wide = lambda v: v.unsqueeze(2).to_broadcast([P, TILES, E])
            down8 = down_row[:].unsqueeze(1).to_broadcast([P, TILES, E])
            dve.wait_ge(n_hi_ready, 1)
            dve.tensor_tensor(n_lo[:], nat[:], n_hi[:].bitcast(F32), ALU.subtract).then_inc(n_ready, 1)
            dve.wait_ge(logits_ready, 1)
            dve.tensor_copy(logit_t[:], ps[0:2 * E, OUT, 0:S]).then_inc(logits_copied, 1)
            dve.wait_ge(logits_ready, 2)
            parts = ps[:, OUT, 0:2 * TILES * E].rearrange("p (t h e) -> p t h e", h=2, e=E)
            link(dve.tensor_copy(R(TMP), parts[:, :, 0, :]))
            link(dve.tensor_tensor(R(LOGIT), R(TMP), parts[:, :, 1, :], ALU.add))
            for a in range(2):
                src, onehot = (LOGIT, FIRST) if a == 0 else (REST, SECOND)
                link(dve.tensor_reduce(gap[:, 2 + a, :], R(src), AX.X, ALU.max))
                link(dve.tensor_tensor(R(TMP), R(src), wide(gap[:, 2 + a, :]), ALU.is_equal))
                link(dve.tensor_tensor(R(TMP), R(TMP), down8, ALU.mult))
                link(dve.tensor_reduce(gap[:, 4, :], R(TMP), AX.X, ALU.min))
                link(dve.tensor_tensor(R(onehot), down8, wide(gap[:, 4, :]), ALU.is_equal))
                if a == 0:
                    link(dve.scalar_tensor_tensor(out=R(REST), in0=R(FIRST), scalar=NEG_BIG, in1=R(LOGIT), op0=ALU.mult, op1=ALU.add))
            dve.tensor_tensor(gap[:, 0, :], gap[:, 3, :], gap[:, 2, :], ALU.subtract).then_inc(gap_ready, 1)
            dve.tensor_tensor(R(MASK), R(FIRST), R(SECOND), ALU.add).then_inc(mask_ready, 1)
            dve.wait_ge(gap_exp, 1)
            link(dve.tensor_scalar(gap[:, 5, :], gap[:, 1, :], 1.0, None, ALU.add))
            link(dve.reciprocal(gap[:, 6, :], gap[:, 5, :]))
            link(dve.tensor_tensor(gap[:, 7, :], gap[:, 1, :], gap[:, 6, :], ALU.mult))
            link(dve.tensor_tensor(R(FIRST), R(FIRST), wide(gap[:, 6, :]), ALU.mult))
            link(dve.tensor_tensor(R(SECOND), R(SECOND), wide(gap[:, 7, :]), ALU.mult))
            link(dve.tensor_tensor(turn_w[:, :, 0:E], R(FIRST), R(SECOND), ALU.add))
            dve.wait_ge(places_ready, 1)
            place = ps[:, OUT + 1, :]
            link(dve.scalar_tensor_tensor(out=R(PLACE1), in0=place[:, 0:2 * E].rearrange("p (t e) -> p t e", e=E), scalar=1.0,
                                          in1=R(MASK), op0=ALU.add, op1=ALU.mult))
            link(dve.tensor_scalar(turn_slot[:, :, 0:E], R(PLACE1), -1.0, None, ALU.add))

            def make_pick(col, waited=True):
                dve.tensor_copy(turn_cw[:].unsqueeze(2), turn_w[:, :, col])
                for t in range(TILES):
                    ins = dve.tensor_scalar(pick[:, t, :], slot_row[:], turn_slot[:, t, col], None, ALU.is_equal)
                ins.then_inc(pick_ready, 1)

            make_pick(slice(0, 1))
            link(dve.tensor_scalar(over[:, 0, :], place[:, 2 * E:3 * E], float(P), None, ALU.is_gt))
            link(dve.tensor_tensor_scan(over[:, 1, :], over[:, 0, :], over[:, 0, :], 0.0, ALU.add, ALU.bypass))
            link(dve.tensor_tensor(over[:, 2, :], over[:, 1, :], over[:, 0, :], ALU.subtract))
            link(dve.tensor_scalar(table[:, 0:1], over[:, 1, E - 1:E], float(E), None, ALU.add))
            small = hid[:].rearrange("p a n -> p (a n)")[:, 0:6 * MAX_EXTRA * E].rearrange("p (a r e) -> p a r e", a=6, e=E)
            sel = small[:, 0]
            per_r = lambda v: v.unsqueeze(1).to_broadcast([P, MAX_EXTRA, E])
            link(dve.tensor_tensor(sel, per_r(over[:, 2, :]), slot_row[:, 0:MAX_EXTRA].unsqueeze(2).to_broadcast([P, MAX_EXTRA, E]),
                                   ALU.is_equal))
            link(dve.tensor_tensor(sel, sel, per_r(over[:, 0, :]), ALU.mult))
            dve.tensor_tensor(small[:, 1], sel, per_r(slot_row[:, 0:E]), ALU.mult)
            for t in range(TILES):
                dve.tensor_tensor(small[:, 2 + t], sel, per_r(route[:, PLACE1, t, :]), ALU.mult)
            for t in range(TILES):
                ins = dve.tensor_tensor(small[:, 4 + t], sel, per_r(turn_w[:, t, 0:E]), ALU.mult)
            link(ins)
            dve.tensor_reduce(table[:, 1:1 + MAX_EXTRA], small[:, 1], AX.X, ALU.add)
            for t in range(TILES):
                dve.tensor_reduce(turn_slot[:, t, E:E + MAX_EXTRA], small[:, 2 + t], AX.X, ALU.add)
            for t in range(TILES):
                ins = dve.tensor_reduce(turn_w[:, t, E:E + MAX_EXTRA], small[:, 4 + t], AX.X, ALU.add)
            link(ins)
            link(dve.tensor_scalar(turn_slot[:, :, E:E + MAX_EXTRA], turn_slot[:, :, E:E + MAX_EXTRA], -1.0 - P, None, ALU.add))
            dve.tensor_copy(table_i[:], table[:]).then_inc(table_ready, 1)

            def take_gather(f, k):
                dve.tensor_copy(g_lo[:, k:k + 4, :], ps[:, SPARE + f % 2, :].rearrange("p (a n) -> p a n", a=4))\
                   .then_inc(spare_taken[f % 2], 1)

            for f in (1, 3):
                F = FILL[("gather", f)]
                dve.wait_ge(fill_ready, F + 1)
                take_gather(F, 2 * (f - 1))
            dve.wait_ge(table_ready, 1)
            turns = dve.value_load(table_i[0:1, 0:1], min_val=E, max_val=E + MAX_EXTRA)
            HI_MOE, SIL_MOE = his[0], FF_GROUPS
            with dve.Fori(0, turns) as i:
                def filled(f):
                    dve.wait_ge(fill_ready, i * TURN_FILLS + (FILL_MOE + f + 1))
                    return FILL_MOE + f

                for b in range(TURN_BLOCKS):
                    if b % 4 == 3 and b < GU_BLOCKS:
                        j = b // 4
                        dve.wait_ge(sil_ready, i * FE_GROUPS + (SIL_MOE + j + 1))
                        if j >= 2:
                            filled(1 + j - 2)
                        dve.tensor_tensor(hid[:, j % 2, :], ps[:, 2 * (j % 2) + 1, :], sil[:, j % 2, :], ALU.mult)\
                           .then_inc(acc_taken[j % 2], 1)
                    if b == 3:
                        f = filled(0)
                        dve.tensor_copy(pick_t[:].rearrange("p t n -> p (t n)"), ps[:, SPARE + f % 2, 0:2 * P])
                        dve.tensor_copy(slot_w[:], ps[:, SPARE + f % 2, 2 * P:2 * P + 1]).then_inc(spare_taken[f % 2], 1)
                    if b == 15:
                        make_pick(bass.ds(i + 1, 1))
                    j, rest = divmod(b - 6, 4)
                    if rest == 0 and 0 <= j < FE_GROUPS:
                        n = FILL_MOE + 1 + j
                        dve.wait_ge(fill_hi, i * FE_GROUPS + (HI_MOE + j + 1))
                        dve.tensor_tensor(e_lo[:, 4 * j:4 * j + 4, :], ps[:, SPARE + n % 2, :].rearrange("p (a n) -> p a n", a=4),
                                          e_hi[:, 4 * j:4 * j + 4, :].bitcast(F32), ALU.subtract).then_inc(spare_taken[n % 2], 1)
                    if b - 1 in GATHER_AT[1::2]:
                        f = GATHER_AT.index(b - 1)
                        take_gather(filled(1 + FE_GROUPS + f), 2 * (f - 1))
                    if b < TURN_BLOCKS - 1:
                        split(BLK_MOE + b + SPLIT_SLOTS, i)
                for h in range(2):
                    if h == 0:
                        dve.wait_ge(y0_summed, i + 1)
                    else:
                        dve.wait_ge(w_used, i * TURN_BLOCKS + (BLK_MOE + TURN_BLOCKS))
                    dve.tensor_scalar(sil[:, h, :], ps[:, OUT + h, :], slot_w[:], None, ALU.mult).then_inc(y_scaled, 1)
                for h in range(2):
                    dve.wait_ge(y_hi_ready, i * 2 + (h + 1))
                    dve.tensor_tensor(y_lo[:, h * BANK:(h + 1) * BANK], sil[:, h, :], y_hi[:, h * BANK:(h + 1) * BANK].bitcast(F32),
                                      ALU.subtract).then_inc(y_lo_ready, 1)
                for f in range(4):
                    h, t = divmod(f, 2)
                    if f == 2:
                        split(BLK_MOE + TURN_BLOCKS - 1 + SPLIT_SLOTS, i)
                    n = filled(5 + FE_GROUPS + f)
                    xs = x[:, t, h * BANK:(h + 1) * BANK]
                    dve.tensor_tensor(xs, xs, ps[:, SPARE + n % 2, :], ALU.add).then_inc(spare_taken[n % 2], 1)

        @block.gpsimd
        def _(pool):
            link = chain(pool, pool_step)
            gains = [attn_norm[0], mem_norm, ffn_norm[0], attn_norm[1], ffn_norm[1]]

            def load_gain(s):
                if s:
                    pool.wait_ge(nat_ready, TILES * s)
                pool.dma_start(gain[:], gains[s].partition_broadcast(P)).then_inc(gain_landed, 16)

            def rsqrt(dst, src, width, n):
                link(pool.tensor_scalar(dst, src, 1.0 / width, EPS, ALU.mult, ALU.add))
                return pool.tensor_tensor(dst, dst, minus_half[:, 0:n], ALU.pow)

            def norm_rstd(s):
                if s:
                    load_gain(s)
                for t in range(TILES):
                    pool.wait_ge(squares_ready, TILES * s + t + 1)
                    rsqrt(norm_r[:, s, 2, t:t + 1], norm_r[:, s, 0, t:t + 1], D, 1).then_inc(rstd_ready, 1)

            def head_rstd(name):
                m = NORMS[name]
                pool.wait_ge(sums_ready, m + 1)
                n = NORM_N[m]
                rsqrt(head_r[:, m, 1, 0:n], head_r[:, m, 0, 0:n], NORM_W[m], n).then_inc(head_rstd_ready, 1)

            load_gain(0)
            link(pool.memset(minus_half[:], -0.5))
            link(pool.memset(ident[:], 0.0))
            link(pool.affine_select(out=ident[:], in_=ident[:], compare_op=ALU.not_equal, fill=1.0, base=0,
                                    pattern=[[-1, P]], channel_multiplier=1))
            link(pool.memset(ones[:], 1.0))
            link(pool.affine_select(out=before[:], in_=ones[:], compare_op=ALU.is_ge, fill=0.0, base=-1,
                                    pattern=[[1, P]], channel_multiplier=-1))
            link(pool.memset(causal[:], 0.0))
            for c in (0, 2 * P):
                link(pool.affine_select(out=causal[:, c:c + P], in_=causal[:, c:c + P], compare_op=ALU.is_ge, fill=NEG_BIG,
                                        base=0, pattern=[[-1, P]], channel_multiplier=1))
            link(pool.iota(slot_row[:], pattern=[[1, P]], base=0, channel_multiplier=0, allow_small_or_imprecise_dtypes=True))
            link(pool.iota(down_row[:], pattern=[[1, E]], base=-E, channel_multiplier=0, allow_small_or_imprecise_dtypes=True))
            for j in range(ROPE // 2):
                link(pool.memset(inv_freq[:, :, j], float(np.float32(ROPE_THETA ** (-2 * j / ROPE)))))
            pool.memset(table[:], 0.0).then_inc(consts_ready, 1)
            norm_rstd(0)
            norm_rstd(1)
            pool.wait_ge(small_landed, 16 * 10)
            A = lambda a: ang[:, a]
            two_pi = 2 * math.pi
            parts = [6.28125, float(np.float32(two_pi - 6.28125).astype(np.float16))]
            parts.append(two_pi - sum(parts))
            link(pool.tensor_copy(A(1)[:, :, 0], pos_i[:]))
            link(pool.tensor_tensor(A(0), inv_freq[:], A(1)[:, :, 0:1].to_broadcast([P, TILES, ROPE // 2]), ALU.mult))
            link(pool.tensor_scalar(A(1), A(0), 1.0 / two_pi, None, ALU.mult))
            link(pool.tensor_copy(ang_i[:], A(1)))
            link(pool.tensor_copy(A(1), ang_i[:]))
            for part in parts:
                link(pool.tensor_scalar(A(2), A(1), -part, None, ALU.mult))
                link(pool.tensor_tensor(A(0), A(0), A(2), ALU.add))

            def into_range(v):
                for op, bound, back in ((ALU.is_lt, -math.pi, two_pi), (ALU.is_gt, math.pi, -two_pi)):
                    link(pool.tensor_scalar(A(4), v, bound, back, op, ALU.mult))
                    link(pool.tensor_tensor(v, v, A(4), ALU.add))
                return pool.tensor_scalar(v, v, 3.1415925, -3.1415925, ALU.min, ALU.max)

            link(pool.tensor_copy(A(2), A(0)))
            link(into_range(A(2)))
            link(pool.tensor_scalar(A(3), A(2), math.pi / 2, None, ALU.add))
            into_range(A(3)).then_inc(ang_ready, 1)
            for u in range(NSB):
                p = u % 2
                pool.wait_ge(z_taken[p], u // 2 + 1)
                for c0, fill in ((0, 0.0), (3 * P, 1.0)):
                    v = att[:, p, c0:c0 + 4 * P].rearrange("p (a n) -> p a n", a=2)[:, :, 0:P]
                    ins = pool.affine_select(out=v, in_=v, compare_op=ALU.is_ge, fill=fill, base=-1,
                                             pattern=[[0, 2], [-1, P]], channel_multiplier=1)
                ins.then_inc(masked_ready, 1)
                if u in (4, 8):
                    head_rstd("qm0" if u == 4 else "km0")
            norm_rstd(2)
            norm_rstd(3)
            for name in ("km1", "q", "k", "qm1", "sub"):
                head_rstd(name)
            norm_rstd(4)


_INS = ["x", "mem", "positions", "attn_norm", "w_in", "w_out", "mem_norm", "w_mem_kv", "mem_q_norm", "mem_k_norm",
        "diff_q_norm", "diff_k_norm", "diff_lambda", "diff_subln", "ffn_norm", "dense_w_gate_up", "dense_w_down",
        "w_router", "moe_w_gate_up", "moe_w_down"]


def kernel(**inputs):
    import concourse.bacc as _bacc
    from concourse.bass_utils import run_bass_kernel_spmd as _run

    nc = _bacc.Bacc("TRN2", target_bir_lowering=False, num_devices=1, dynamic_dma_scratch_size=4096)
    arrays, args = {}, []
    for name in _INS:
        a = np.ascontiguousarray(inputs[name])
        arrays[f"in_{name}"] = a
        args.append(nc.dram_tensor(f"in_{name}", a.shape, mybir.dt.from_np(a.dtype), kind="ExternalInput").ap())
    out = nc.dram_tensor("out_x", inputs["x"].shape, F32, kind="ExternalOutput").ap()
    build(nc, *args, out)
    r = _run(nc, [arrays], core_ids=[0])
    return r.results[0]["out_x"]
```

```python
import math
from contextlib import ExitStack

import numpy as np

import concourse.bass as bass
from concourse import mybir

ALU = mybir.AluOpType
ACT = mybir.ActivationFunctionType
AX = mybir.AxisListType
F32 = mybir.dt.float32
F32R = mybir.dt.float32r
BF16 = mybir.dt.bfloat16
I32 = mybir.dt.int32

P = 128
BANK = 512
RAW_SLOTS = 6
SPLIT_SLOTS = 3
AHEAD = 2
HEAD = 64
ROPE = HEAD // 4
ROPE_THETA = 500000.0
EPS = 1e-6
NEG_BIG = -2.0 ** 100


def build(nc, x_in, mem, positions, attn_norm, w_in, w_out, mem_norm, w_mem_kv, mem_q_norm, mem_k_norm,
          diff_q_norm, diff_k_norm, diff_lambda, diff_subln, ffn_norm, dense_w_gate_up, dense_w_down,
          w_router, moe_w_gate_up, moe_w_down, out):
    _, S, D = x_in.shape
    TILES = S // P
    KD = D // P
    MIX = 3 * D // 4
    WIN = w_in.shape[2]
    FF = dense_w_down.shape[1]
    E = w_router.shape[2]
    FE = moe_w_down.shape[2]
    HALF = BANK // 2
    SCALE = float(HEAD) ** -0.5
    LAM_INIT = 0.8 - 0.6 * math.exp(-0.3 * 1)
    BLOCK = 4 * BANK
    QKW = 2 * MIX
    NSB = MIX // HEAD
    NDIFF = MIX // (2 * HEAD)
    NMEM = (D - MIX) // HEAD
    IN_GROUPS = WIN // BANK
    FF_GROUPS = FF // HALF
    FE_GROUPS = FE // BANK
    assert TILES == 2 and MIX == 768 and WIN == 5 * BANK and FF % HALF == 0 and FE % BANK == 0 and D == 2 * BANK

    BLK_IN, BLK_OUT = [0, 0], [0, 0]
    BLK_IN[0], n = 0, 2 * IN_GROUPS
    BLK_MEM, n = n, n + 4
    BLK_OUT[0], n = n, n + KD // 2
    BLK_FF, n = n, n + 2 * FF_GROUPS
    BLK_FD, n = n, n + FF // P // 2
    BLK_IN[1], n = n, n + 2 * IN_GROUPS
    BLK_OUT[1], n = n, n + KD // 2
    BLK_MOE = n
    GU_BLOCKS = 4 * FE_GROUPS
    DOWN_BLOCKS = FE // P // 2
    TURN_BLOCKS = GU_BLOCKS + DOWN_BLOCKS
    assert TURN_BLOCKS % RAW_SLOTS == 0 and TURN_BLOCKS % SPLIT_SLOTS == 0
    UNITS = [NSB + NMEM, NDIFF + NMEM]
    LOGIT, REST, FIRST, SECOND, MASK, PLACE1, TMP = range(7)
    MIXED = [BLK_MEM, BLK_OUT[1]]
    PIECES = 4 * (BLK_OUT[0] - BLK_MEM)
    PIECE_AT = {**{2 + i: [2 * i, 2 * i + 1] for i in range(PIECES // 4)}, **{i - 2: [i] for i in range(PIECES // 2, PIECES)}}
    SPLIT_AT = [3, 5, 9, 13]
    LAG = 2
    STEP_FILLS = [{0: [("qk0", 1), ("memT", 0), ("memT", 1)], 1: [("memT", 2), ("memT", 3)], 2: [("qk0", 2)], 4: [("qk0", 3)],
                   6: [("qk0", 4)], 8: [("qk0", 5)], 10: [("qk0", 6)], 11: [("km", 0)]},
                  {0: [("qk1", 1)], 1: [("qk1", 2)], 2: [("qk1", 3)], 3: [("qk1", 4)], 4: [("qk1", 5), ("km", 1)],
                   6: [("qk1", 6)]}]
    fills = []
    for l in range(2):
        fills += [(f"xT{l}", f) for f in range(4)] + [(f"qk{l}", 0)]
        for s in range(UNITS[l] + LAG):
            fills += STEP_FILLS[l].get(s, []) + ([(f"w{l}", s - LAG)] if s >= LAG else [])
        fills += [(f"oT{l}", f) for f in range(4)] + [(f"fT{l}", f) for f in range(4)]
        fills += [("hT", j) for j in range(FF_GROUPS)] if l == 0 else []
    fills += [("gather", f) for f in range(4)]
    FILL = {name: i for i, name in enumerate(fills)}
    FILL_MOE = len(fills)
    SCATTER, SLOTS, HIDDEN, GATHER, TURN_FILLS = 0, 4, 5, 5 + FE_GROUPS, 9 + FE_GROUPS
    assert TURN_FILLS % 2 == 0
    SCATTER_AT, SLOTS_AT = [2, 2, 3, 3], 4
    GATHER_AT = [GU_BLOCKS + 3 + 2 * f for f in range(4)]
    MAX_EXTRA = TILES * S // (P + 1)

    ctx = ExitStack()
    with ctx:
        def sb(name, shape, dt=F32, to=None):
            return (to or ctx).enter_context(nc.sbuf_tensor(name, shape, dt))

        def sem(name):
            return ctx.enter_context(nc.semaphore(name))

        raw = sb("raw", [P, RAW_SLOTS, BLOCK])
        w_hi = sb("w_hi", [P, SPLIT_SLOTS, BLOCK], F32R)
        w_lo = sb("w_lo", [P, SPLIT_SLOTS, BLOCK], F32R)
        x = sb("x", [P, TILES, D])
        nat = sb("nat", [P, TILES, D])
        t_hi = sb("t_hi", [P, KD, S], F32R)
        t_lo = sb("t_lo", [P, KD, S], F32R)
        sil = sb("sil", [P, 2, BANK])
        hid = sb("hid", [P, 2, BANK])
        gain = sb("gain", [P, D])
        km_t = sb("km_t", [P, 2, 2, S])
        vm = sb("vm", [P, 2, TILES, 4 * HEAD])
        km = sb("km", [P, 2, TILES, 4 * HEAD])
        ident = sb("ident", [P, P])
        ones = sb("ones", [P, P], BF16)
        before = sb("before", [P, P], BF16)
        mask_b = sb("mask_b", [P, TILES, E], BF16)
        slot_row = sb("slot_row", [P, P])
        hide = sb("hide", [P, 2, P])
        hide_b = sb("hide_b", [P, 2, P], BF16)
        ident_b = sb("ident_b", [P, P], BF16)
        head_gain = sb("head_gain", [P, 2, HEAD])
        memq_gain = sb("memq_gain", [P, 2, HEAD])
        diff_gain = sb("diff_gain", [P, 2, HEAD])
        sub_gain = sb("sub_gain", [P, 2 * HEAD])
        lam4 = sb("lam4", [P, 4, HEAD])
        pos_i = sb("pos_i", [P, TILES], I32)
        norm_r = sb("norm_r", [P, 5, 3, TILES])
        stat = sb("stat", [P, 4, 3, 4])
        lam = sb("lam", [P, 5])
        gap = sb("gap", [P, 8, TILES])
        minus_half = sb("minus_half", [P, 24])
        inv_freq = sb("inv_freq", [P, TILES, ROPE // 2])
        down_row = sb("down_row", [P, E])
        ang = sb("ang", [P, 6, TILES, ROPE // 2])
        ang_i = sb("ang_i", [P, TILES, ROPE // 2], I32)
        head_r = sb("head_r", [P, 7, 2, 24])
        wr = sb("wr", [P, KD, E])
        wr_split = sb("wr_split", [P, KD, 2 * E], F32R)
        logit_t = sb("logit_t", [2 * E, S])
        route = sb("route", [P, 7, TILES, E])
        turn_slot = sb("turn_slot", [P, TILES, 12])
        turn_w = sb("turn_w", [P, TILES, 12])
        over = sb("over", [P, 5, E])
        table = sb("table", [P, 4])
        table_i = sb("table_i", [P, 4], I32)
        pick = sb("pick", [P, TILES, P], F32R)
        pick_t = sb("pick_t", [P, TILES, P], F32R)
        turn_cw = sb("turn_cw", [P, TILES])
        slot_w = sb("slot_w", [P, 1])

        with ExitStack() as here:
            proj = sb("proj", [P, TILES, WIN], to=here)
            qk_t = sb("qk_t", [P, 7, 2 * S], to=here)
            att = sb("att", [P, 2, 2 * BANK], to=here)
            keep = sb("keep", [P, 2, BANK], to=here)
            att_t = sb("att_t", [P, 2, BANK], to=here)
        with ExitStack() as here:
            h_hi = sb("h_hi", [P, FF // P, S], F32R, to=here)
            h_lo = sb("h_lo", [P, FF // P, S], F32R, to=here)
        with ExitStack() as here:
            e_hi = sb("e_hi", [P, FE // P, P], F32R, to=here)
            e_lo = sb("e_lo", [P, FE // P, P], F32R, to=here)
            n_hi = sb("n_hi", [P, TILES, D], F32R, to=here)
            n_lo = sb("n_lo", [P, TILES, D], F32R, to=here)
        g_hi, g_lo = (t[:, 0:KD // 2, :].rearrange("p a (b s) -> p (a b) s", b=2) for t in (t_hi, t_lo))
        y_hi, y_lo = (t[:, KD // 2:KD, :].rearrange("p a s -> p (a s)") for t in (t_hi, t_lo))

        ps = ctx.enter_context(nc.psum_tensor("ps", [P, 8, BANK], F32))
        SPARE = 4
        OUT = 6

        raw_landed = [sem(f"raw_landed{s}") for s in range(RAW_SLOTS)]
        hi_ready, lo_ready = sem("hi_ready"), sem("lo_ready")
        w_used = sem("w_used")
        fill_ready, fill_hi = sem("fill_ready"), sem("fill_hi")
        spare_taken = [sem(f"spare_taken{b}") for b in range(2)]
        acc_taken = [sem(f"acc_taken{b}") for b in range(2)]
        z_ready, z_taken = sem("z_ready"), [sem(f"z_taken{b}") for b in range(2)]
        head_ready, head_taken = sem("head_ready"), sem("head_taken")
        small_landed, mem_landed = sem("small_landed"), sem("mem_landed")
        x_landed = [sem(f"x_landed{t}") for t in range(TILES)]
        gain_landed, consts_ready = sem("gain_landed"), sem("consts_ready")
        squares_ready, rstd_ready, nat_ready = sem("squares_ready"), sem("rstd_ready"), sem("nat_ready")
        km_copied, sums_ready, head_rstd_ready, heads_normed = (
            sem("km_copied"), sem("sums_ready"), sem("head_rstd_ready"), sem("heads_normed"))
        max_ready, att_ready = sem("max_ready"), sem("att_ready")
        sil_ready = sem("sil_ready")
        tile0_summed = sem("tile0_summed")
        lam_sums, lam_exp = sem("lam_sums"), sem("lam_exp")
        ang_ready, rope_ready = sem("ang_ready"), sem("rope_ready")
        wr_hi_ready, wr_ready = sem("wr_hi_ready"), sem("wr_ready")
        logits_ready, gap_ready, gap_exp = sem("logits_ready"), sem("gap_ready"), sem("gap_exp")
        logits_copied = sem("logits_copied")
        mask_ready, places_ready, table_ready = sem("mask_ready"), sem("places_ready"), sem("table_ready")
        n_hi_ready, pick_ready = sem("n_hi_ready"), sem("pick_ready")
        nat_read = sem("nat_read")
        y0_summed = sem("y0_summed")
        y_scaled, y_hi_ready, y_lo_ready = sem("y_scaled"), sem("y_hi_ready"), sem("y_lo_ready")
        dve_step, act_step, pool_step = sem("dve_step"), sem("act_step"), sem("pool_step")
        stored = sem("stored")

        def chain(eng, own):
            done = [0]

            def link(ins):
                done[0] += 1
                ins.then_inc(own, 1)
                eng.wait_ge(own, done[0])
            return link

        def taken(eng, f):
            eng.wait_ge(spare_taken[f % 2], f // 2 + 1)

        groups = []
        for l in range(2):
            groups += [(f"in{l}.{g}", g % 2) for g in range(IN_GROUPS)]
            groups += [(f"mem{g}", 1) for g in range(2)] if l == 0 else []
            groups += [(f"out{l}.{p}", p) for p in range(2)]
            if l == 0:
                groups += [(f"ff{g}", g % 2) for g in range(FF_GROUPS)] + [(f"fd{p}", p) for p in range(2)]
        ACC = {name: (p, sum(q == p for _, q in groups[:i])) for i, (name, p) in enumerate(groups)}

        def group_taken(eng, name):
            p, uses = ACC[name]
            eng.wait_ge(acc_taken[p], uses + 1)

        ACC_MOE = [sum(q == p for _, q in groups) for p in range(2)]
        ACC_TURN = [(FE_GROUPS + 1) // 2, FE_GROUPS // 2]
        NORMS = {"qm0": 0, "km0": 1, "km1": 2, "q": 3, "k": 4, "qm1": 5, "sub": 6}
        NORM_N = [2 * NMEM] * 3 + [2 * 2 * NDIFF] * 2 + [2 * NMEM, 2 * NDIFF]
        NORM_W = [HEAD] * 6 + [2 * HEAD]

        def score_banks(l, u, half):
            z = ps[:, u % 2 if l == 0 else 2 * (u % 2) + half, :]
            return z[:, 0:P], z[:, P:3 * P]

        def memory_scores(l, u):
            return ps[:, u % 2 * (l + 1), :]

        def output_part(v, f):
            h, t = divmod(f, 2)
            return v[:, t, h * BANK:(h + 1) * BANK]

        block = ctx.enter_context(nc.Block())

        def rows(w, k0, kn, c0, cn):
            return w[k0 * P:(k0 + kn) * P, c0:c0 + cn].rearrange("(k p) n -> p k n", p=P)

        def halves(slot):
            v = slot.rearrange("p (k h n) -> p k h n", k=4, h=2)
            return v[:, :, 0, :], v[:, :, 1, :]

        dense = []
        for l in range(2):
            dense += [[(None, rows(w_in[l], k, 4, g * BANK, BANK))] for g in range(IN_GROUPS) for k in (0, 4)]
            if l == 0:
                dense += [[(None, rows(w_mem_kv[m], k, 4, 0, BANK))] for m in range(2) for k in (0, 4)]
            dense += [[(None, rows(w_out[l], k, 2, 0, D))] for k in range(0, KD, 2)]
            if l == 0:
                dense += [[(h, rows(dense_w_gate_up[0], k, 4, h * FF + g * HALF, HALF)) for h in range(2)]
                          for g in range(FF_GROUPS) for k in (0, 4)]
                dense += [[(None, rows(dense_w_down[0], k, 2, 0, D))] for k in range(0, FF // P, 2)]
        assert len(dense) == BLK_MOE

        def raw_count(n):
            return 16 * sum(len(dense[m]) for m in range(n % RAW_SLOTS, n + 1, RAW_SLOTS))

        RAW_MOE = [16 * (1 + sum(len(dense[m]) for m in range(s, BLK_MOE, RAW_SLOTS))) for s in range(RAW_SLOTS)]

        def wait_raw(eng, n, turn=None):
            s = n % RAW_SLOTS
            if turn is None and n < BLK_MOE:
                eng.wait_ge(raw_landed[s], raw_count(n))
            else:
                at = RAW_MOE[s] + 16 * ((n - BLK_MOE) // RAW_SLOTS)
                eng.wait_ge(raw_landed[s], at if turn is None else turn * (16 * TURN_BLOCKS // RAW_SLOTS) + at)

        @block.sync
        def _(sp):
            for t in range(TILES):
                sp.dma_start(x[:, t, :], x_in[0, t * P:(t + 1) * P, :]).then_inc(x_landed[t], 16)
            sp.wait_ge(x_landed[0], 16)
            for b, parts in enumerate(dense):
                slot = raw[:, b % RAW_SLOTS, :]
                if b >= RAW_SLOTS:
                    sp.wait_ge(lo_ready, b - RAW_SLOTS + 1)
                for h, src in parts:
                    dst = slot.rearrange("p (k n) -> p k n", n=src.shape[2]) if h is None else halves(slot)[h]
                    sp.dma_start(dst, src).then_inc(raw_landed[b % RAW_SLOTS], 16)
                if b == SPLIT_SLOTS - 1:
                    sp.dma_start(proj[:, :, 0:D], mem.rearrange("b (t p) d -> p (b t) d", p=P)).then_inc(mem_landed, 16)

            def turn_loads(i, expert):
                gate_up = moe_w_gate_up[0, bass.ds(expert, 1)].rearrange("e (k p) n -> p (e k) n", p=P)
                down = moe_w_down[0, bass.ds(expert, 1)].rearrange("e (k p) n -> p (e k) n", p=P)
                for b in range(TURN_BLOCKS):
                    n = BLK_MOE + b
                    slot = raw[:, n % RAW_SLOTS, :]
                    sp.wait_ge(lo_ready, i * TURN_BLOCKS + (n - RAW_SLOTS + 1))
                    if b < GU_BLOCKS:
                        j, half, k = b // 4, b // 2 % 2, b % 2 * 4
                        src = gate_up[:, k:k + 4, half * FE + j * BANK:half * FE + (j + 1) * BANK]
                    else:
                        k = (b - GU_BLOCKS) * 2
                        src = down[:, k:k + 2, :]
                    sp.dma_start(slot.rearrange("p (k n) -> p k n", n=src.shape[2]), src)\
                      .then_inc(raw_landed[n % RAW_SLOTS], 16)

            with sp.Fori(0, E) as i:
                turn_loads(i, i)
            sp.wait_ge(table_ready, 1)
            turns = sp.value_load(table_i[0:1, 0:1], min_val=E, max_val=E + MAX_EXTRA)
            with sp.If(turns > E):
                with sp.Fori(E, turns) as i:
                    expert = sp.value_load(table_i[0:1, bass.ds(i - (E - 1), 1)], min_val=0, max_val=E - 1)
                    turn_loads(i, expert)
            for b in range(SPLIT_SLOTS):
                n = BLK_MOE + b
                sp.wait_ge(lo_ready, turns * TURN_BLOCKS + (n - RAW_SLOTS + 1))
                sp.dma_start(raw[0:16, n % RAW_SLOTS, 0:P], x_in[0, 0:16, 0:P]).then_inc(raw_landed[n % RAW_SLOTS], 16)
            for h in range(2):
                n = FILL_MOE + SCATTER + 2 * h + 1
                sp.wait_ge(spare_taken[n % 2], turns * (TURN_FILLS // 2) + (n // 2 + 1))
                cols = slice(h * BANK, (h + 1) * BANK)
                sp.dma_start(out[0, :, cols].rearrange("(t p) d -> p t d", p=P), x[:, :, cols]).then_inc(stored, 16)
            sp.wait_ge(stored, 32)

        @block.tensor
        def _(pe):
            def spare(f):
                if f >= 2:
                    taken(pe, f - 2)
                return ps[:, SPARE + f % 2, :]

            def product(dst, hi, lo, slot, c0, cn, first, last):
                pe.matmul(dst, hi, w_hi[:, slot, c0:c0 + cn], start=first, stop=False)
                pe.matmul(dst, lo, w_hi[:, slot, c0:c0 + cn], start=False, stop=False)
                return pe.matmul(dst, hi, w_lo[:, slot, c0:c0 + cn], start=False, stop=last)

            def acc_free(name):
                p, uses = ACC[name]
                if uses:
                    pe.wait_ge(acc_taken[p], uses)
                return p

            def group_tile(b, b0, name, t, part=range(4)):
                g, half = divmod(b - b0, 2)
                p = ACC[f"{name}{g}"][0]
                for kk in part:
                    k = 4 * half + kk
                    mm = product(ps[:, 2 * p + t, :], t_hi[:, k, t * P:(t + 1) * P], t_lo[:, k, t * P:(t + 1) * P],
                                 b % SPLIT_SLOTS, kk * BANK, BANK, k == 0, k == KD - 1)
                return mm

            def group_block(b, b0, name):
                g, half = divmod(b - b0, 2)
                if half == 0:
                    acc_free(f"{name}{g}")
                pe.wait_ge(lo_ready, b + 1)
                for t in range(TILES):
                    mm = group_tile(b, b0, name, t)
                mm.then_inc(w_used, 1)

            def wide_tile(b, b0, chunks, hi, lo, t, part=range(2)):
                for kk in part:
                    k = 2 * (b - b0) + kk
                    for h in range(2):
                        mm = product(ps[:, 2 * t + h, :], hi[:, k, t * P:(t + 1) * P], lo[:, k, t * P:(t + 1) * P],
                                     b % SPLIT_SLOTS, kk * D + h * BANK, BANK, k == 0, k == chunks - 1)
                return mm

            def wide_block(b, b0, name, chunks, hi, lo):
                if b == b0:
                    for p in range(2):
                        acc_free(f"{name}{p}")
                pe.wait_ge(lo_ready, b + 1)
                for t in range(TILES):
                    mm = wide_tile(b, b0, chunks, hi, lo, t)
                    if t == 0 and 2 * (b - b0) + 2 == chunks:
                        mm.then_inc(tile0_summed, 1)
                mm.then_inc(w_used, 1)

            def fill_nat(name, f):
                bank = spare(FILL[(name, f)])
                t, c0 = f // 2, 4 * (f % 2)
                for j in range(4):
                    mm = pe.transpose(bank[:, j * P:(j + 1) * P], nat[:, t, (c0 + j) * P:(c0 + j + 1) * P], ident[:])
                mm.then_inc(fill_ready, 1)

            def first_block(name, tile_ready, b, tile_block):
                for t in range(TILES):
                    tile_ready(t)
                    fill_nat(name, 2 * t)
                    fill_nat(name, 2 * t + 1)
                    if t == 1:
                        tile_block(0, 1)
                    else:
                        pe.wait_ge(lo_ready, b + 1)
                    taken(pe, FILL[(name, 2 * t)])
                    tile_block(t, 0)
                tile_block(1, 1).then_inc(w_used, 1)

            def all_taken(name):
                for f in (2, 3):
                    taken(pe, FILL[(name, f)])

            def piece(i):
                m, kk = divmod(i, 4)
                b, half = BLK_MEM + m, m % 2
                if kk == 0:
                    if half == 0:
                        acc_free(f"mem{m // 2}")
                    pe.wait_ge(lo_ready, b + 1)
                if i == 0:
                    all_taken("memT")
                k = 4 * half + kk
                for t in range(TILES):
                    mm = product(ps[:, 2 + t, :], t_hi[:, k, t * P:(t + 1) * P], t_lo[:, k, t * P:(t + 1) * P],
                                 b % SPLIT_SLOTS, kk * BANK, BANK, k == 0, k == KD - 1)
                if kk == 3:
                    mm.then_inc(w_used, 1)

            def step_fill(l, name, c):
                if name == "memT":
                    if c == 0:
                        pe.wait_ge(nat_ready, 2 * TILES)
                    return fill_nat(name, c)
                bank = spare(FILL[(name, c)])
                if name == "km":
                    pe.wait_ge(heads_normed, [2, 3][c])
                elif c == 6:
                    pe.wait_ge(heads_normed, [1, 7][l])
                for j in range(4):
                    a, t = divmod(j, 2)
                    if name == "km":
                        src = km[:, c, t, a * P:(a + 1) * P]
                    else:
                        col = MIX * a + c * P if c < 6 else 3 * MIX + a * P
                        src = proj[:, t, col:col + P]
                    mm = pe.transpose(bank[:, j * P:(j + 1) * P], src, ident[:])
                mm.then_inc(fill_ready, 1)

            def attention(l):
                U, n_mix, base = UNITS[l], UNITS[l] - NMEM, l * UNITS[0]

                def scores(u):
                    if base + u >= 2:
                        pe.wait_ge(z_taken[u % 2], (base + u) // 2)
                    if u < n_mix:
                        for half in range(1 + l):
                            c, s = (u // 2, u % 2) if l == 0 else (u, half)
                            taken(pe, FILL[(f"qk{l}", c)])
                            q, k = qk_t[64 * s:64 * s + 64, c, 0:S], qk_t[64 * s:64 * s + 64, c, S:2 * S]
                            z0, z1 = score_banks(l, u, half)
                            pe.matmul(z0, q[:, 0:P], k[:, 0:P], start=True, stop=False)
                            pe.matmul(z0, ident_b[:], hide_b[:, l, :], start=False, stop=True)
                            pe.matmul(z1[:, 0:P], q[:, P:2 * P], k[:, 0:P], start=True, stop=True)
                            pe.matmul(z1[:, P:2 * P], q[:, P:2 * P], k[:, P:2 * P], start=True, stop=False)
                            mm = pe.matmul(z1[:, P:2 * P], ident_b[:], hide_b[:, l, :], start=False, stop=True)
                    else:
                        c, s = divmod(u - n_mix, 2)
                        taken(pe, FILL[(f"qk{l}", 6)])
                        if u == n_mix:
                            taken(pe, FILL[("km", l)])
                        for t in range(TILES):
                            mm = pe.matmul(memory_scores(l, u)[:, t * S:(t + 1) * S],
                                           qk_t[64 * s:64 * s + 64, 6, c * S + t * P:c * S + (t + 1) * P],
                                           km_t[64 * s:64 * s + 64, l, c, :], start=True, stop=True)
                    mm.then_inc(z_ready, 1)

                def turn(u):
                    bank = spare(FILL[(f"w{l}", u)])
                    if u < n_mix:
                        pe.wait_ge(att_ready, l * NSB + u + 1)
                    else:
                        pe.wait_ge(z_taken[u % 2], (base + u) // 2 + 1)
                    for j in range(3 if u < n_mix else 4):
                        mm = pe.transpose(bank[:, j * P:(j + 1) * P], att[:, u % 2, j * P:(j + 1) * P], ident[:])
                    mm.then_inc(fill_ready, 1)

                def values(u):
                    taken(pe, FILL[(f"w{l}", u)])
                    if base + u >= 2:
                        pe.wait_ge(head_taken, base + u - 1)
                    n = HEAD * (l + 1) if u < n_mix else HEAD
                    for t in range(TILES):
                        if u < n_mix:
                            parts = [[(0, 0)], [(1, 0), (2, 1)]][t]
                            v = proj[:, :, QKW + n * u:QKW + n * (u + 1)]
                        else:
                            parts = [(2 * t, 0), (2 * t + 1, 1)]
                            v = vm[:, l, :, n * (u - n_mix):n * (u - n_mix + 1)]
                        for j, s in parts:
                            mm = pe.matmul(ps[:, OUT + u % 2, t * n:(t + 1) * n], att_t[:, u % 2, j * P:(j + 1) * P],
                                           v[:, s, :], start=(j == parts[0][0]), stop=(j == parts[-1][0]))
                    mm.then_inc(head_ready, 1)

                step_fill(l, f"qk{l}", 0)
                for s in range(U + LAG + 1):
                    for name, c in STEP_FILLS[l].get(s, []):
                        step_fill(l, name, c)
                    if l == 0 and 0 <= s - LAG < U:
                        turn(s - LAG)
                    if s < U:
                        scores(s)
                    for i in PIECE_AT.get(s, []) if l == 0 else []:
                        piece(i)
                    if l == 1 and 0 <= s - LAG < U:
                        turn(s - LAG)
                    if s > LAG:
                        values(s - LAG - 1)

            for l in range(2):
                acc_free(f"in{l}.0")
                first_block(f"xT{l}", lambda t: pe.wait_ge(nat_ready, [0, 3][l] * TILES + t + 1), BLK_IN[l],
                            lambda t, part: group_tile(BLK_IN[l], BLK_IN[l], f"in{l}.", t, range(2 * part, 2 * part + 2)))
                for f in (1, 3):
                    taken(pe, FILL[(f"xT{l}", f)])
                for b in range(BLK_IN[l] + 1, MIXED[l]):
                    group_block(b, BLK_IN[l], f"in{l}.")
                for g in (3, 4):
                    group_taken(pe, f"in{l}.{g}")
                if l == 1:
                    pe.wait_ge(heads_normed, 6)
                if l == 0:
                    pe.wait_ge(consts_ready, 1)
                attention(l)
                pe.wait_ge(head_taken, sum(UNITS[:l + 1]))
                if l == 1:
                    pe.wait_ge(heads_normed, 8)
                for p in range(2):
                    acc_free(f"out{l}.{p}")
                first_block(f"oT{l}", lambda t: None, BLK_OUT[l],
                            lambda t, part: wide_tile(BLK_OUT[l], BLK_OUT[l], KD, t_hi, t_lo, t, [part]))
                for b in range(BLK_OUT[l] + 1, BLK_OUT[l] + KD // 2):
                    if b == BLK_OUT[l] + 2:
                        for f in (1, 3):
                            taken(pe, FILL[(f"oT{l}", f)])
                    wide_block(b, BLK_OUT[l], f"out{l}.", KD, t_hi, t_lo)
                if l == 1:
                    pe.wait_ge(wr_ready, 1)
                    for t in range(TILES):
                        pe.wait_ge(nat_ready, 4 * TILES + t + 1)
                        fill_nat("fT1", 2 * t)
                        fill_nat("fT1", 2 * t + 1)
                        logits = ps[:, OUT, t * P:(t + 1) * P]
                        for k in range(KD):
                            if k % 4 == 0:
                                taken(pe, FILL[("fT1", 2 * t + k // 4)])
                            tokens = slice(t * P, (t + 1) * P)
                            pe.matmul(logits[0:2 * E], wr_split[:, k, :], t_hi[:, k, tokens], start=(k == 0), stop=False)
                            mm = pe.matmul(logits[0:E], wr_split[:, k, 0:E], t_lo[:, k, tokens], start=False, stop=(k == KD - 1))
                    mm.then_inc(logits_ready, 1)
                if l == 1:
                    break
                acc_free("ff0")
                first_block("fT0", lambda t: pe.wait_ge(nat_ready, 2 * TILES + t + 1), BLK_FF,
                            lambda t, part: group_tile(BLK_FF, BLK_FF, "ff", t, range(2 * part, 2 * part + 2)))
                for f in (1, 3):
                    taken(pe, FILL[("fT0", f)])
                for b in range(BLK_FF + 1, BLK_IN[1]):
                    if b < BLK_FD:
                        group_block(b, BLK_FF, "ff")
                    else:
                        taken(pe, FILL[("hT", b - BLK_FD)])
                        wide_block(b, BLK_FD, "fd", FF // P, h_hi, h_lo)
                    j, odd = divmod(b - BLK_FF - 3, 2)
                    if odd == 0 and 0 <= j < FF_GROUPS:
                        bank = spare(FILL[("hT", j)])
                        p, uses = ACC[f"ff{j}"]
                        pe.wait_ge(acc_taken[p], uses + 1)
                        for i in range(4):
                            c, t = divmod(i, 2)
                            mm = pe.transpose(bank[:, i * P:(i + 1) * P],
                                              hid[:, j % 2, t * HALF + c * P:t * HALF + (c + 1) * P], ident[:])
                        mm.then_inc(fill_ready, 1)

            pe.wait_ge(logits_copied, 1)
            for t in range(TILES):
                mm = pe.transpose(ps[:, OUT, t * 2 * E:(t + 1) * 2 * E], logit_t[:, t * P:(t + 1) * P], ident[0:2 * E, 0:2 * E])
            mm.then_inc(logits_ready, 1)
            pe.wait_ge(mask_ready, 1)
            place = ps[:, OUT + 1, :]
            pe.matmul(place[:, 0:E], before[:], mask_b[:, 0, :], start=True, stop=True)
            pe.matmul(place[:, E:2 * E], ones[:], mask_b[:, 0, :], start=True, stop=False)
            pe.matmul(place[:, E:2 * E], before[:], mask_b[:, 1, :], start=False, stop=True)
            pe.matmul(place[:, 2 * E:3 * E], ones[:], mask_b[:, 0, :], start=True, stop=False)
            pe.matmul(place[:, 2 * E:3 * E], ones[:], mask_b[:, 1, :], start=False, stop=True).then_inc(places_ready, 1)

            def gather(f, bank):
                part = (n_hi, n_lo)[f % 2]
                for j in range(4):
                    k = f // 2 * 4 + j
                    for t in range(TILES):
                        mm = pe.matmul(bank[:, j * P:(j + 1) * P], part[:, t, k * P:(k + 1) * P], pick[:, t, :],
                                       start=(t == 0), stop=(t == TILES - 1))
                mm.then_inc(fill_ready, 1)

            def scatter(f, bank, before):
                h, t = divmod(f, 2)
                pe.wait_ge(y_lo_ready, before + (h + 1))
                pe.matmul(bank, pick_t[:, t, :], y_hi[:, h * BANK:(h + 1) * BANK], start=True, stop=False)
                pe.matmul(bank, pick_t[:, t, :], y_lo[:, h * BANK:(h + 1) * BANK], start=False, stop=True)\
                  .then_inc(fill_ready, 1)

            pe.wait_ge(nat_read, TILES)
            pe.wait_ge(pick_ready, 1)
            for f in range(4):
                gather(f, spare(FILL[("gather", f)]))
            for f in (0, 1):
                taken(pe, FILL[("gather", f)])
            pe.wait_ge(table_ready, 1)
            turns = pe.value_load(table_i[0:1, 0:1], min_val=E, max_val=E + MAX_EXTRA)
            with pe.Fori(0, turns) as i:
                def turn_taken(f):
                    n = FILL_MOE + f
                    pe.wait_ge(spare_taken[n % 2], i * (TURN_FILLS // 2) + (n // 2 + 1))

                def turn_spare(f):
                    turn_taken(f - 2)
                    return ps[:, SPARE + (FILL_MOE + f) % 2, :]

                for b in range(TURN_BLOCKS):
                    n = BLK_MOE + b
                    if b < GU_BLOCKS and b % 4 == 0:
                        j = b // 4
                        pe.wait_ge(acc_taken[j % 2], i * ACC_TURN[j % 2] + (ACC_MOE[j % 2] + j // 2))
                    if b == 1:
                        for f in (-2, -1):
                            turn_taken(f)
                    if b >= GU_BLOCKS:
                        turn_taken(HIDDEN + (b - GU_BLOCKS) // 2)
                    pe.wait_ge(lo_ready, i * TURN_BLOCKS + (n + 1))
                    if b < GU_BLOCKS:
                        j, half, k0 = b // 4, b // 2 % 2, b % 2 * 4
                        for kk in range(4):
                            k = k0 + kk
                            mm = product(ps[:, 2 * (j % 2) + half, :], g_hi[:, k, :], g_lo[:, k, :], n % SPLIT_SLOTS,
                                         kk * BANK, BANK, k == 0, k == KD - 1)
                    else:
                        for h in range(2):
                            for kk in range(2):
                                k = 2 * (b - GU_BLOCKS) + kk
                                mm = product(ps[:, OUT + h, :], e_hi[:, k, :], e_lo[:, k, :], n % SPLIT_SLOTS,
                                             kk * D + h * BANK, BANK, k == 0, k == FE // P - 1)
                            if b == TURN_BLOCKS - 1 and h == 0:
                                mm.then_inc(y0_summed, 1)
                    mm.then_inc(w_used, 1)
                    for f in range(4):
                        if b == SCATTER_AT[f]:
                            scatter(f, turn_spare(SCATTER + f), i * 2)
                    if b == SLOTS_AT:
                        bank = turn_spare(SLOTS)
                        for t in range(TILES):
                            pe.transpose(bank[:, t * P:(t + 1) * P], pick[:, t, :].bitcast(F32), ident[:])
                        for t in range(TILES):
                            mm = pe.matmul(bank[:, 2 * P:2 * P + 1], pick[:, t, :].bitcast(F32), turn_cw[:, t:t + 1],
                                           start=(t == 0), stop=(t == TILES - 1))
                        mm.then_inc(fill_ready, 1)
                    j, rest = divmod(b - 5, 4)
                    if rest == 0 and 0 <= j < FE_GROUPS:
                        bank = turn_spare(HIDDEN + j)
                        pe.wait_ge(acc_taken[j % 2], i * ACC_TURN[j % 2] + (ACC_MOE[j % 2] + j // 2 + 1))
                        for c in range(4):
                            mm = pe.transpose(bank[:, c * P:(c + 1) * P], hid[:, j % 2, c * P:(c + 1) * P], ident[:])
                        mm.then_inc(fill_ready, 1)
                    if b in GATHER_AT:
                        f = GATHER_AT.index(b)
                        if f == 0:
                            pe.wait_ge(pick_ready, i + 2)
                        gather(f, turn_spare(GATHER + f))
            for f in range(4):
                n = FILL_MOE + SCATTER + f
                pe.wait_ge(spare_taken[n % 2], turns * (TURN_FILLS // 2) + n // 2)
                scatter(f, ps[:, SPARE + n % 2, :], turns * 2)

        @block.scalar
        def _(act):
            link = chain(act, act_step)
            split_at = [0]

            def split(n, turn=None):
                wait_raw(act, n, turn)
                if turn is None:
                    if n >= SPLIT_SLOTS:
                        act.wait_ge(w_used, n - SPLIT_SLOTS + 1)
                else:
                    act.wait_ge(w_used, turn * TURN_BLOCKS + (n - SPLIT_SLOTS + 1))
                act.copy(w_hi[:, n % SPLIT_SLOTS, :], raw[:, n % RAW_SLOTS, :]).then_inc(hi_ready, 1)

            def split_to(n):
                while split_at[0] < n:
                    split(split_at[0])
                    split_at[0] += 1

            def squares(s, src, t):
                if s + t:
                    act.wait_ge(squares_ready, TILES * s + t)
                act.activation(sil[:].rearrange("p a n -> p (a n)"), src[:, t, :], ACT.Square,
                               accum_out=norm_r[:, s, 0, t:t + 1]).then_inc(squares_ready, 1)

            def take_hi(f, dst):
                act.wait_ge(fill_ready, f + 1)
                act.copy(dst, ps[:, SPARE + f % 2, 0:BANK].rearrange("p (a n) -> p a n", a=dst.shape[1])).then_inc(fill_hi, 1)

            def take_nat(name, f):
                t, c0 = f // 2, 4 * (f % 2)
                take_hi(FILL[(name, f)], t_hi[:, c0:c0 + 4, t * P:(t + 1) * P])

            def split_nat(name):
                for f in range(4):
                    take_nat(name, f)

            def norm_and_split(s, added, name, b):
                for t in range(TILES):
                    group_taken(act, f"{added}{t}")
                    squares(s, x, t)
                    if t == 1:
                        split_to(b + SPLIT_SLOTS)
                    for f in (2 * t, 2 * t + 1):
                        take_nat(name, f)
                    if s == 4:
                        act.copy(n_hi[:, t, :], nat[:, t, :]).then_inc(n_hi_ready, 1)

            act.wait_ge(pool_step, 1)
            act.activation(stat[:, 0, 0, :], minus_half[:, 0:4], ACT.Square)
            for t in range(TILES):
                act.wait_ge(x_landed[t], 16)
                squares(0, x, t)

            def unit(l, u):
                n_mix, base, p = UNITS[l] - NMEM, l * UNITS[0], u % 2
                a = att[:, p, :]
                if u >= 2:
                    act.wait_ge(fill_ready, FILL[(f"w{l}", u - 2)] + 1)
                if u < n_mix and l == 0:
                    act.wait_ge(z_ready, base + u + 1)
                    act.activation(a[:, 0:3 * P], ps[:, p, 0:3 * P], ACT.Sigmoid, scale=SCALE)
                    act.activation(a[:, 3 * P:6 * P], ps[:, p, 0:3 * P], ACT.Sigmoid, scale=-SCALE)\
                       .then_inc(z_taken[p], 1)
                elif u < n_mix:
                    act.wait_ge(max_ready, NMEM * l + u + 1)
                    for half in range(2):
                        for t, (c0, c1) in enumerate([(0, P), (P, 3 * P)]):
                            v = a[:, half * 3 * P + c0:half * 3 * P + c1]
                            ins = act.activation(v, score_banks(1, u, half)[t], ACT.Exp, scale=SCALE, bias=stat[:, u % 4, 0, 2 * half + t:2 * half + t + 1],
                                                 accum_out=stat[:, u % 4, 1, 2 * half + t:2 * half + t + 1])
                    ins.then_inc(z_taken[p], 1)
                else:
                    act.wait_ge(max_ready, [u - n_mix, NMEM + u][l] + 1)
                    for t in range(TILES):
                        ins = act.activation(a[:, t * S:(t + 1) * S], memory_scores(l, u)[:, t * S:(t + 1) * S], ACT.Exp,
                                             scale=SCALE, bias=stat[:, u % 4, 0, t:t + 1], accum_out=stat[:, u % 4, 1, t:t + 1])
                    ins.then_inc(z_taken[p], 1)

            def take_weights(l, u):
                f = FILL[(f"w{l}", u)]
                act.wait_ge(fill_ready, f + 1)
                if l * UNITS[0] + u >= 2:
                    act.wait_ge(head_ready, l * UNITS[0] + u - 1)
                n = 3 * P if u < UNITS[l] - NMEM else 4 * P
                act.copy(att_t[:, u % 2, 0:n], ps[:, SPARE + f % 2, 0:n]).then_inc(spare_taken[f % 2], 1)

            def take_step_fills(l, s):
                for name, c in STEP_FILLS[l].get(s, []):
                    f = FILL[(name, c)]
                    if name == "memT":
                        take_nat(name, c)
                    elif name != "km" and c % 2 == 0:
                        act.wait_ge(fill_ready, f + 1)
                        act.copy(qk_t[:, c, :], ps[:, SPARE + f % 2, :]).then_inc(spare_taken[f % 2], 1)

            def take_memory(m):
                act.wait_ge(w_used, BLK_MEM + 2 * m + 2)
                kv = ps[:, 2:4, :]
                act.copy(km[:, m, :, :], kv[:, :, 0:4 * HEAD]).then_inc(km_copied, 1)
                act.copy(vm[:, m, :, :], kv[:, :, 4 * HEAD:8 * HEAD]).then_inc(acc_taken[1], 1)

            for l in range(2):
                if l == 0:
                    for f in range(4):
                        take_nat("xT0", f)
                        if f % 2:
                            split_to(1 + f // 2)
                    split_to(SPLIT_SLOTS)
                    def bcast(dst, src):
                        act.dma_start(dst, src).then_inc(small_landed, 16)

                    for m in range(2):
                        bcast(head_gain[:, m, :], mem_k_norm[m].partition_broadcast(P))
                        bcast(memq_gain[:, m, :], mem_q_norm[m].partition_broadcast(P))
                    bcast(diff_gain[:, 0, :], diff_q_norm[0].partition_broadcast(P))
                    bcast(diff_gain[:, 1, :], diff_k_norm[0].partition_broadcast(P))
                    bcast(sub_gain[:], diff_subln[0].partition_broadcast(P))
                    bcast(lam4[:], diff_lambda[0].partition_broadcast(P))
                    with nc.allow_non_contiguous_dma(reason="one position a partition"):
                        bcast(pos_i[:], positions.rearrange("b (t p) -> p (b t)", p=P))
                    bcast(wr[:], w_router[0].rearrange("(k p) e -> p k e", p=P))
                for b in range(BLK_IN[l], MIXED[l]):
                    split_to(b + 1 + AHEAD)
                    g, half = divmod(b - BLK_IN[l], 2)
                    if l == 0 and b == 0:
                        act.wait_ge(mem_landed, 16)
                        for t in range(TILES):
                            squares(1, proj[:, :, 0:D], t)
                        act.wait_ge(nat_ready, 2 * TILES)
                    if l == 0 and b == 4:
                        act.wait_ge(small_landed, 16 * 10)
                        act.copy(wr_split[:, :, 0:E], wr[:]).then_inc(wr_hi_ready, 1)
                        act.wait_ge(lam_sums, 1)
                        act.activation(lam[:, 2:4], lam[:, 0:2], ACT.Exp).then_inc(lam_exp, 1)
                    if l == 0 and b == 6:
                        act.wait_ge(ang_ready, 1)
                        act.activation(ang[:, 4, :, :], ang[:, 2, :, :], ACT.Sin)
                        act.activation(ang[:, 5, :, :], ang[:, 3, :, :], ACT.Sin).then_inc(rope_ready, 1)
                    if half and (l == 1 or g % 2 == 0):
                        p, _ = ACC[f"in{l}.{g}"]
                        act.wait_ge(w_used, b + 1)
                        act.copy(proj[:, :, g * BANK:(g + 1) * BANK], ps[:, 2 * p:2 * p + 2, :]).then_inc(acc_taken[p], 1)
                split_to(MIXED[l] + SPLIT_SLOTS)
                f = FILL[(f"qk{l}", 0)]
                act.wait_ge(fill_ready, f + 1)
                act.copy(qk_t[:, 0, :], ps[:, SPARE + f % 2, :]).then_inc(spare_taken[f % 2], 1)
                for s in range(UNITS[l] + LAG):
                    take_step_fills(l, s)
                    if s >= LAG:
                        take_weights(l, s - LAG)
                    if s < UNITS[l]:
                        unit(l, s)
                    if l == 0 and PIECE_AT.get(s, [0])[-1] % 8 == 7:
                        take_memory(PIECE_AT[s][-1] // 8)
                    if l == 0 and s in SPLIT_AT:
                        split_to(split_at[0] + 1)
                split_nat(f"oT{l}")
                for b in range(BLK_OUT[l], BLK_OUT[l] + KD // 2):
                    split_to(b + 1 + AHEAD)
                norm_and_split([2, 4][l], f"out{l}.", f"fT{l}", BLK_OUT[l] + KD // 2)
                if l == 1:
                    break
                for b in range(BLK_FF, BLK_IN[1]):
                    split_to(b + 1 + AHEAD)
                    bb = b - BLK_FF
                    if bb % 2 and b < BLK_FD:
                        j = bb // 2
                        p, uses = ACC[f"ff{j}"]
                        act.wait_ge(w_used, b + 1)
                        if j >= 2:
                            act.wait_ge(acc_taken[p], uses)
                        act.activation(sil[:, j % 2, :].rearrange("p (t n) -> p t n", t=2),
                                       ps[:, 2 * p:2 * p + 2, 0:HALF], ACT.Silu).then_inc(sil_ready, 1)
                    j, odd = divmod(bb - 4, 2)
                    if odd == 0 and 0 <= j < FF_GROUPS:
                        take_hi(FILL[("hT", j)], h_hi[:, 2 * j:2 * j + 2, :])
                norm_and_split(3, "fd", "xT1", BLK_IN[1])

            act.activation(stat[:, 0, 0, :], minus_half[:, 0:4], ACT.Exp)
            act.wait_ge(gap_ready, 1)
            act.activation(gap[:, 1, :], gap[:, 0, :], ACT.Exp).then_inc(gap_exp, 1)

            def take_gather(f, k):
                act.copy(g_hi[:, k:k + 4, :], ps[:, SPARE + f % 2, :].rearrange("p (a n) -> p a n", a=4))\
                   .then_inc(spare_taken[f % 2], 1)

            for f in (0, 2):
                F = FILL[("gather", f)]
                act.wait_ge(fill_ready, F + 1)
                take_gather(F, 2 * f)
            for h in range(2):
                act.wait_ge(y_scaled, h + 1)
                act.copy(y_hi[:, h * BANK:(h + 1) * BANK], sil[:, h, :]).then_inc(y_hi_ready, 1)
            act.wait_ge(table_ready, 1)
            turns = act.value_load(table_i[0:1, 0:1], min_val=E, max_val=E + MAX_EXTRA)
            with act.Fori(0, turns) as i:
                def filled(f):
                    act.wait_ge(fill_ready, i * TURN_FILLS + (FILL_MOE + f + 1))

                for b in range(TURN_BLOCKS):
                    for f in range(4):
                        if b == SCATTER_AT[f] + 1:
                            filled(SCATTER + f)
                            if f == 0:
                                act.wait_ge(nat_read, i * 4 + TILES)
                            n = FILL_MOE + SCATTER + f
                            act.copy(output_part(nat, f), ps[:, SPARE + n % 2, :]).then_inc(spare_taken[n % 2], 1)
                    if b % 4 == 3 and b < GU_BLOCKS:
                        j = b // 4
                        act.wait_ge(w_used, i * TURN_BLOCKS + (BLK_MOE + b + 1))
                        if j == 0:
                            act.wait_ge(y_lo_ready, i * 2 + 2)
                        q = (j - 2) % 2
                        if j >= 2:
                            act.wait_ge(acc_taken[q], i * ACC_TURN[q] + (ACC_MOE[q] + j // 2))
                        act.activation(sil[:, j % 2, :], ps[:, 2 * (j % 2), :], ACT.Silu).then_inc(sil_ready, 1)
                    j, rest = divmod(b - 6, 4)
                    if rest == 0 and 0 <= j < FE_GROUPS:
                        filled(HIDDEN + j)
                        act.copy(e_hi[:, 4 * j:4 * j + 4, :],
                                 ps[:, SPARE + (FILL_MOE + HIDDEN + j) % 2, :].rearrange("p (a n) -> p a n", a=4))\
                           .then_inc(fill_hi, 1)
                    if b - 1 in GATHER_AT[::2]:
                        f = GATHER_AT.index(b - 1)
                        filled(GATHER + f)
                        take_gather(FILL_MOE + GATHER + f, 2 * f)
                    if b < TURN_BLOCKS - 1:
                        split(BLK_MOE + b + SPLIT_SLOTS, i)
                split(BLK_MOE + TURN_BLOCKS - 1 + SPLIT_SLOTS, i)
                for h in range(2):
                    act.wait_ge(y_scaled, i * 2 + (h + 3))
                    act.copy(y_hi[:, h * BANK:(h + 1) * BANK], sil[:, h, :]).then_inc(y_hi_ready, 1)

        @block.vector
        def _(dve):
            link = chain(dve, dve_step)
            split_at = [0]

            def split(n, turn=None):
                if turn is None:
                    dve.wait_ge(hi_ready, n + 1)
                else:
                    dve.wait_ge(hi_ready, turn * TURN_BLOCKS + (n + 1))
                dve.tensor_tensor(w_lo[:, n % SPLIT_SLOTS, :], raw[:, n % RAW_SLOTS, :],
                                  w_hi[:, n % SPLIT_SLOTS, :].bitcast(F32), ALU.subtract).then_inc(lo_ready, 1)

            def split_to(n):
                while split_at[0] < n:
                    split(split_at[0])
                    split_at[0] += 1

            def norm(s, src, t):
                if t == 0:
                    dve.wait_ge(gain_landed, 16 * (s + 1))
                dve.wait_ge(rstd_ready, TILES * s + t + 1)
                dve.scalar_tensor_tensor(out=nat[:, t, :], in0=src[:, t, :], scalar=norm_r[:, s, 2, t:t + 1],
                                         in1=gain[:], op0=ALU.mult, op1=ALU.mult).then_inc(nat_ready, 1)

            his = [0]

            def take_lo(f, dst, hi):
                his[0] += 1
                dve.wait_ge(fill_hi, his[0])
                dve.tensor_tensor(dst, ps[:, SPARE + f % 2, 0:BANK].rearrange("p (a n) -> p a n", a=dst.shape[1]),
                                  hi.bitcast(F32), ALU.subtract).then_inc(spare_taken[f % 2], 1)

            def take_nat(name, f):
                t, c0 = f // 2, 4 * (f % 2)
                take_lo(FILL[(name, f)], t_lo[:, c0:c0 + 4, t * P:(t + 1) * P], t_hi[:, c0:c0 + 4, t * P:(t + 1) * P])

            def split_nat(name):
                for f in range(4):
                    take_nat(name, f)

            def norm_parts(name):
                heads = lambda v, w=HEAD: v.rearrange("p t (h w) -> p t h w", w=w)
                l = int(name[2]) if name[1:2] == "m" else 1
                src, g = {"km": (heads(km[:, l]), head_gain[:, l, :]),
                          "qm": (heads(proj[:, :, 3 * MIX:WIN]), memq_gain[:, l, :]),
                          "q": (heads(proj[:, :, 0:MIX]), diff_gain[:, 0, :]),
                          "k": (heads(proj[:, :, MIX:QKW]), diff_gain[:, 1, :]),
                          "su": (heads(nat[:, :, 0:MIX], 2 * HEAD), sub_gain[:])}[name[:2]]
                return NORMS[name], src, g

            def head_sums(name):
                m, src, _ = norm_parts(name)
                if m:
                    dve.wait_ge(sums_ready, m)
                _, A, N, W = src.shape
                sums = head_r[:, m, 0, 0:A * N].rearrange("p (a n) -> p a n", a=A)
                for a in range(A):
                    sq = hid[:].rearrange("p a n -> p (a n)")[:, 0:N * W].rearrange("p (n w) -> p n w", w=W)
                    link(dve.tensor_tensor(sq, src[:, a], src[:, a], ALU.mult))
                    ins = dve.tensor_reduce(sums[:, a, :], sq, AX.X, ALU.add)
                    if a < A - 1:
                        link(ins)
                ins.then_inc(sums_ready, 1)

            def head_apply(name):
                m, src, g = norm_parts(name)
                _, A, N, W = src.shape
                rstd = head_r[:, m, 1, 0:A * N].rearrange("p (a n) -> p a n", a=A)
                dve.wait_ge(head_rstd_ready, m + 1)
                for a in range(A):
                    ins = dve.tensor_tensor(src[:, a], src[:, a], rstd[:, a].unsqueeze(2).to_broadcast([P, N, W]), ALU.mult)
                    if a == A - 1:
                        link(ins)
                for a in range(A):
                    ins = dve.tensor_tensor(src[:, a], src[:, a], g.unsqueeze(1).to_broadcast([P, N, W]), ALU.mult)
                ins.then_inc(heads_normed, 1)

            def norm_and_split(s, added, order, name, b):
                for t in range(TILES):
                    if t == 0:
                        dve.wait_ge(tile0_summed, order + 1)
                    else:
                        dve.wait_ge(w_used, b)
                    dve.tensor_tensor(x[:, t, :], x[:, t, :], ps[:, 2 * t:2 * t + 2, :].rearrange("p a n -> p (a n)"),
                                      ALU.add).then_inc(acc_taken[t], 1)
                    if t == 1:
                        for f in (0, 1):
                            take_nat(name, f)
                    group_taken(dve, f"{added}{t}")
                    norm(s, x, t)
                for f in (2, 3):
                    if b < BLK_MOE:
                        split_to(b + f)
                    take_nat(name, f)
                if b < BLK_MOE:
                    split_to(b + SPLIT_SLOTS)

            dve.memset(keep[:], 1.0)
            link(dve.memset(turn_slot[:], -1.0))
            link(dve.memset(turn_w[:], 0.0))
            for t in range(TILES):
                norm(0, x, t)

            def lambda_sums():
                dve.wait_ge(small_landed, 16 * 10)
                link(dve.tensor_tensor(hid[:, 0, 0:HEAD], lam4[:, 0, :], lam4[:, 1, :], ALU.mult))
                link(dve.tensor_tensor(hid[:, 0, HEAD:2 * HEAD], lam4[:, 2, :], lam4[:, 3, :], ALU.mult))
                dve.tensor_reduce(lam[:, 0:2], hid[:, 0, 0:2 * HEAD].rearrange("p (a n) -> p a n", a=2), AX.X, ALU.add)\
                   .then_inc(lam_sums, 1)
                dve.wait_ge(lam_sums, 1)

            def lambda_end():
                dve.wait_ge(wr_hi_ready, 1)
                dve.tensor_tensor(wr_split[:, :, E:2 * E], wr[:], wr_split[:, :, 0:E].bitcast(F32), ALU.subtract).then_inc(wr_ready, 1)
                dve.wait_ge(lam_exp, 1)
                link(dve.tensor_tensor(lam[:, 4:5], lam[:, 3:4], lam[:, 2:3], ALU.subtract))
                link(dve.tensor_scalar(lam[:, 4:5], lam[:, 4:5], -LAM_INIT, None, ALU.add))
                link(dve.tensor_scalar(sub_gain[:], sub_gain[:], 1.0 - LAM_INIT, None, ALU.mult))

            def turn_by_position():
                dve.wait_ge(heads_normed, 5)
                dve.wait_ge(rope_ready, 1)
                half_rope = ROPE // 2
                n = 2 * 2 * NDIFF
                for t in range(TILES):
                    heads = proj[:, t, 0:QKW].rearrange("p (h w) -> p h w", w=HEAD)
                    t1, t2 = heads[:, :, 0:half_rope], heads[:, :, half_rope:ROPE]
                    sin, cos = (ang[:, 4 + a, t, :].unsqueeze(1).to_broadcast([P, n, half_rope]) for a in range(2))
                    tmp = [hid[:, a // 2, a % 2 * HALF:a % 2 * HALF + n * half_rope].rearrange("p (h w) -> p h w", w=half_rope)
                           for a in range(4)]
                    dve.tensor_tensor(tmp[0], t1, cos, ALU.mult)
                    dve.tensor_tensor(tmp[1], t2, sin, ALU.mult)
                    dve.tensor_tensor(tmp[2], t2, cos, ALU.mult)
                    link(dve.tensor_tensor(tmp[3], t1, sin, ALU.mult))
                    dve.tensor_tensor(t1, tmp[0], tmp[1], ALU.subtract)
                    ins = dve.tensor_tensor(t2, tmp[2], tmp[3], ALU.add)
                    if t < TILES - 1:
                        link(ins)
                ins.then_inc(heads_normed, 1)

            def unit(l, u):
                n_mix, base, p = UNITS[l] - NMEM, l * UNITS[0], u % 2
                a = att[:, p, :]
                tiles = [(0, P), (P, 3 * P)]
                if u < n_mix and l == 0:
                    dve.wait_ge(z_taken[p], u // 2 + 1)
                    for t, (c0, c1) in enumerate(tiles):
                        kp = a[:, 3 * P + c0:3 * P + c1][:, ::-1]
                        ins = dve.tensor_tensor_scan(keep[:, p, c0 + 2 * t:c1 + 2 * t][:, ::-1], kp, kp, 1.0, ALU.mult, ALU.bypass)
                    link(ins)
                    for t, (c0, c1) in enumerate(tiles):
                        ins = dve.tensor_tensor(a[:, c0:c1], a[:, c0:c1], keep[:, p, c0 + 2 * t + 1:c1 + 2 * t + 1], ALU.mult)
                    ins.then_inc(att_ready, 1)
                elif u < n_mix:
                    dve.wait_ge(z_ready, base + u + 1)
                    mx = stat[:, u % 4, 0, :]
                    z = ps[:, 2 * p:2 * p + 2, :]
                    for t, (c0, c1) in enumerate(tiles):
                        ins = dve.tensor_reduce(mx[:, t:3 + t:2], z[:, :, c0:c1], AX.X, ALU.max)
                    link(ins)
                    ins = dve.tensor_scalar(mx, mx, -SCALE, None, ALU.mult)
                    ins.then_inc(max_ready, 1)
                else:
                    dve.wait_ge(z_ready, base + u + 1)
                    link(dve.tensor_reduce(stat[:, u % 4, 0, 0:TILES], memory_scores(l, u).rearrange("p (t n) -> p t n", t=TILES),
                                           AX.X, ALU.max))
                    dve.tensor_scalar(stat[:, u % 4, 0, 0:TILES], stat[:, u % 4, 0, 0:TILES], -SCALE, None, ALU.mult).then_inc(max_ready, 1)

            def differ(u):
                a, tiles, (_, sums, factor) = att[:, u % 2, :], [(0, P), (P, 3 * P)], (stat[:, u % 4, i, :] for i in range(3))
                dve.wait_ge(z_taken[u % 2], (UNITS[0] + u) // 2 + 1)
                link(dve.reciprocal(factor, sums))
                link(dve.scalar_tensor_tensor(out=factor[:, 2:4], in0=factor[:, 2:4], scalar=lam[:, 4:5], in1=sums[:, 0:2],
                                              op0=ALU.mult, op1=ALU.mult))
                for t, (c0, c1) in enumerate(tiles):
                    ins = dve.scalar_tensor_tensor(out=a[:, c0:c1], in0=a[:, 3 * P + c0:3 * P + c1], scalar=factor[:, 2 + t:3 + t],
                                                   in1=a[:, c0:c1], op0=ALU.mult, op1=ALU.add)
                ins.then_inc(att_ready, 1)

            def take_head(l, u):
                n_mix = UNITS[l] - NMEM
                o = ps[:, OUT + u % 2, :]
                if l == 0 and u < n_mix:
                    dve.wait_ge(head_ready, u + 1)
                    ins = dve.tensor_copy(nat[:, :, HEAD * u:HEAD * (u + 1)], o[:, 0:2 * HEAD].rearrange("p (t n) -> p t n", t=TILES))
                else:
                    c0, n = (2 * HEAD * u, 2 * HEAD) if u < n_mix else (MIX + HEAD * (u - n_mix), HEAD)
                    if u >= n_mix:
                        link(dve.reciprocal(stat[:, u % 4, 2, 0:TILES], stat[:, u % 4, 1, 0:TILES]))
                    dve.wait_ge(head_ready, l * UNITS[0] + u + 1)
                    for t in range(TILES):
                        ins = dve.tensor_scalar(nat[:, t, c0:c0 + n], o[:, t * n:(t + 1) * n],
                                                stat[:, u % 4, 2, t:t + 1], None, ALU.mult)
                ins.then_inc(head_taken, 1)

            def take_step_fills(l, s):
                for name, c in STEP_FILLS[l].get(s, []):
                    f = FILL[(name, c)]
                    if name == "memT":
                        take_nat(name, c)
                    elif name == "km" or c % 2:
                        dst = km_t[:, c].rearrange("p c s -> p (c s)") if name == "km" else qk_t[:, c, :]
                        dve.wait_ge(fill_ready, f + 1)
                        dve.tensor_copy(dst, ps[:, SPARE + f % 2, :]).then_inc(spare_taken[f % 2], 1)

            for l in range(2):
                if l == 0:
                    for f in range(4):
                        take_nat("xT0", f)
                        if f % 2:
                            split_to(1 + f // 2)
                    split_to(SPLIT_SLOTS)
                for b in range(BLK_IN[l], MIXED[l]):
                    split_to(min(b + 1 + AHEAD, MIXED[l]) if l else b + 1 + AHEAD)
                    g, half = divmod(b - BLK_IN[l], 2)
                    if l == 0 and half and g % 2 == 1:
                        p, _ = ACC[f"in{l}.{g}"]
                        dve.wait_ge(w_used, b + 1)
                        dve.tensor_copy(proj[:, :, g * BANK:(g + 1) * BANK], ps[:, 2 * p:2 * p + 2, :]).then_inc(acc_taken[p], 1)
                    if l == 0 and b == 0:
                        dve.wait_ge(fill_ready, FILL[("xT0", 3)] + 1)
                        dve.wait_ge(mem_landed, 16)
                        for t in range(TILES):
                            norm(1, proj[:, :, 0:D], t)
                    if l == 0 and b == 2:
                        lambda_sums()
                    if l == 0 and b == 5:
                        lambda_end()
                    if l == 1 and b == BLK_IN[1]:
                        dve.wait_ge(km_copied, 2)
                        head_sums("km1")
                    if l == 1 and b == BLK_IN[1] + 1:
                        head_apply("km1")
                    if l == 1 and b == BLK_IN[1] + 3:
                        for g in range(2):
                            group_taken(dve, f"in1.{g}")
                        head_sums("q")
                    if l == 1 and b == BLK_IN[1] + 5:
                        head_apply("q")
                        group_taken(dve, "in1.2")
                        head_sums("k")
                    if l == 1 and b == BLK_IN[1] + 7:
                        head_apply("k")
                        turn_by_position()
                split_to(MIXED[l] + SPLIT_SLOTS)
                for s in range(UNITS[l] + LAG + 1):
                    take_step_fills(l, s)
                    if s < UNITS[l]:
                        unit(l, s)
                    if l == 1 and 1 <= s <= NDIFF:
                        differ(s - 1)
                    if s > LAG:
                        take_head(l, s - LAG - 1)
                    if l == 0 and s - 1 in SPLIT_AT:
                        split_to(split_at[0] + 1)
                    if (l, s) in ((0, 4), (1, 1)):
                        group_taken(dve, f"in{l}.{IN_GROUPS - 1}")
                        head_sums(f"qm{l}")
                    if (l, s) in ((0, 5), (1, 3)):
                        head_apply(f"qm{l}")
                    if (l, s) == (0, 6):
                        dve.wait_ge(km_copied, 1)
                        head_sums("km0")
                    if (l, s) == (0, 8):
                        head_apply("km0")
                    if (l, s) == (1, NDIFF + LAG):
                        dve.wait_ge(head_taken, UNITS[0] + NDIFF)
                        head_sums("sub")
                    if (l, s) == (1, NDIFF + LAG + 2):
                        head_apply("sub")
                split_nat(f"oT{l}")
                for b in range(BLK_OUT[l], BLK_OUT[l] + KD // 2):
                    split_to(min(b + 1 + AHEAD, BLK_OUT[l] + KD // 2 + 1))
                norm_and_split([2, 4][l], f"out{l}.", 2 * l, f"fT{l}", BLK_OUT[l] + KD // 2)
                if l == 1:
                    break
                for b in range(BLK_FF, BLK_IN[1]):
                    split_to(min(b + 1 + AHEAD, BLK_IN[1] + 1))
                    bb = b - BLK_FF
                    if bb % 2 and b < BLK_FD:
                        j = bb // 2
                        p, uses = ACC[f"ff{j}"]
                        dve.wait_ge(sil_ready, j + 1)
                        if j >= 2:
                            dve.wait_ge(fill_ready, FILL[("hT", j - 2)] + 1)
                        dve.tensor_tensor(hid[:, j % 2, :].rearrange("p (t n) -> p t n", t=2),
                                          ps[:, 2 * p:2 * p + 2, HALF:BANK], sil[:, j % 2, :].rearrange("p (t n) -> p t n", t=2),
                                          ALU.mult).then_inc(acc_taken[p], 1)
                    j, odd = divmod(bb - 4, 2)
                    if odd == 0 and 0 <= j < FF_GROUPS:
                        take_lo(FILL[("hT", j)], h_lo[:, 2 * j:2 * j + 2, :], h_hi[:, 2 * j:2 * j + 2, :])
                norm_and_split(3, "fd", 1, "xT1", BLK_IN[1])

            R = lambda a: route[:, a]
            wide = lambda v: v.unsqueeze(2).to_broadcast([P, TILES, E])
            down8 = down_row[:].unsqueeze(1).to_broadcast([P, TILES, E])
            split_to(BLK_MOE + 2)
            for h in range(2):
                dve.memset(sil[:, h, :], 0.0).then_inc(y_scaled, 1)
            dve.wait_ge(y_scaled, 2)
            dve.tensor_copy(pick_t[:].rearrange("p t n -> p (t n)"), sil[:, 0, 0:2 * P])
            dve.wait_ge(logits_ready, 1)
            dve.tensor_copy(logit_t[:], ps[0:2 * E, OUT, 0:S]).then_inc(logits_copied, 1)
            dve.wait_ge(logits_ready, 2)
            parts = ps[:, OUT, 0:2 * TILES * E].rearrange("p (t h e) -> p t h e", h=2, e=E)
            link(dve.tensor_copy(R(TMP), parts[:, :, 0, :]))
            link(dve.tensor_tensor(R(LOGIT), R(TMP), parts[:, :, 1, :], ALU.add))
            for a in range(2):
                src, onehot = (LOGIT, FIRST) if a == 0 else (REST, SECOND)
                link(dve.tensor_reduce(gap[:, 2 + a, :], R(src), AX.X, ALU.max))
                link(dve.tensor_tensor(R(TMP), R(src), wide(gap[:, 2 + a, :]), ALU.is_equal))
                link(dve.tensor_tensor(R(TMP), R(TMP), down8, ALU.mult))
                link(dve.tensor_reduce(gap[:, 4, :], R(TMP), AX.X, ALU.min))
                link(dve.tensor_tensor(R(onehot), down8, wide(gap[:, 4, :]), ALU.is_equal))
                if a == 0:
                    link(dve.scalar_tensor_tensor(out=R(REST), in0=R(FIRST), scalar=NEG_BIG, in1=R(LOGIT), op0=ALU.mult, op1=ALU.add))
            dve.tensor_tensor(gap[:, 0, :], gap[:, 3, :], gap[:, 2, :], ALU.subtract).then_inc(gap_ready, 1)
            dve.tensor_tensor(mask_b[:], R(FIRST), R(SECOND), ALU.add).then_inc(mask_ready, 1)
            dve.tensor_tensor(R(MASK), R(FIRST), R(SECOND), ALU.add)
            dve.wait_ge(gap_exp, 1)
            link(dve.tensor_scalar(gap[:, 5, :], gap[:, 1, :], 1.0, None, ALU.add))
            link(dve.reciprocal(gap[:, 6, :], gap[:, 5, :]))
            link(dve.tensor_tensor(gap[:, 7, :], gap[:, 1, :], gap[:, 6, :], ALU.mult))
            link(dve.tensor_tensor(R(FIRST), R(FIRST), wide(gap[:, 6, :]), ALU.mult))
            link(dve.tensor_tensor(R(SECOND), R(SECOND), wide(gap[:, 7, :]), ALU.mult))
            link(dve.tensor_tensor(turn_w[:, :, 0:E], R(FIRST), R(SECOND), ALU.add))
            dve.wait_ge(places_ready, 1)
            place = ps[:, OUT + 1, :]
            link(dve.scalar_tensor_tensor(out=R(PLACE1), in0=place[:, 0:2 * E].rearrange("p (t e) -> p t e", e=E), scalar=1.0,
                                          in1=R(MASK), op0=ALU.add, op1=ALU.mult))
            link(dve.tensor_scalar(turn_slot[:, :, 0:E], R(PLACE1), -1.0, None, ALU.add))

            def make_pick(col):
                dve.tensor_copy(turn_cw[:].unsqueeze(2), turn_w[:, :, col])
                for t in range(TILES):
                    ins = dve.tensor_scalar(pick[:, t, :], slot_row[:], turn_slot[:, t, col], None, ALU.is_equal)
                ins.then_inc(pick_ready, 1)

            make_pick(slice(0, 1))
            link(dve.tensor_scalar(over[:, 0, :], place[:, 2 * E:3 * E], float(P), None, ALU.is_gt))
            link(dve.tensor_tensor_scan(over[:, 1, :], over[:, 0, :], over[:, 0, :], 0.0, ALU.add, ALU.bypass))
            link(dve.tensor_tensor(over[:, 2, :], over[:, 1, :], over[:, 0, :], ALU.subtract))
            link(dve.tensor_scalar(table[:, 0:1], over[:, 1, E - 1:E], float(E), None, ALU.add))
            small = hid[:].rearrange("p a n -> p (a n)")[:, 0:6 * MAX_EXTRA * E].rearrange("p (a r e) -> p a r e", a=6, e=E)
            sel = small[:, 0]
            per_r = lambda v: v.unsqueeze(1).to_broadcast([P, MAX_EXTRA, E])
            link(dve.tensor_tensor(sel, per_r(over[:, 2, :]), slot_row[:, 0:MAX_EXTRA].unsqueeze(2).to_broadcast([P, MAX_EXTRA, E]),
                                   ALU.is_equal))
            link(dve.tensor_tensor(sel, sel, per_r(over[:, 0, :]), ALU.mult))
            dve.tensor_tensor(small[:, 1], sel, per_r(slot_row[:, 0:E]), ALU.mult)
            for t in range(TILES):
                dve.tensor_tensor(small[:, 2 + t], sel, per_r(route[:, PLACE1, t, :]), ALU.mult)
            for t in range(TILES):
                ins = dve.tensor_tensor(small[:, 4 + t], sel, per_r(turn_w[:, t, 0:E]), ALU.mult)
            link(ins)
            dve.tensor_reduce(table[:, 1:1 + MAX_EXTRA], small[:, 1], AX.X, ALU.add)
            for t in range(TILES):
                dve.tensor_reduce(turn_slot[:, t, E:E + MAX_EXTRA], small[:, 2 + t], AX.X, ALU.add)
            for t in range(TILES):
                ins = dve.tensor_reduce(turn_w[:, t, E:E + MAX_EXTRA], small[:, 4 + t], AX.X, ALU.add)
            link(ins)
            link(dve.tensor_scalar(turn_slot[:, :, E:E + MAX_EXTRA], turn_slot[:, :, E:E + MAX_EXTRA], -1.0 - P, None, ALU.add))
            dve.tensor_copy(table_i[:], table[:]).then_inc(table_ready, 1)

            def take_gather(f, k):
                dve.tensor_copy(g_lo[:, k:k + 4, :], ps[:, SPARE + f % 2, :].rearrange("p (a n) -> p a n", a=4))\
                   .then_inc(spare_taken[f % 2], 1)

            for f in (1, 3):
                F = FILL[("gather", f)]
                dve.wait_ge(fill_ready, F + 1)
                take_gather(F, 2 * (f - 1))
            split_to(BLK_MOE + SPLIT_SLOTS)

            def split_y(h, before):
                dve.wait_ge(y_hi_ready, before + (h + 1))
                dve.tensor_tensor(y_lo[:, h * BANK:(h + 1) * BANK], sil[:, h, :], y_hi[:, h * BANK:(h + 1) * BANK].bitcast(F32),
                                  ALU.subtract).then_inc(y_lo_ready, 1)

            for h in range(2):
                split_y(h, 0)

            dve.wait_ge(table_ready, 1)
            turns = dve.value_load(table_i[0:1, 0:1], min_val=E, max_val=E + MAX_EXTRA)
            HI_MOE, SIL_MOE = his[0], FF_GROUPS
            with dve.Fori(0, turns) as i:
                def filled(f):
                    dve.wait_ge(fill_ready, i * TURN_FILLS + (FILL_MOE + f + 1))
                    return FILL_MOE + f

                for b in range(TURN_BLOCKS):
                    if b % 4 == 3 and b < GU_BLOCKS:
                        j = b // 4
                        dve.wait_ge(sil_ready, i * FE_GROUPS + (SIL_MOE + j + 1))
                        if j >= 2:
                            filled(HIDDEN + j - 2)
                        dve.tensor_tensor(hid[:, j % 2, :], ps[:, 2 * (j % 2) + 1, :], sil[:, j % 2, :], ALU.mult)\
                           .then_inc(acc_taken[j % 2], 1)
                    if b == SLOTS_AT + 1:
                        f = filled(SLOTS)
                        dve.tensor_copy(pick_t[:].rearrange("p t n -> p (t n)"), ps[:, SPARE + f % 2, 0:2 * P])
                        dve.tensor_copy(slot_w[:], ps[:, SPARE + f % 2, 2 * P:2 * P + 1]).then_inc(spare_taken[f % 2], 1)
                    if b == 15:
                        make_pick(bass.ds(i + 1, 1))
                    j, rest = divmod(b - 6, 4)
                    if rest == 0 and 0 <= j < FE_GROUPS:
                        n = FILL_MOE + HIDDEN + j
                        dve.wait_ge(fill_hi, i * FE_GROUPS + (HI_MOE + j + 1))
                        dve.tensor_tensor(e_lo[:, 4 * j:4 * j + 4, :], ps[:, SPARE + n % 2, :].rearrange("p (a n) -> p a n", a=4),
                                          e_hi[:, 4 * j:4 * j + 4, :].bitcast(F32), ALU.subtract).then_inc(spare_taken[n % 2], 1)
                    if b - 1 in GATHER_AT[1::2]:
                        f = GATHER_AT.index(b - 1)
                        take_gather(filled(GATHER + f), 2 * (f - 1))
                    if b < TURN_BLOCKS - 1:
                        split(BLK_MOE + b + SPLIT_SLOTS, i)
                for h in range(2):
                    if h == 0:
                        dve.wait_ge(y0_summed, i + 1)
                    else:
                        dve.wait_ge(w_used, i * TURN_BLOCKS + (BLK_MOE + TURN_BLOCKS))
                    dve.tensor_scalar(sil[:, h, :], ps[:, OUT + h, :], slot_w[:], None, ALU.mult).then_inc(y_scaled, 1)
                split(BLK_MOE + TURN_BLOCKS - 1 + SPLIT_SLOTS, i)
                for h in range(2):
                    split_y(h, i * 2 + 2)
            for f in range(4):
                n = FILL_MOE + SCATTER + f
                if f == 0:
                    dve.wait_ge(nat_read, turns * 4 + TILES)
                dve.wait_ge(fill_ready, turns * TURN_FILLS + (n + 1))
                xs = output_part(x, f)
                dve.tensor_tensor(xs, xs, ps[:, SPARE + n % 2, :], ALU.add).then_inc(spare_taken[n % 2], 1)

        @block.gpsimd
        def _(pool):
            link = chain(pool, pool_step)
            gains = [attn_norm[0], mem_norm, ffn_norm[0], attn_norm[1], ffn_norm[1]]

            def load_gain(s):
                if s:
                    pool.wait_ge(nat_ready, TILES * s)
                pool.dma_start(gain[:], gains[s].partition_broadcast(P)).then_inc(gain_landed, 16)

            def rsqrt(dst, src, width, n):
                link(pool.tensor_scalar(dst, src, 1.0 / width, EPS, ALU.mult, ALU.add))
                return pool.tensor_tensor(dst, dst, minus_half[:, 0:n], ALU.pow)

            def norm_rstd(s):
                if s:
                    load_gain(s)
                for t in range(TILES):
                    pool.wait_ge(squares_ready, TILES * s + t + 1)
                    rsqrt(norm_r[:, s, 2, t:t + 1], norm_r[:, s, 0, t:t + 1], D, 1).then_inc(rstd_ready, 1)

            def head_rstd(name):
                m = NORMS[name]
                pool.wait_ge(sums_ready, m + 1)
                n = NORM_N[m]
                rsqrt(head_r[:, m, 1, 0:n], head_r[:, m, 0, 0:n], NORM_W[m], n).then_inc(head_rstd_ready, 1)

            load_gain(0)
            link(pool.memset(minus_half[:], -0.5))
            link(pool.memset(ident[:], 0.0))
            link(pool.affine_select(out=ident[:], in_=ident[:], compare_op=ALU.not_equal, fill=1.0, base=0,
                                    pattern=[[-1, P]], channel_multiplier=1))
            norm_rstd(0)
            link(pool.memset(ones[:], 1.0))
            link(pool.affine_select(out=before[:], in_=ones[:], compare_op=ALU.is_ge, fill=0.0, base=-1,
                                    pattern=[[1, P]], channel_multiplier=-1))
            link(pool.memset(hide[:], 0.0))
            for l in range(2):
                link(pool.affine_select(out=hide[:, l, :], in_=hide[:, l, :], compare_op=ALU.is_ge, fill=NEG_BIG, base=l - 1,
                                        pattern=[[-1, P]], channel_multiplier=1))
            link(pool.tensor_copy(hide_b[:], hide[:]))
            link(pool.tensor_copy(ident_b[:], ident[:]))
            link(pool.iota(slot_row[:], pattern=[[1, P]], base=0, channel_multiplier=0, allow_small_or_imprecise_dtypes=True))
            link(pool.iota(down_row[:], pattern=[[1, E]], base=-E, channel_multiplier=0, allow_small_or_imprecise_dtypes=True))
            for j in range(ROPE // 2):
                link(pool.memset(inv_freq[:, :, j], float(np.float32(ROPE_THETA ** (-2 * j / ROPE)))))
            pool.memset(table[:], 0.0).then_inc(consts_ready, 1)
            norm_rstd(1)
            pool.wait_ge(small_landed, 16 * 10)
            A = lambda a: ang[:, a]
            two_pi = 2 * math.pi
            parts = [6.28125, float(np.float32(two_pi - 6.28125).astype(np.float16))]
            parts.append(two_pi - sum(parts))
            link(pool.tensor_copy(A(1)[:, :, 0], pos_i[:]))
            link(pool.tensor_tensor(A(0), inv_freq[:], A(1)[:, :, 0:1].to_broadcast([P, TILES, ROPE // 2]), ALU.mult))
            link(pool.tensor_scalar(A(1), A(0), 1.0 / two_pi, None, ALU.mult))
            link(pool.tensor_copy(ang_i[:], A(1)))
            link(pool.tensor_copy(A(1), ang_i[:]))
            for part in parts:
                link(pool.tensor_scalar(A(2), A(1), -part, None, ALU.mult))
                link(pool.tensor_tensor(A(0), A(0), A(2), ALU.add))

            def into_range(v):
                for op, bound, back in ((ALU.is_lt, -math.pi, two_pi), (ALU.is_gt, math.pi, -two_pi)):
                    link(pool.tensor_scalar(A(4), v, bound, back, op, ALU.mult))
                    link(pool.tensor_tensor(v, v, A(4), ALU.add))
                return pool.tensor_scalar(v, v, 3.1415925, -3.1415925, ALU.min, ALU.max)

            link(pool.tensor_copy(A(2), A(0)))
            link(into_range(A(2)))
            link(pool.tensor_scalar(A(3), A(2), math.pi / 2, None, ALU.add))
            into_range(A(3)).then_inc(ang_ready, 1)
            head_rstd("qm0")
            head_rstd("km0")
            norm_rstd(2)
            norm_rstd(3)
            for name in ("km1", "q", "k", "qm1", "sub"):
                head_rstd(name)
            norm_rstd(4)
            for t in range(TILES):
                pool.wait_ge(n_hi_ready, t + 1)
                pool.tensor_tensor(n_lo[:, t, :], nat[:, t, :], n_hi[:, t, :].bitcast(F32), ALU.subtract).then_inc(nat_read, 1)

            pool.wait_ge(table_ready, 1)
            turns = pool.value_load(table_i[0:1, 0:1], min_val=E, max_val=E + MAX_EXTRA)
            with pool.Fori(0, turns) as i:
                for f in range(4):
                    n = FILL_MOE + SCATTER + f
                    pool.wait_ge(spare_taken[n % 2], i * (TURN_FILLS // 2) + (n // 2 + 1))
                    xs = output_part(x, f)
                    pool.tensor_tensor(xs, xs, output_part(nat, f), ALU.add).then_inc(nat_read, 1)


_INS = ["x", "mem", "positions", "attn_norm", "w_in", "w_out", "mem_norm", "w_mem_kv", "mem_q_norm", "mem_k_norm",
        "diff_q_norm", "diff_k_norm", "diff_lambda", "diff_subln", "ffn_norm", "dense_w_gate_up", "dense_w_down",
        "w_router", "moe_w_gate_up", "moe_w_down"]


def kernel(**inputs):
    import concourse.bacc as _bacc
    from concourse.bass_utils import run_bass_kernel_spmd as _run

    nc = _bacc.Bacc("TRN2", target_bir_lowering=False, num_devices=1, dynamic_dma_scratch_size=4096)
    arrays, args = {}, []
    for name in _INS:
        a = np.ascontiguousarray(inputs[name])
        arrays[f"in_{name}"] = a
        args.append(nc.dram_tensor(f"in_{name}", a.shape, mybir.dt.from_np(a.dtype), kind="ExternalInput").ap())
    out = nc.dram_tensor("out_x", inputs["x"].shape, F32, kind="ExternalOutput").ap()
    build(nc, *args, out)
    r = _run(nc, [arrays], core_ids=[0])
    return r.results[0]["out_x"]
```
